# Optimizing a Trainium2 kernel written in Bass

```python
import math
import jax, jax.numpy as jnp
from jax import lax
import numpy as np

D_MODEL = 1024
BATCH = 1
SEQ = 1024
DEPTH = 2

CTX_LEN = 256
GRID_W = 64
EPS = 1e-6
ROPE_BASE = 10000.0
RET_HEADS = 4
RET_DK = 64
RET_DV = 64
RET_CHUNK = 128
RET_QK = RET_HEADS * RET_DK
RET_WIDTH = RET_HEADS * RET_DV
DIFF_HEADS = 4
DIFF_DK = 64
DIFF_DV = 2 * DIFF_DK
DIFF_QK = DIFF_HEADS * 2 * DIFF_DK
DIFF_WIDTH = DIFF_HEADS * DIFF_DV
Q_BLOCK = 128
CONV_CH = D_MODEL // 4
CONV_WIDTH = 31
CONV_PAD = (CONV_WIDTH - 1) // 2
MIX_WIDTH = RET_WIDTH + DIFF_WIDTH + CONV_CH
IN_WIDTH = 2 * RET_QK + 2 * RET_WIDTH + 2 * DIFF_QK + DIFF_WIDTH + 2 * CONV_CH
D_FF = 4 * D_MODEL
N_MOD = 6

kernel_name = 'hybrid_retention_diffattn_conformer_dit'

def rmsnorm(x, w):
    xf = x.astype(jnp.float32)
    y = xf * lax.rsqrt(jnp.mean(xf * xf, axis=-1, keepdims=True) + EPS)
    return (y * w).astype(x.dtype)

def layernorm(x, w, b):
    xf = x.astype(jnp.float32)
    mu = jnp.mean(xf, axis=-1, keepdims=True)
    var = jnp.mean(jnp.square(xf - mu), axis=-1, keepdims=True)
    return (xf - mu) * lax.rsqrt(var + EPS) * w + b

def modulate(h, shift, scale):
    return h * (1.0 + scale) + shift

def split_proj(p):
    sizes = (RET_QK, RET_QK, RET_WIDTH, RET_WIDTH, DIFF_QK, DIFF_QK, DIFF_WIDTH, CONV_CH, CONV_CH)
    out, start = [], 0
    for s in sizes:
        out.append(p[..., start:start + s])
        start += s
    return out

def rope_angles(pos, dim):
    inv = ROPE_BASE ** (-jnp.arange(0, dim, 2, dtype=jnp.float32) / dim)
    ang = pos.astype(jnp.float32)[:, None] * inv[None, :]
    return jnp.cos(ang), jnp.sin(ang)

def apply_rope(x, cos, sin):
    half = x.shape[-1] // 2
    shape = (cos.shape[0],) + (1,) * (x.ndim - 3) + (half,)
    cos = cos.reshape(shape)
    sin = sin.reshape(shape)
    x1, x2 = x[..., :half], x[..., half:]
    return jnp.concatenate([x1 * cos - x2 * sin, x2 * cos + x1 * sin], axis=-1).astype(x.dtype)

def axial_rope(x, rows, cols):
    h = x.shape[-1] // 2
    cr, sr = rope_angles(rows, h)
    cc, sc = rope_angles(cols, h)
    return jnp.concatenate([apply_rope(x[..., :h], cr, sr), apply_rope(x[..., h:], cc, sc)], axis=-1)

def retention_chunkwise(q, k, v, log_gamma, s0):
    b, h, l, dk = q.shape
    dv = v.shape[-1]
    n = l // RET_CHUNK
    qc = q.reshape(b, h, n, RET_CHUNK, dk)
    kc = k.reshape(b, h, n, RET_CHUNK, dk)
    vc = v.reshape(b, h, n, RET_CHUNK, dv)
    idx = jnp.arange(RET_CHUNK, dtype=jnp.float32)
    lg = log_gamma[:, None]
    rel = idx[:, None] - idx[None, :]
    intra = jnp.where(rel >= 0, jnp.exp(lg[:, :, None] * jnp.maximum(rel, 0.0)), 0.0)
    scores = jnp.einsum('bhncd,bhnsd->bhncs', qc, kc) * intra[:, None]
    o_intra = jnp.einsum('bhncs,bhnse->bhnce', scores, vc)
    q_decay = jnp.exp(lg * (idx + 1.0))
    k_decay = jnp.exp(lg * (RET_CHUNK - 1.0 - idx))
    chunk_decay = jnp.exp(log_gamma * RET_CHUNK)[None, :, None, None]
    kv = jnp.einsum('bhncd,hc,bhnce->nbhde', kc, k_decay, vc)

    def step(s, kv_n):
        return chunk_decay * s + kv_n, s

    _, s_prev = lax.scan(step, s0, kv)
    o_cross = jnp.einsum('bhncd,hc,nbhde->bhnce', qc, q_decay, s_prev)
    return (o_intra + o_cross).reshape(b, h, l, dv)

def retention_final_state(k, v, log_gamma):
    l = k.shape[2]
    w = jnp.exp(log_gamma[:, None] * (l - 1.0 - jnp.arange(l, dtype=jnp.float32)))
    return jnp.einsum('bhld,hl,bhle->bhde', k, w, v)

def retention_output(o, g, gn_w):
    b, h, l, dv = o.shape
    t = layernorm(o.transpose(0, 2, 1, 3), gn_w.reshape(h, dv), 0.0)
    return t.reshape(b, l, h * dv) * jax.nn.silu(g)

def diff_attend(q, k, v, lam):
    b, lq, h, _, dk = q.shape
    nb = lq // Q_BLOCK
    qb = jnp.moveaxis(q.reshape(b, nb, Q_BLOCK, h, 2, dk), 1, 0)
    scale = dk ** -0.5

    def block(qblk):
        s = jnp.einsum('bqhmd,bkhmd->bhmqk', qblk, k).astype(jnp.float32) * scale
        p = jax.nn.softmax(s, axis=-1)
        a = p[:, :, 0] - lam * p[:, :, 1]
        return jnp.einsum('bhqk,bkhe->bqhe', a.astype(v.dtype), v)

    o = lax.map(block, qb)
    return jnp.moveaxis(o, 0, 1).reshape(b, lq, h, v.shape[-1])

def diff_output(o, gn_w, lam_init):
    b, l, h, dv = o.shape
    return (rmsnorm(o, gn_w.reshape(h, dv)) * (1.0 - lam_init)).reshape(b, l, h * dv)

def conformer_conv(val, gate, conv_w, conv_b, ln_w, ln_b):
    u = val * jax.nn.sigmoid(gate)
    y = lax.conv_general_dilated(u, conv_w[:, None, :].astype(u.dtype), window_strides=(1,),
                                 padding=[(CONV_PAD, CONV_PAD)],
                                 dimension_numbers=('NWC', 'WIO', 'NWC'),
                                 feature_group_count=CONV_CH) + conv_b
    return jax.nn.silu(layernorm(y, ln_w, ln_b)).astype(val.dtype)

def sq_relu_mlp(h, w1, w2):
    return jnp.square(jax.nn.relu(h @ w1)) @ w2

def hybrid_mixer(hx, hc, w_in, ret_log_decay, ret_gn_w, diff_lam, lam_init, diff_gn_w,
                 conv_w, conv_b, conv_ln_w, conv_ln_b, w_out, rows, cols, need_ctx_out):
    b, l, _ = hx.shape
    lc = hc.shape[1]
    rq_x, rk_x, rv_x, rg_x, dq_x, dk_x, dv_x, cv_x, cg_x = split_proj(hx @ w_in)
    rq_c, rk_c, rv_c, rg_c, dq_c, dk_c, dv_c, cv_c, cg_c = split_proj(hc @ w_in)
    flip = lambda t: jnp.flip(t, axis=2)

    cos1, sin1 = rope_angles(jnp.arange(l), RET_DK)
    rk_scale = RET_DK ** -0.5
    q_lat = apply_rope(rq_x.reshape(b, l, RET_HEADS, RET_DK), cos1, sin1).transpose(0, 2, 1, 3)
    k_lat = (apply_rope(rk_x.reshape(b, l, RET_HEADS, RET_DK), cos1, sin1) * rk_scale).transpose(0, 2, 1, 3)
    v_lat = rv_x.reshape(b, l, RET_HEADS, RET_DV).transpose(0, 2, 1, 3)
    k_ctx = (rk_c.reshape(b, lc, RET_HEADS, RET_DK) * rk_scale).transpose(0, 2, 1, 3)
    v_ctx = rv_c.reshape(b, lc, RET_HEADS, RET_DV).transpose(0, 2, 1, 3)
    log_g = -jnp.exp(ret_log_decay.astype(jnp.float32))
    s_fwd = retention_final_state(k_ctx, v_ctx, log_g[0])
    s_bwd = retention_final_state(flip(k_ctx), flip(v_ctx), log_g[1])
    o_f = retention_chunkwise(q_lat, k_lat, v_lat, log_g[0], s_fwd)
    o_b = retention_chunkwise(flip(q_lat), flip(k_lat), flip(v_lat), log_g[1], s_bwd)
    ret_x = retention_output(o_f + flip(o_b), rg_x, ret_gn_w)

    dq_lat = axial_rope(dq_x.reshape(b, l, DIFF_HEADS, 2, DIFF_DK), rows, cols)
    dk_lat = axial_rope(dk_x.reshape(b, l, DIFF_HEADS, 2, DIFF_DK), rows, cols)
    dv_lat = dv_x.reshape(b, l, DIFF_HEADS, DIFF_DV)
    dk_ctx = dk_c.reshape(b, lc, DIFF_HEADS, 2, DIFF_DK)
    dv_ctx = dv_c.reshape(b, lc, DIFF_HEADS, DIFF_DV)
    lam = (jnp.exp(jnp.sum(diff_lam[0] * diff_lam[1])) - jnp.exp(jnp.sum(diff_lam[2] * diff_lam[3]))
           + lam_init).astype(jnp.float32)
    k_all = jnp.concatenate([dk_lat, dk_ctx], axis=1)
    v_all = jnp.concatenate([dv_lat, dv_ctx], axis=1)
    diff_x = diff_output(diff_attend(dq_lat, k_all, v_all, lam), diff_gn_w, lam_init)

    conv_x = conformer_conv(cv_x, cg_x, conv_w, conv_b, conv_ln_w, conv_ln_b)

    y_x = (jnp.concatenate([ret_x, diff_x, conv_x], axis=-1) @ w_out).astype(hx.dtype)
    if not need_ctx_out:
        return y_x, None

    q_ctx = rq_c.reshape(b, lc, RET_HEADS, RET_DK).transpose(0, 2, 1, 3)
    s0 = jnp.zeros((b, RET_HEADS, RET_DK, RET_DV), jnp.float32)
    oc_f = retention_chunkwise(q_ctx, k_ctx, v_ctx, log_g[0], s0)
    oc_b = retention_chunkwise(flip(q_ctx), flip(k_ctx), flip(v_ctx), log_g[1], s0)
    ret_c = retention_output(oc_f + flip(oc_b), rg_c, ret_gn_w)
    dq_ctx = dq_c.reshape(b, lc, DIFF_HEADS, 2, DIFF_DK)
    diff_c = diff_output(diff_attend(dq_ctx, dk_ctx, dv_ctx, lam), diff_gn_w, lam_init)
    conv_c = conformer_conv(cv_c, cg_c, conv_w, conv_b, conv_ln_w, conv_ln_b)
    y_c = (jnp.concatenate([ret_c, diff_c, conv_c], axis=-1) @ w_out).astype(hc.dtype)
    return y_x, y_c

def setup_inputs(seed: int = 0) -> dict:
    key = jax.random.key(seed)
    ks = jax.random.split(key, 24)
    nrm = lambda k, shape, s: jax.random.normal(k, shape, jnp.float32) * s
    gain = lambda k, shape: 1.0 + 0.1 * jax.random.normal(k, shape, jnp.float32)
    base_decay = jnp.log(-jnp.log(1.0 - 2.0 ** (-5.0 - jnp.arange(RET_HEADS, dtype=jnp.float32))))
    return {
        'x': nrm(ks[0], (BATCH, SEQ, D_MODEL), 1.0),
        'c': nrm(ks[1], (BATCH, D_MODEL), 1.0),
        'ctx': nrm(ks[2], (BATCH, CTX_LEN, D_MODEL), 1.0),
        'c_ctx': nrm(ks[3], (D_MODEL,), 1.0),
        'norm1_w': gain(ks[4], (DEPTH, D_MODEL)),
        'norm2_w': gain(ks[5], (DEPTH, D_MODEL)),
        'ada_w': nrm(ks[6], (DEPTH, D_MODEL, N_MOD * D_MODEL), 0.5 * D_MODEL ** -0.5),
        'ada_b': nrm(ks[7], (DEPTH, N_MOD * D_MODEL), 0.01),
        'w_in': nrm(ks[8], (DEPTH, D_MODEL, IN_WIDTH), D_MODEL ** -0.5),
        'ret_log_decay': base_decay[None, None, :] + nrm(ks[9], (DEPTH, 2, RET_HEADS), 0.05),
        'ret_gn_w': gain(ks[10], (DEPTH, RET_WIDTH)),
        'diff_lam': nrm(ks[11], (DEPTH, 4, DIFF_DK), 0.1),
        'diff_gn_w': gain(ks[12], (DEPTH, DIFF_WIDTH)),
        'conv_w': nrm(ks[13], (DEPTH, CONV_WIDTH, CONV_CH), CONV_WIDTH ** -0.5),
        'conv_b': nrm(ks[14], (DEPTH, CONV_CH), 0.01),
        'conv_ln_w': gain(ks[15], (DEPTH, CONV_CH)),
        'conv_ln_b': nrm(ks[16], (DEPTH, CONV_CH), 0.01),
        'w_out': nrm(ks[17], (DEPTH, MIX_WIDTH, D_MODEL), MIX_WIDTH ** -0.5),
        'mlp_w1': nrm(ks[18], (DEPTH, D_MODEL, D_FF), D_MODEL ** -0.5),
        'mlp_w2': nrm(ks[19], (DEPTH, D_FF, D_MODEL), D_FF ** -0.5),
        'final_norm_w': gain(ks[20], (D_MODEL,)),
    }

def reference(x, c, ctx, c_ctx, norm1_w, norm2_w, ada_w, ada_b, w_in, ret_log_decay, ret_gn_w,
              diff_lam, diff_gn_w, conv_w, conv_b, conv_ln_w, conv_ln_b, w_out, mlp_w1, mlp_w2,
              final_norm_w):
    l = x.shape[1]
    rows_n = l // GRID_W
    rows = jnp.repeat(jnp.arange(rows_n), GRID_W)
    cols = jnp.tile(jnp.arange(GRID_W), rows_n)
    silu_c = jax.nn.silu(c)
    silu_cc = jax.nn.silu(c_ctx)
    for i in range(DEPTH):
        last = i == DEPTH - 1
        lam_init = 0.8 - 0.6 * math.exp(-0.3 * i)
        mod_x = jnp.split((silu_c @ ada_w[i] + ada_b[i])[:, None, :], N_MOD, axis=-1)
        mod_c = jnp.split(silu_cc @ ada_w[i] + ada_b[i], N_MOD, axis=-1)
        hx = modulate(rmsnorm(x, norm1_w[i]), mod_x[0], mod_x[1])
        hc = modulate(rmsnorm(ctx, norm1_w[i]), mod_c[0], mod_c[1])
        y_x, y_c = hybrid_mixer(hx, hc, w_in[i], ret_log_decay[i], ret_gn_w[i], diff_lam[i], lam_init,
                                diff_gn_w[i], conv_w[i], conv_b[i], conv_ln_w[i], conv_ln_b[i], w_out[i],
                                rows, cols, not last)
        x = x + mod_x[2] * y_x
        hx2 = modulate(rmsnorm(x, norm2_w[i]), mod_x[3], mod_x[4])
        x = x + mod_x[5] * sq_relu_mlp(hx2, mlp_w1[i], mlp_w2[i])
        if not last:
            ctx = ctx + mod_c[2] * y_c
            hc2 = modulate(rmsnorm(ctx, norm2_w[i]), mod_c[3], mod_c[4])
            ctx = ctx + mod_c[5] * sq_relu_mlp(hc2, mlp_w1[i], mlp_w2[i])
    return rmsnorm(x, final_norm_w)


_drawn_inputs = setup_inputs


def setup_inputs(seed=0):
    import zlib

    import numpy as np

    out = dict(_drawn_inputs(seed))
    spreads = {}
    factors = {'ret_gn_w': 3.852,
     'diff_lam': 4.032,
     'conv_b': 8.0,
     'conv_ln_w': 3.663,
     'conv_ln_b': 36.574,
     'diff_gn_w': 2.673}
    for name, (base, spread) in spreads.items():
        noise = np.random.default_rng([zlib.crc32(name.encode()), seed]).standard_normal(out[name].shape)
        drawn = base * np.exp(spread * noise) if base else spread * noise
        out[name] = __import__('jax').numpy.asarray(drawn.astype(out[name].dtype))
    for name, factor in factors.items():
        out[name] = (out[name] * factor).astype(out[name].dtype)
    return out
```

```python
import math
from contextlib import ExitStack


import numpy as np

import concourse.bass as bass
from concourse import mybir

class NormSemaphores:

    def __init__(self, sem, name):
        self.squared, self.summed, self.total = sem(f"{name}_squared"), sem(f"{name}_summed"), sem(f"{name}_total")
        self.psum_free, self.rstd = sem(f"{name}_psum_free"), sem(f"{name}_rstd")
        self.normed, self.shifted = sem(f"{name}_normed"), sem(f"{name}_shifted")
        self.hi, self.lo = sem(f"{name}_hi"), sem(f"{name}_lo")


class NormBuffers:
    def __init__(self, sq, acc, rstd, tmp, ps):
        self.sq, self.acc, self.rstd, self.tmp, self.ps = sq, acc, rstd, tmp, ps


class Shared:
    pass


F32 = mybir.dt.float32
R32 = mybir.dt.float32r
ACT = mybir.ActivationFunctionType
ALU = mybir.AluOpType
AX = mybir.AxisListType.X

P = 128
D_MODEL, SEQ, CTX, DEPTH = 1024, 1024, 256, 2
T = SEQ + CTX
KT = D_MODEL // P
N_MOD = 6
D_FF = 4 * D_MODEL
EPS = 1e-6
GRID_W = 64
ROPE_BASE = 10000.0
DK = 64
HEADS = 4
TAPS = 31
PAD = (TAPS - 1) // 2
CONV_TILES = 2
NCH = T // P
NCH_X = SEQ // P
SLOT = KT * P
K_SCALE = DK ** -0.5

ADA_TILES = N_MOD * KT
IN_TILES = 24
OUT_TILES = KT
FF_CHUNK_TILES = 4
FF_CHUNKS = D_FF // (FF_CHUNK_TILES * P)
ADA0 = 0
IN0 = ADA0 + ADA_TILES
OUT0 = IN0 + IN_TILES
FF0 = OUT0 + OUT_TILES
FF_SLOTS = FF_CHUNK_TILES + KT // 2
LAYER_SLOTS = FF0 + FF_CHUNKS * FF_SLOTS

CV, CG, RQ, RK, RV, RG, DQ, DKK, DV = 0, 2, 4, 6, 8, 10, 12, 16, 20
STORED0 = RQ

U_X0 = PAD
U_C0 = PAD + SEQ + PAD
U_LEN = U_C0 + CTX + PAD
Y_C0 = SEQ + PAD
Y_LEN = Y_C0 + CTX

SV_COLS = {}
_at = 0
for _name, _n in (("n1w", KT), ("n2w", KT), ("adab", ADA_TILES), ("rgn", 2), ("dgn", 4), ("cw", CONV_TILES * TAPS),
                  ("cb", 2), ("clw", 2), ("clb", 2), ("lga", 8), ("lgp", 4), ("dlam", 4 * DK), ("final", KT)):
    SV_COLS[_name] = (_at, _at + _n)
    _at += _n
SV_LEN = _at

RT_RELF, RT_MASKF, RT_RELB, RT_MASKB, RT_QF, RT_QB, RT_BLK, RT_BLK64 = range(8)
RT_LEN = 8 * P + 2


def blocks(width):
    return [(a, min(a + 512, width)) for a in range(0, width, 512)]


def mm3(nc, out, w_hi, w_lo, x_hi, x_lo, start, stop):
    nc.tensor.matmul(out, w_hi, x_hi, start=start, stop=False)
    nc.tensor.matmul(out, w_hi, x_lo, start=False, stop=False)
    return nc.tensor.matmul(out, w_lo, x_hi, start=False, stop=stop)


def sv(e, name, a=0, n=1):
    lo, _ = SV_COLS[name]
    return e.SV[:, lo + a:lo + a + n]


def modulation_block(nc, e, layer):
    with ExitStack() as ctx:
        sem = lambda n: e.semaphore((f"{n}_m{layer}"))
        vectors_loaded, inputs_loaded, x_loaded = sem("vectors_loaded"), sem("inputs_loaded"), sem("x_loaded")
        slot_loaded = [sem("slot_loaded0"), sem("slot_loaded1")]
        cond_ready, constants_set, tile_summed, tile_biased, mod_chain = map(
            sem, ("cond_ready", "constants_set", "tile_summed", "tile_biased", "mod_chain"))
        stage = ctx.enter_context(nc.sbuf_tensor(f"ada_stage{layer}", [P, 2, SLOT], F32))
        ps = ctx.enter_context(nc.psum_tensor(f"ada_ps{layer}", [P, 2, 512], F32))
        block = ctx.enter_context(nc.Block())

        @block.sync
        def _(sp):
            sp.dma_start(e.SV[:], e.sv_dram[layer]).then_inc(vectors_loaded, 16)
            if layer == 0:
                sp.dma_start(e.COND[:], e.cond_dram).then_inc(inputs_loaded, 16)
                sp.dma_start(e.ID1[:], e.id1_dram).then_inc(inputs_loaded, 16)
            for u in range(2):
                sp.dma_start(stage[:, u], e.w_dram[layer, ADA0 + u]).then_inc(slot_loaded[u], 16)
            if layer == 0:
                for k in range(KT):
                    sp.dma_start(e.X[:, k], e.x_dram[k]).then_inc(x_loaded, 16)
            with sp.Fori(0, ADA_TILES // 2 - 1) as i:
                for u in range(2):
                    sp.wait_ge(tile_summed, 2 * i + u + 1)
                    sp.dma_start(stage[:, u], e.w_dram[layer, bass.ds(ADA0 + 2 + u + 2 * i, 1)].rearrange(
                        "a p c -> p (a c)")).then_inc(slot_loaded[u], 16)
            sp.wait_ge(vectors_loaded, 16)
            if layer == 0:
                sp.wait_ge(x_loaded, 16 * KT)

        @block.scalar
        def _(act):
            if layer == 0:
                act.wait_ge(inputs_loaded, 32)
                nc.scalar.activation(e.COND[:], e.COND[:], ACT.Silu).then_inc(cond_ready, 1)

        @block.tensor
        def _(pe):
            if layer == 0:
                pe.wait_ge(cond_ready, 1)
            with pe.Fori(0, ADA_TILES // 2) as i:
                for u in range(2):
                    pe.wait_ge(slot_loaded[u], 16 * i + 16)
                    pe.wait_ge(tile_biased, 2 * i + u + 1)
                    for k in range(KT):
                        last = nc.tensor.matmul(ps[:, u, 0:2], stage[:, u, k * P:(k + 1) * P], e.COND[:, k],
                                                start=k == 0, stop=k == KT - 1)
                    last.then_inc(tile_summed, 1)

        @block.vector
        def _(dve):
            if layer == 0:
                nc.vector.memset(e.EPS[:], EPS)
                nc.vector.memset(e.ONES[:], 1.0)
            nc.vector.memset(e.UNIT[:], 1.0).then_inc(tile_biased, 2)
            dve.wait_ge(vectors_loaded, 16)
            lo = SV_COLS["adab"][0]
            with dve.Fori(0, ADA_TILES // 2) as i:
                for u in range(2):
                    dve.wait_ge(tile_summed, 2 * i + u + 1)
                    nc.vector.tensor_scalar(e.MOD[:, bass.ds(4 * i + 2 * u, 2)], ps[:, u, 0:2],
                                            e.SV[:, bass.ds(lo + u + 2 * i, 1)], None, ALU.add).then_inc(tile_biased, 1)
            dve.wait_ge(tile_biased, ADA_TILES + 2)
            for gain, w, scale in ((e.GAIN1, "n1w", 1), (e.GAIN2, "n2w", 4)):
                w_ap = sv(e, w, 0, KT).rearrange("p (k a) -> p k a", a=1).to_broadcast([P, KT, 2])
                nc.vector.scalar_tensor_tensor(
                    gain[:], e.MOD[:, 2 * KT * scale:2 * KT * (scale + 1)].rearrange("p (k a) -> p k a", a=2), 1.0,
                    w_ap, ALU.add, ALU.mult).then_inc(mod_chain, 1)


def norm_act(nc, act, e, s, b, width):
    for k in range(KT):
        if k >= 2:
            act.wait_ge(s.summed, k - 1)
        nc.scalar.activation(b.sq[:, k % 2, 0:width], e.X[:, k, 0:width], ACT.Square).then_inc(s.squared, 1)
    act.wait_ge(s.total, 1)
    nc.scalar.activation(b.rstd[:, 0:width], b.ps[:, 0, 0:width], ACT.Ln, scale=1.0 / D_MODEL,
                         bias=e.EPS[:]).then_inc(s.psum_free, 2)
    act.wait_ge(s.psum_free, 2)
    nc.scalar.activation(b.rstd[:, 0:width], b.rstd[:, 0:width], ACT.Exp, scale=-0.5).then_inc(s.rstd, 1)
    per = 2 if width > SEQ else 1
    for k in range(KT):
        act.wait_ge(s.shifted, per * (k + 1))
        nc.scalar.activation(e.H_HI[:, k, 0:width], b.tmp[:, k % 3, 0:width], ACT.Copy).then_inc(s.hi, 1)


def norm_pe(nc, pe, e, s, b, width):
    pe.wait_ge(s.summed, KT)
    for a, z in blocks(width):
        last = nc.tensor.matmul(b.ps[:, 0, a:z], e.ONES[:], b.acc[:, a:z], start=True, stop=True)
    last.then_inc(s.total, 1)


def norm_dve(nc, dve, e, s, b, width):
    for k in range(KT):
        dve.wait_ge(s.squared, k + 1)
        if k == 0:
            nc.vector.tensor_copy(b.acc[:, 0:width], b.sq[:, 0, 0:width]).then_inc(s.summed, 1)
        else:
            dve.wait_ge(s.summed, k)
            nc.vector.tensor_tensor(b.acc[:, 0:width], b.acc[:, 0:width], b.sq[:, k % 2, 0:width],
                                    ALU.add).then_inc(s.summed, 1)
    dve.wait_ge(s.rstd, 1)
    for k in range(KT + 2):
        if k < KT:
            if k >= 3:
                dve.wait_ge(s.lo, k - 2)
            nc.vector.tensor_tensor(b.tmp[:, k % 3, 0:width], e.X[:, k, 0:width], b.rstd[:, 0:width],
                                    ALU.mult).then_inc(s.normed, 1)
        if k >= 2:
            j = k - 2
            dve.wait_ge(s.hi, j + 1)
            nc.vector.tensor_tensor(e.H_LO[:, j, 0:width], b.tmp[:, j % 3, 0:width],
                                    e.H_HI[:, j, 0:width].bitcast(F32), ALU.subtract).then_inc(s.lo, 1)


def norm_pool(nc, pool, e, s, b, width, gain, shift):
    for k in range(KT):
        pool.wait_ge(s.normed, k + 1)
        for j, (a, z) in enumerate(((0, SEQ), (SEQ, width))):
            if z > a:
                sh = 2 * (KT * shift + k) + j
                nc.gpsimd.tensor_scalar(b.tmp[:, k % 3, a:z], b.tmp[:, k % 3, a:z], gain[:, k, j:j + 1],
                                        e.MOD[:, sh:sh + 1], ALU.mult, ALU.add).then_inc(s.shifted, 1)


def projection_block(nc, e, layer):
    with ExitStack() as ctx:
        sem = lambda n: e.semaphore((f"{n}_p{layer}"))
        sb = lambda n, s, d=F32: ctx.enter_context(nc.sbuf_tensor(f"{n}_p{layer}", s, d))
        s = NormSemaphores(sem, "n1")
        slot_loaded = [sem("slot_loaded0"), sem("slot_loaded1")]
        w_hi_made, w_lo_made, tile_done = sem("w_hi_made"), sem("w_lo_made"), sem("tile_done")
        evacuated = s.psum_free
        table_loaded, rope_step, cos_made = sem("table_loaded"), sem("rope_step"), sem("cos_made")
        stored = [sem("stored0"), sem("stored1")]
        margins_zeroed, gated, conv_step, conv_stored, x_stored = map(
            sem, ("margins_zeroed", "gated", "conv_step", "conv_stored", "x_stored"))

        stage, w_hi, w_lo = sb("stage", [P, 2, SLOT]), sb("w_hi", [P, 2, SLOT], R32), sb("w_lo", [P, 2, SLOT], R32)
        raw, rot, cosx, table = sb("raw", [P, 2, T]), sb("rot", [P, T]), sb("cosx", [P, T]), sb("table", [P, 2, T])
        with nc.sbuf_tensor(f"tmp_p{layer}", [P, 3, T], F32) as tmp:
            pass
        u_buf, y_buf = sb("u_buf", [P, CONV_TILES, U_LEN]), sb("y_buf", [P, CONV_TILES, Y_LEN])
        ps = ctx.enter_context(nc.psum_tensor(f"ps_p{layer}", [P, 2, 3 * 512], F32))
        b = NormBuffers(sq=raw, acc=rot, rstd=cosx, tmp=tmp, ps=ps)
        block = ctx.enter_context(nc.Block())
        scratch = e.scratch[layer]

        out_of_psum = lambda n: n + 3

        @block.sync
        def _(sp):
            for u in range(2):
                sp.dma_start(stage[:, u], e.w_dram[layer, IN0 + u]).then_inc(slot_loaded[u], 16)
            sp.dma_start(table[:], e.rope_dram[0]).then_inc(table_loaded, 16)
            if layer > 0:
                for k in range(KT):
                    sp.dma_start(e.x_kept[k], e.X[:, k]).then_inc(x_stored, 16)

            def load(n, u):
                sp.wait_ge(w_lo_made, n + 1)
                sp.dma_start(stage[:, u], e.w_dram[layer, bass.ds(IN0 + 2 + n, 1)].rearrange(
                    "a p c -> p (a c)")).then_inc(slot_loaded[u], 16)

            def store(n, u):
                sp.dma_start(scratch[bass.ds(n, 1)].rearrange("a p c -> p (a c)"), raw[:, u]).then_inc(stored[u], 16)

            def store_conv(t):
                for (a, z), y in (((0, SEQ), 0), ((SEQ, T), Y_C0)):
                    sp.dma_start(scratch[t][:, a:z], y_buf[:, t, y:y + z - a]).then_inc(conv_stored, 16)

            for n in range(RQ):
                load(n, n % 2)
            for n in range(RQ, RV):
                load(n, n % 2)
                sp.wait_ge(rope_step, 3 * (n - RQ) + 3)
                store(n, n % 2)
            sp.dma_start(table[:], e.rope_dram[1]).then_inc(table_loaded, 16)
            for n in range(RV, DQ):
                load(n, n % 2)
                sp.wait_ge(evacuated, out_of_psum(n))
                store(n, n % 2)
            sp.wait_ge(conv_step, TAPS)
            store_conv(0)
            with sp.Fori(0, (DV - DQ) // 2) as i:
                for u in range(2):
                    load(DQ + u + 2 * i, u)
                    sp.wait_ge(rope_step, 3 * (RV - RQ) + 3 * u + 3 + 6 * i)
                    store(DQ + u + 2 * i, u)
            for n in range(DV, IN_TILES):
                if n < IN_TILES - 2:
                    load(n, n % 2)
                sp.wait_ge(evacuated, out_of_psum(n))
                store(n, n % 2)
            sp.wait_ge(conv_step, 2 * TAPS)
            store_conv(1)
            for u in range(2):
                sp.wait_ge(stored[u], 16 * (IN_TILES - STORED0) // 2)
            sp.wait_ge(conv_stored, 16 * 4)
            if layer > 0:
                sp.wait_ge(x_stored, 16 * KT)

        @block.scalar
        def _(act):
            def split(n, u):
                nc.scalar.activation(w_hi[:, u], stage[:, u], ACT.Copy).then_inc(w_hi_made, 1)

            for u in range(2):
                act.wait_ge(slot_loaded[u], 16)
                split(u, u)
            norm_act(nc, act, e, s, b, T)

            def tile(n, u, func, loads=True, load_count=None):
                act.wait_ge(tile_done, n + 1)
                nc.scalar.activation(raw[:, u], ps[:, u, 0:T], func).then_inc(evacuated, 1)
                if loads:
                    act.wait_ge(slot_loaded[u], load_count)
                    split(n + 2, u)

            loads_of = lambda n: 16 * (n // 2 + 2)
            act.wait_ge(margins_zeroed, 2)
            for n in range(CV, CG):
                act.wait_ge(tile_done, n + 1)
                nc.scalar.activation(u_buf[:, n - CV, U_X0:U_X0 + SEQ], ps[:, n % 2, 0:SEQ], ACT.Copy)
                nc.scalar.activation(u_buf[:, n - CV, U_C0:U_C0 + CTX], ps[:, n % 2, SEQ:T], ACT.Copy).then_inc(evacuated, 1)
                act.wait_ge(slot_loaded[n % 2], loads_of(n))
                split(n + 2, n % 2)
            for n in range(CG, RQ):
                tile(n, n % 2, ACT.Sigmoid, True, loads_of(n))
            for n in range(RQ, DQ):
                if n < RQ + 2:
                    act.wait_ge(gated, n - RQ + 1)
                else:
                    act.wait_ge(stored[n % 2], 16 * ((n - STORED0) // 2))
                tile(n, n % 2, ACT.Silu if n >= RG else ACT.Copy, True, loads_of(n))
            with act.Fori(0, (DV - DQ) // 2) as i:
                for u in range(2):
                    act.wait_ge(stored[u], 16 * ((DQ - STORED0) // 2) + 16 * i)
                    tile(DQ + u + 2 * i, u, ACT.Copy, True, loads_of(DQ) + 16 * i)
            for n in range(DV, IN_TILES):
                act.wait_ge(stored[n % 2], 16 * ((n - STORED0) // 2))
                tile(n, n % 2, ACT.Copy, n < IN_TILES - 2, loads_of(n))

        @block.tensor
        def _(pe):
            norm_pe(nc, pe, e, s, b, T)
            with pe.Fori(0, IN_TILES // 2) as i:
                for u in range(2):
                    pe.wait_ge(w_lo_made, 2 * i + u + 1)
                    pe.wait_ge(evacuated, 2 * i + u + 1)
                    for k in range(KT):
                        pe.wait_ge(s.lo, k + 1)
                        kk = slice(k * P, (k + 1) * P)
                        for a, z in blocks(T):
                            last = mm3(nc, ps[:, u, a:z], w_hi[:, u, kk], w_lo[:, u, kk], e.H_HI[:, k, a:z],
                                       e.H_LO[:, k, a:z], k == 0, k == KT - 1)
                    last.then_inc(tile_done, 1)

        @block.gpsimd
        def _(pool):
            norm_pool(nc, pool, e, s, b, T, e.GAIN1, 0)

            def rope_cos(n, r, u):
                pool.wait_ge(evacuated, out_of_psum(n))
                nc.gpsimd.tensor_tensor(cosx[:], raw[:, u], table[:, 0], ALU.mult).then_inc(cos_made, 1)

            pool.wait_ge(table_loaded, 16)
            for n in range(RQ, RV):
                if n > RQ:
                    pool.wait_ge(rope_step, 3 * (n - RQ))
                rope_cos(n, n - RQ, n % 2)
            pool.wait_ge(table_loaded, 32)
            with pool.Fori(0, (DV - DQ) // 2) as i:
                for u in range(2):
                    pool.wait_ge(rope_step, 3 * (RV - RQ) + 3 * u + 6 * i)
                    rope_cos(DQ + u + 2 * i, 0, u)

        @block.vector
        def _(dve):
            def split_rest(n, u):
                dve.wait_ge(w_hi_made, n + 1)
                nc.vector.tensor_tensor(w_lo[:, u], stage[:, u], w_hi[:, u].bitcast(F32),
                                        ALU.subtract).then_inc(w_lo_made, 1)

            split_rest(0, 0)
            split_rest(1, 1)
            norm_dve(nc, dve, e, s, b, T)
            dve.wait_ge(s.lo, KT)
            nc.vector.memset(u_buf[:, :, 0:PAD], 0.0)
            nc.vector.memset(u_buf[:, :, U_X0 + SEQ:U_C0], 0.0).then_inc(margins_zeroed, 1)
            nc.vector.memset(u_buf[:, :, U_C0 + CTX:U_LEN], 0.0).then_inc(margins_zeroed, 1)

            swap = [(p + 16) % 32 for p in range(32)]

            def rope(n, r3, u, cos_count, tables):
                dve.wait_ge(table_loaded, tables)
                dve.wait_ge(evacuated, out_of_psum(n))
                nc.vector.tensor_copy(e.SCRAP[:, 1:2], e.UNIT[:, 0:1])
                nc.vector.stream_shuffle(rot[:], raw[:, u], swap).then_inc(rope_step, 1)
                dve.wait_ge(rope_step, r3 + 1)
                nc.vector.tensor_tensor(rot[:], rot[:], table[:, 1], ALU.mult).then_inc(rope_step, 1)
                dve.wait_ge(cos_made, cos_count)
                dve.wait_ge(rope_step, r3 + 2)
                nc.vector.tensor_tensor(raw[:, u], rot[:], cosx[:], ALU.add).then_inc(rope_step, 1)

            w0, b0 = SV_COLS["cw"][0], SV_COLS["cb"][0]

            def tap(t, j, weight, count):
                dve.wait_ge(conv_step, count)
                nc.vector.scalar_tensor_tensor(y_buf[:, t], u_buf[:, t, bass.ds(j, Y_LEN)], e.SV[:, bass.ds(weight, 1)],
                                               y_buf[:, t], ALU.mult, ALU.add).then_inc(conv_step, 1)

            def first_tap(t):
                nc.vector.tensor_scalar(y_buf[:, t], u_buf[:, t, 0:Y_LEN], e.SV[:, w0 + t * TAPS:w0 + t * TAPS + 1],
                                        e.SV[:, b0 + t:b0 + t + 1], ALU.mult, ALU.add).then_inc(conv_step, 1)

            for n in range(CV, CG):
                split_rest(n + 2, n % 2)
            for n in range(CG, RQ):
                t = n - CG
                dve.wait_ge(evacuated, out_of_psum(n))
                for c0, a, z in ((U_X0, 0, SEQ), (U_C0, SEQ, T)):
                    g = nc.vector.tensor_tensor(u_buf[:, t, c0:c0 + z - a], u_buf[:, t, c0:c0 + z - a],
                                                raw[:, n % 2, a:z], ALU.mult)
                g.then_inc(gated, 1)
                split_rest(n + 2, n % 2)
            dve.wait_ge(gated, 2)
            taps_done = 0
            for n in range(RQ, DQ):
                if n < RV:
                    rope(n, 3 * (n - RQ), n % 2, n - RQ + 1, 16)
                split_rest(n + 2, n % 2)
                for _ in range(4):
                    if taps_done == 0:
                        first_tap(0)
                        taps_done = 1
                    elif taps_done < TAPS:
                        tap(0, taps_done, w0 + taps_done, taps_done)
                        taps_done += 1
            first_tap(1)
            with dve.Fori(0, (DV - DQ) // 2) as i:
                for u in range(2):
                    rope(DQ + u + 2 * i, 3 * (RV - RQ) + 3 * u + 6 * i, u, RV - RQ + 1 + u + 2 * i, 32)
                    split_rest(DQ + 2 + u + 2 * i, u)
                    for j in range(3):
                        q = 3 * u + j + 1
                        tap(1, 6 * i + q, w0 + TAPS + q + 6 * i, TAPS + q + 6 * i)
            for n in range(DV, IN_TILES):
                if n < IN_TILES - 2:
                    split_rest(n + 2, n % 2)
                for _ in range(2):
                    j = 1 + 3 * (DV - DQ) + 2 * (n - DV) + _
                    if j < TAPS:
                        tap(1, j, w0 + TAPS + j, TAPS + j)


def conv_norm_block(nc, e, layer):
    lam_init = 0.8 - 0.6 * math.exp(-0.3 * layer)
    with ExitStack() as ctx:
        sem = lambda n: e.semaphore((f"{n}_c{layer}"))
        sb = lambda n, s, d=F32: ctx.enter_context(nc.sbuf_tensor(f"{n}_c{layer}", s, d))
        loaded, tables_loaded, summed, centered, squared, varied, rstd_step, scaled, silu_step, hi_made, done = map(
            sem, ("loaded", "tables_loaded", "summed", "centered", "squared", "varied", "rstd_step", "scaled",
                  "silu_step", "hi_made", "done"))
        pa, pv = sem("prep_act"), sem("prep_dve")
        y, sq, rstd = sb("y", [P, 2, T]), sb("sq", [P, 2, T]), sb("rstd", [P, T])
        ef, eb = sb("ef", [P, HEADS, P]), sb("eb", [P, HEADS, P])
        lam_prod, lam_sum = sb("lam_prod", [P, 2, DK]), sb("lam_sum", [P, 4])
        ps = ctx.enter_context(nc.psum_tensor(f"ps_c{layer}", [P, 2, 3 * 512], F32))
        block = ctx.enter_context(nc.Block())
        rt = lambda i: e.RT[:, i * P:(i + 1) * P]

        @block.sync
        def _(sp):
            sp.dma_start(e.RT[:], e.rt_dram).then_inc(tables_loaded, 16)
            for t in range(CONV_TILES):
                sp.dma_start(y[:, t], e.scratch[layer][t]).then_inc(loaded, 16)

        @block.tensor
        def _(pe):
            pe.wait_ge(loaded, 32)
            for a, z in blocks(T):
                for t in range(CONV_TILES):
                    last = nc.tensor.matmul(ps[:, 0, a:z], e.ONES[:], y[:, t, a:z], start=t == 0, stop=t == 1)
            last.then_inc(summed, 1)
            pe.wait_ge(squared, 2)
            for a, z in blocks(T):
                for t in range(CONV_TILES):
                    last = nc.tensor.matmul(ps[:, 1, a:z], e.ONES[:], sq[:, t, a:z], start=t == 0, stop=t == 1)
            last.then_inc(varied, 1)

        @block.scalar
        def _(act):
            act.wait_ge(tables_loaded, 16)
            nc.scalar.activation(e.LGA[:], sv(e, "lga", 0, 8), ACT.Exp).then_inc(pa, 1)
            nc.scalar.activation(e.LGP[:], sv(e, "lgp", 0, 4), ACT.Exp).then_inc(pa, 1)
            act.wait_ge(pa, 2)
            nc.scalar.activation(e.LGA[:], e.LGA[:], ACT.Copy, scale=-1.0).then_inc(pa, 1)
            nc.scalar.activation(e.LGP[:], e.LGP[:], ACT.Copy, scale=-1.0).then_inc(pa, 1)
            act.wait_ge(pa, 4)
            nc.scalar.activation(e.CHUNK_DECAY[:], e.LGP[:], ACT.Exp, scale=float(P)).then_inc(pa, 1)
            for d in range(2):
                for p in range(2):
                    nc.scalar.activation(e.Q_DECAY[:, 2 * d + p], rt(RT_QF + d), ACT.Exp,
                                         scale=e.LGP[:, 2 * d + p:2 * d + p + 1]).then_inc(pa, 1)
                nc.scalar.activation(e.K_DECAY[:, d], e.LGA[:, 4 * d:4 * d + 4], ACT.Exp,
                                     scale=e.RT[:, 8 * P + d:8 * P + d + 1]).then_inc(pa, 1)
            act.wait_ge(pa, 11)
            nc.scalar.activation(e.K_DECAY[:], e.K_DECAY[:], ACT.Copy, scale=K_SCALE).then_inc(pa, 1)
            for h in range(HEADS):
                nc.scalar.activation(ef[:, h], rt(RT_RELF), ACT.Exp, scale=e.LGA[:, h:h + 1]).then_inc(pa, 1)
                nc.scalar.activation(eb[:, h], rt(RT_RELB), ACT.Exp, scale=e.LGA[:, 4 + h:5 + h]).then_inc(pa, 1)
            act.wait_ge(pv, 4)
            nc.scalar.activation(lam_sum[:, 2:4], lam_sum[:, 0:2], ACT.Exp).then_inc(pa, 1)
            for t in range(CONV_TILES):
                act.wait_ge(centered, t + 1)
                nc.scalar.activation(sq[:, t], y[:, t], ACT.Square).then_inc(squared, 1)
            act.wait_ge(varied, 1)
            nc.scalar.activation(rstd[:], ps[:, 1, 0:T], ACT.Ln, scale=1.0 / (CONV_TILES * P),
                                 bias=e.EPS[:]).then_inc(rstd_step, 1)
            act.wait_ge(rstd_step, 1)
            nc.scalar.activation(rstd[:], rstd[:], ACT.Exp, scale=-0.5).then_inc(rstd_step, 1)
            for t in range(CONV_TILES):
                act.wait_ge(scaled, t + 1)
                nc.scalar.activation(y[:, t], y[:, t], ACT.Silu, scale=sv(e, "clw", t), bias=sv(e, "clb", t)).then_inc(silu_step, 1)
                act.wait_ge(silu_step, t + 1)
                nc.scalar.activation(e.H_HI[:, 6 + t], y[:, t], ACT.Copy).then_inc(hi_made, 1)

        @block.vector
        def _(dve):
            for j in range(2):
                nc.vector.tensor_tensor(lam_prod[:, j], sv(e, "dlam", 2 * j * DK, DK), sv(e, "dlam", (2 * j + 1) * DK, DK),
                                        ALU.mult).then_inc(pv, 1)
            for j in range(2):
                dve.wait_ge(pv, j + 1)
                nc.vector.reduce_sum(lam_sum[:, j:j + 1], lam_prod[:, j], AX).then_inc(pv, 1)
            dve.wait_ge(pa, 20)
            for h in range(HEADS):
                nc.vector.scalar_tensor_tensor(ef[:, h], ef[:, h], K_SCALE, rt(RT_MASKF), ALU.mult, ALU.mult).then_inc(pv, 1)
                nc.vector.scalar_tensor_tensor(eb[:, h], eb[:, h], K_SCALE, rt(RT_MASKB), ALU.mult, ALU.mult).then_inc(pv, 1)
            dve.wait_ge(pv, 12)
            nc.vector.tensor_tensor(e.INTRA[:], ef[:], eb[:], ALU.add).then_inc(pv, 1)
            dve.wait_ge(pa, 21)
            nc.vector.tensor_tensor(e.NEG_LAM[:], lam_sum[:, 3:4], lam_sum[:, 2:3], ALU.subtract).then_inc(pv, 1)
            dve.wait_ge(pv, 14)
            nc.vector.tensor_scalar(e.NEG_LAM[:], e.NEG_LAM[:], -lam_init, None, ALU.add).then_inc(pv, 1)
            nc.vector.tensor_scalar(e.DGN[:], sv(e, "dgn", 0, 4), 1.0 - lam_init, None, ALU.mult).then_inc(pv, 1)
            dve.wait_ge(summed, 1)
            for t in range(CONV_TILES):
                nc.vector.scalar_tensor_tensor(y[:, t], ps[:, 0, 0:T], -1.0 / (CONV_TILES * P), y[:, t], ALU.mult,
                                               ALU.add).then_inc(centered, 1)
            dve.wait_ge(rstd_step, 2)
            for t in range(CONV_TILES):
                dve.wait_ge(squared, t + 1)
                dve.wait_ge(centered, t + 1)
                nc.vector.tensor_tensor(y[:, t], y[:, t], rstd[:], ALU.mult).then_inc(scaled, 1)
            for t in range(CONV_TILES):
                dve.wait_ge(hi_made, t + 1)
                nc.vector.tensor_tensor(e.H_LO[:, 6 + t], y[:, t], e.H_HI[:, 6 + t].bitcast(F32),
                                        ALU.subtract).then_inc(done, 1)


def retention_block(nc, e, layer):
    with ExitStack() as ctx:
        sem = lambda n: e.semaphore((f"{n}_r{layer}"))
        sb = lambda n, s, d=F32: ctx.enter_context(nc.sbuf_tensor(f"{n}_r{layer}", s, d))
        loaded, transposed, tok_made, kd_f, kd_b, q_f, q_b, kv_made, kv_masked, state_step, scored, decayed = map(
            sem, ("loaded", "transposed", "tok_made", "kd_f", "kd_b", "q_f", "q_b", "kv_made", "kv_masked",
                  "state_step", "scored", "decayed"))
        out_made, out_copied, mean_made, centered, squared, var_made, rstd_step, scaled, hi_made, pair_done = map(
            sem, ("out_made", "out_copied", "mean_made", "centered", "squared", "var_made", "rstd_step", "scaled",
                  "hi_made", "pair_done"))
        q, k, v, g = (sb(n, [P, T]) for n in "qkvg")
        ktok, vtok = sb("ktok", [P, NCH, P]), sb("vtok", [P, NCH, P])
        kd, qd = sb("kd", [P, 2, NCH, P]), sb("qd", [P, 2, NCH, P])
        state, prob = sb("state", [P, 2, NCH, P]), sb("prob", [P, 2, NCH, P])
        o, o2 = q, k
        ps = ctx.enter_context(nc.psum_tensor(f"ps_r{layer}", [P, 2, 3 * 512], F32))
        block = ctx.enter_context(nc.Block())
        scratch = e.scratch[layer]
        chunk = lambda n: slice(n * P, (n + 1) * P)
        chunks = lambda ap: ap.rearrange("p (n c) -> p n c", c=P)
        orders = ([NCH_X, NCH_X + 1] + list(range(NCH_X)), list(range(NCH))[::-1])

        @block.sync
        def _(sp):
            for p in range(2):
                if p:
                    sp.wait_ge(loaded, 64 * p)
                    sp.wait_ge(pair_done, p)
                for buf, n in ((k, RK), (v, RV), (q, RQ), (g, RG)):
                    sp.dma_start(buf[:], scratch[n + p]).then_inc(loaded, 16)

        @block.tensor
        def _(pe):
            with pe.Fori(0, 2) as p:
                pe.wait_ge(loaded, 64 * p + 64)
                for j, src in enumerate((k, v)):
                    for n in range(NCH):
                        last = nc.tensor.transpose(ps[:, j, chunk(n)], src[:, chunk(n)], e.IDENT)
                    last.then_inc(transposed, 1)
                pe.wait_ge(tok_made, 2 * p + 2)
                for j, ready in enumerate((kd_f, kd_b)):
                    pe.wait_ge(ready, p + 1)
                    for n in range(NCH):
                        last = nc.tensor.matmul(ps[:, j, chunk(n)], kd[:, j, n], vtok[:, n], start=True, stop=True)
                    last.then_inc(kv_made, 1)
                for j in range(2):
                    pe.wait_ge(kv_masked, 2 * p + j + 1)
                    rows = slice(64 * j, 64 * j + 64)
                    for n in range(NCH):
                        last = nc.tensor.matmul(ps[:, j, chunk(n)], k[rows, chunk(n)], q[rows, chunk(n)], start=True, stop=True)
                    last.then_inc(scored, 1)
                pe.wait_ge(decayed, 2 * p + 2)
                pe.wait_ge(q_f, p + 1)
                pe.wait_ge(q_b, p + 1)
                for n in range(NCH):
                    nc.tensor.matmul(ps[:, 0, chunk(n)], state[:, 0, n], qd[:, 0, n], start=True, stop=False)
                    nc.tensor.matmul(ps[:, 0, chunk(n)], state[:, 1, n], qd[:, 1, n], start=False, stop=True)
                    for j in range(2):
                        last = nc.tensor.matmul(ps[64 * j:64 * j + 64, 0, chunk(n)], vtok[:, n, 64 * j:64 * j + 64],
                                                prob[:, j, n], start=False, stop=True, skip_group_check=True)
                last.then_inc(out_made, 1)
                pe.wait_ge(out_copied, p + 1)
                for a, z in blocks(T):
                    last = nc.tensor.matmul(ps[:, 1, a:z], e.RT[:, RT_BLK64 * P:(RT_BLK64 + 1) * P], o[:, a:z], start=True, stop=True)
                last.then_inc(mean_made, 1)
                pe.wait_ge(squared, p + 1)
                for a, z in blocks(T):
                    last = nc.tensor.matmul(ps[:, 0, a:z], e.RT[:, RT_BLK64 * P:(RT_BLK64 + 1) * P], o2[:, a:z], start=True, stop=True)
                last.then_inc(var_made, 1)

        @block.scalar
        def _(act):
            with act.Fori(0, 2) as p:
                for j, dst in enumerate((ktok, vtok)):
                    act.wait_ge(transposed, 2 * p + j + 1)
                    nc.scalar.activation(dst[:].rearrange("p n c -> p (n c)"), ps[:, j, 0:T], ACT.Copy).then_inc(tok_made, 1)
                act.wait_ge(out_made, p + 1)
                nc.scalar.activation(o[:], ps[:, 0, 0:T], ACT.Copy).then_inc(out_copied, 1)
                act.wait_ge(centered, p + 1)
                nc.scalar.activation(o2[:], o[:], ACT.Square).then_inc(squared, 1)
                act.wait_ge(var_made, p + 1)
                nc.scalar.activation(o2[:], ps[:, 0, 0:T], ACT.Ln, bias=e.EPS[:]).then_inc(rstd_step, 1)
                act.wait_ge(rstd_step, 2 * p + 1)
                nc.scalar.activation(o2[:], o2[:], ACT.Exp, scale=-0.5).then_inc(rstd_step, 1)
                act.wait_ge(scaled, 2 * p + 2)
                nc.scalar.activation(e.H_HI[:, bass.ds(p, 1)].rearrange("p a t -> p (a t)"), o[:], ACT.Copy).then_inc(hi_made, 1)

        def k_decay(j, p):
            return (e.K_DECAY[:, j, bass.ds(2 * p, 2)].rearrange("p (a h b) -> p a h b", a=1, b=1)
                    .to_broadcast([P, NCH, 2, DK]))

        def by_head(ap):
            return ap.rearrange("p n (h d) -> p n h d", h=2)

        def q_decay(j, p):
            return e.Q_DECAY[:, bass.ds(2 * j + p, 1)].to_broadcast([P, NCH, P])

        @block.gpsimd
        def _(pool):
            with pool.Fori(0, 2) as p:
                pool.wait_ge(loaded, 64 * p + 64)
                nc.gpsimd.tensor_tensor(qd[:, 1], chunks(q[:]), q_decay(1, p), ALU.mult).then_inc(q_b, 1)
                pool.wait_ge(tok_made, 2 * p + 1)
                nc.gpsimd.tensor_tensor(by_head(kd[:, 1]), by_head(ktok[:]), k_decay(1, p), ALU.mult).then_inc(kd_b, 1)

        @block.vector
        def _(dve):
            with dve.Fori(0, 2) as p:
                dve.wait_ge(loaded, 64 * p + 64)
                nc.vector.tensor_tensor(qd[:, 0], chunks(q[:]), q_decay(0, p), ALU.mult).then_inc(q_f, 1)
                dve.wait_ge(tok_made, 2 * p + 1)
                nc.vector.tensor_tensor(by_head(kd[:, 0]), by_head(ktok[:]), k_decay(0, p), ALU.mult).then_inc(kd_f, 1)
                for j in range(2):
                    first = nc.vector.memset(state[:, j, orders[j][0]], 0.0)
                first.then_inc(state_step, 1)
                mask = e.RT[:, RT_BLK * P:(RT_BLK + 1) * P].rearrange("p (a c) -> p a c", a=1).to_broadcast([P, NCH, P])
                for j in range(2):
                    dve.wait_ge(kv_made, 2 * p + j + 1)
                    nc.vector.tensor_tensor(prob[:, j], chunks(ps[:, j, 0:T]), mask, ALU.mult).then_inc(kv_masked, 1)
                dve.wait_ge(kv_masked, 2 * p + 2)
                for a, z in zip(range(NCH - 1), range(1, NCH)):
                    for j in range(2):
                        dve.wait_ge(state_step, (2 * (NCH - 1) + 1) * p + (2 * a + j if a else 1))
                        nc.vector.scalar_tensor_tensor(
                            state[:, j, orders[j][z]], state[:, j, orders[j][a]], e.CHUNK_DECAY[:, bass.ds(2 * j + p, 1)],
                            prob[:, j, orders[j][a]], ALU.mult, ALU.add).then_inc(state_step, 1)
                dve.wait_ge(state_step, (2 * (NCH - 1) + 1) * (p + 1))
                for j in range(2):
                    dve.wait_ge(scored, 2 * p + j + 1)
                    nc.vector.tensor_tensor(prob[:, j], chunks(ps[:, j, 0:T]),
                                            e.INTRA[:, bass.ds(2 * p + j, 1)].to_broadcast([P, NCH, P]),
                                            ALU.mult).then_inc(decayed, 1)
                dve.wait_ge(mean_made, p + 1)
                nc.vector.tensor_tensor(o[:], o[:], ps[:, 1, 0:T], ALU.subtract).then_inc(centered, 1)
                dve.wait_ge(rstd_step, 2 * p + 2)
                dve.wait_ge(centered, p + 1)
                nc.vector.tensor_tensor(o[:], o[:], o2[:], ALU.mult).then_inc(scaled, 1)
                dve.wait_ge(scaled, 2 * p + 1)
                gw = SV_COLS["rgn"][0]
                nc.vector.scalar_tensor_tensor(o[:], o[:], e.SV[:, bass.ds(gw + p, 1)], g[:], ALU.mult, ALU.mult).then_inc(scaled, 1)
                dve.wait_ge(hi_made, p + 1)
                nc.vector.tensor_tensor(e.H_LO[:, bass.ds(p, 1)].rearrange("p a t -> p (a t)"), o[:],
                                        e.H_HI[:, bass.ds(p, 1)].rearrange("p a t -> p (a t)").bitcast(F32),
                                        ALU.subtract).then_inc(pair_done, 1)


def attention_block(nc, e, layer, last_layer):
    n_q = NCH_X if last_layer else NCH
    width = n_q * P
    keys_of = lambda i: (0, T) if i < NCH_X else (SEQ, T)
    n_keys = lambda i: keys_of(i)[1] - keys_of(i)[0]
    in_fours = lambda n: [list(range(a, min(a + 4, n))) for a in range(0, n, 4)]
    rounds_of = lambda i: in_fours(n_keys(i) // P)
    v_rounds = in_fours(NCH)
    first_round = [len(v_rounds)]
    for i in range(n_q):
        first_round.append(first_round[-1] + len(rounds_of(i)))
    per_head = first_round[-1]
    e0_buffer = [i % 4 for i in range(n_q)] if n_q % 4 == 0 else [i % 3 for i in range(n_q - 1)] + [3]

    with ExitStack() as ctx:
        sem = lambda n: e.semaphore(f"{n}_a{layer}")
        sb = lambda n, s, d=F32: ctx.enter_context(nc.sbuf_tensor(f"{n}_a{layer}", s, d))
        v_loaded, qk_loaded, scored, max_step, exped, recip_step, scaled1, combined = map(
            sem, ("v_loaded", "qk_loaded", "scored", "max_step", "exped", "recip_step", "scaled1", "combined"))
        transposed, t_copied, av_made, o_copied = map(sem, ("transposed", "t_copied", "av_made", "o_copied"))
        squared, total, rstd_step, normed, hi_made, lo_made = map(
            sem, ("squared", "total", "rstd_step", "normed", "hi_made", "lo_made"))
        q, k, v = (sb(n, [P, T]) for n in "qkv")
        vtok, at = sb("vtok", [P, NCH, P]), sb("at", [P, NCH, P])
        ex0, ex1 = sb("ex0", [P, 4, T]), sb("ex1", [P, 2, T])
        o_all = sb("o_all", [P, HEADS, T])
        peak, neg_peak, total_e, recip = (sb(n, [P, 2, 2]) for n in ("peak", "neg_peak", "total_e", "recip"))
        ps = ctx.enter_context(nc.psum_tensor(f"ps_a{layer}", [P, 2, 3 * 512], F32))
        ps_t = ctx.enter_context(nc.psum_tensor(f"ps_t{layer}", [P, 512], F32))
        ps_o = ctx.enter_context(nc.psum_tensor(f"ps_o{layer}", [P, 512], F32))
        block = ctx.enter_context(nc.Block())
        scratch = e.scratch[layer]
        chunk = lambda n: slice(n * P, (n + 1) * P)

        def after(h, i):
            return (h, i + 1) if i + 1 < n_q else (h + 1, 0)

        @block.sync
        def _(sp):
            for buf, n, loaded in ((v, DV, v_loaded), (k, DKK, qk_loaded), (q, DQ, qk_loaded)):
                sp.dma_start(buf[:], scratch[n]).then_inc(loaded, 16)
            with sp.Fori(0, HEADS - 1) as h:
                def load(buf, n, loaded):
                    sp.dma_start(buf[:], scratch[bass.ds(n + 1 + h, 1)].rearrange("a p c -> p (a c)")).then_inc(loaded, 16)

                sp.wait_ge(v_loaded, 16 * h + 16)
                sp.wait_ge(transposed, per_head * h + len(v_rounds))
                load(v, DV, v_loaded)
                sp.wait_ge(qk_loaded, 32 * h + 32)
                sp.wait_ge(scored, 2 * n_q * h + 2 * n_q)
                load(k, DKK, qk_loaded)
                load(q, DQ, qk_loaded)

        @block.tensor
        def _(pe):
            def transposes(h, r, src, ids):
                pe.wait_ge(t_copied, per_head * h + r + 1)
                for n in ids:
                    t = nc.tensor.transpose(ps_t[:, (n - ids[0]) * P:(n - ids[0] + 1) * P], src[:, chunk(n)], e.IDENT)
                t.then_inc(transposed, 1)

            def scores(h, i, m):
                a0, z0 = keys_of(i)
                rows = slice(64 * m, 64 * m + 64)
                pe.wait_ge(exped, 2 * n_q * h + 2 * i + m + 1)
                for a, z in blocks(z0 - a0):
                    t = nc.tensor.matmul(ps[:, m, a:z], q[rows, chunk(i)], k[rows, a0 + a:a0 + z], start=True, stop=True)
                t.then_inc(scored, 1)

            def values(h, i, r, ids):
                pe.wait_ge(t_copied, per_head * h + first_round[i] + r + 2)
                for n in ids:
                    t = nc.tensor.matmul(ps_o[:, 0:P], vtok[:, keys_of(i)[0] // P + n], at[:, n], start=n == 0,
                                         stop=n == n_keys(i) // P - 1)
                return t

            def v_transposes(h):
                pe.wait_ge(v_loaded, 16 * h + 16)
                for r, ids in enumerate(v_rounds):
                    transposes(h, r, v, ids)

            def step(nxt, prev):
                if nxt is not None:
                    if nxt[1] == 0:
                        pe.wait_ge(qk_loaded, 32 * nxt[0] + 32)
                    scores(*nxt, 0)
                h, i = prev
                rounds = rounds_of(i)
                pe.wait_ge(combined, n_q * h + i + 1)
                transposes(h, first_round[i], ex0[:, e0_buffer[i]], rounds[0])
                if nxt is not None:
                    scores(*nxt, 1)
                if len(rounds) > 1:
                    transposes(h, first_round[i] + 1, ex0[:, e0_buffer[i]], rounds[1])
                pe.wait_ge(o_copied, n_q * h + i + 1)
                for r, ids in enumerate(rounds):
                    t = values(h, i, r, ids)
                    if r + 2 < len(rounds):
                        transposes(h, first_round[i] + r + 2, ex0[:, e0_buffer[i]], rounds[r + 2])
                t.then_inc(av_made, 1)

            v_transposes(0)
            pe.wait_ge(qk_loaded, 32)
            for i in range(2):
                for m in range(2):
                    scores(0, i, m)
            with pe.Fori(0, HEADS - 1) as h:
                for i in range(1, n_q):
                    step(after(h, i), (h, i - 1))
                step((h + 1, 1), (h, n_q - 1))
                v_transposes(h + 1)
            for i in range(1, n_q):
                step(after(HEADS - 1, i) if i + 1 < n_q else None, (HEADS - 1, i - 1))
            step(None, (HEADS - 1, n_q - 1))
            for h in range(HEADS):
                pe.wait_ge(squared, h + 1)
                if h >= 2:
                    pe.wait_ge(rstd_step, 2 * (h - 2) + 1)
                for a, z in blocks(width):
                    t = nc.tensor.matmul(ps[:, h % 2, a:z], e.ONES[:], ex0[:, h % 2, a:z], start=True, stop=True)
                t.then_inc(total, 1)

        @block.scalar
        def _(act):
            def copy_round(h, r, dst):
                act.wait_ge(transposed, per_head * h + r + 1)
                nc.scalar.activation(dst.rearrange("p n c -> p (n c)"), ps_t[:, 0:dst.shape[1] * P],
                                     ACT.Copy).then_inc(t_copied, 1)

            def exp(h, i, m):
                n, dst = n_keys(i), ex1[:, i % 2] if m else ex0[:, e0_buffer[i]]
                act.wait_ge(max_step, 4 * n_q * h + 4 * i + 2 * m + 2)
                nc.scalar.activation(dst[:, 0:n], ps[:, m, 0:n], ACT.Exp, bias=neg_peak[:, i % 2, m:m + 1],
                                     scale=K_SCALE, accum_out=total_e[:, i % 2, m:m + 1]).then_inc(exped, 1)

            def v_copies(h):
                for r, ids in enumerate(v_rounds):
                    copy_round(h, r, vtok[:, ids[0]:ids[-1] + 1])

            def step(nxt, prev):
                h, i = prev
                for r, ids in enumerate(rounds_of(i)):
                    copy_round(h, first_round[i] + r, at[:, ids[0]:ids[-1] + 1])
                    if r == 0 and nxt is not None:
                        exp(*nxt, 0)
                if nxt is not None:
                    exp(*nxt, 1)
                act.wait_ge(av_made, n_q * h + i + 1)
                nc.scalar.activation(o_all[:, bass.ds(h, 1), chunk(i)].rearrange("p a t -> p (a t)"), ps_o[:, 0:P],
                                     ACT.Copy).then_inc(o_copied, 1)

            nc.scalar.activation(neg_peak[:, 0], e.UNIT[:, 0:2], ACT.Copy).then_inc(exped, 2)
            nc.scalar.activation(neg_peak[:, 1], e.UNIT[:, 0:2], ACT.Copy).then_inc(t_copied, 1)
            nc.scalar.activation(recip[:, 0], e.UNIT[:, 0:2], ACT.Copy).then_inc(o_copied, 1)
            v_copies(0)
            for i in range(2):
                for m in range(2):
                    exp(0, i, m)
            with act.Fori(0, HEADS - 1) as h:
                for i in range(1, n_q):
                    step(after(h, i), (h, i - 1))
                step((h + 1, 1), (h, n_q - 1))
                v_copies(h + 1)
            for i in range(1, n_q):
                step(after(HEADS - 1, i) if i + 1 < n_q else None, (HEADS - 1, i - 1))
            step(None, (HEADS - 1, n_q - 1))
            act.wait_ge(o_copied, n_q * HEADS + 1)

            def square(h):
                if h >= 2:
                    act.wait_ge(total, h - 1)
                nc.scalar.activation(ex0[:, h % 2, 0:width], o_all[:, h, 0:width], ACT.Square).then_inc(squared, 1)

            square(0)
            square(1)
            for h in range(HEADS):
                act.wait_ge(total, h + 1)
                if h >= 2:
                    act.wait_ge(normed, h - 1)
                nc.scalar.activation(ex1[:, h % 2, 0:width], ps[:, h % 2, 0:width], ACT.Ln, scale=1.0 / P,
                                     bias=e.EPS[:]).then_inc(rstd_step, 1)
                act.wait_ge(rstd_step, 2 * h + 1)
                nc.scalar.activation(ex1[:, h % 2, 0:width], ex1[:, h % 2, 0:width], ACT.Exp, scale=-0.5).then_inc(rstd_step, 1)
                if h + 2 < HEADS:
                    square(h + 2)
                act.wait_ge(normed, h + 1)
                nc.scalar.activation(e.H_HI[:, 2 + h, 0:width], o_all[:, h, 0:width], ACT.Copy).then_inc(hi_made, 1)

        @block.gpsimd
        def _(pool):
            with pool.Fori(0, HEADS) as h:
                for i in range(n_q):
                    n = n_keys(i)
                    pool.wait_ge(recip_step, 2 * n_q * h + 2 * i + 2)
                    nc.gpsimd.tensor_tensor(e.POOL_SCRAP[:], e.UNIT[:], e.UNIT[:], ALU.mult)
                    nc.gpsimd.tensor_scalar(ex1[:, i % 2, 0:n], ex1[:, i % 2, 0:n], recip[:, i % 2, 1:2], 1.0,
                                            ALU.mult, ALU.mult).then_inc(scaled1, 1)

        @block.vector
        def _(dve):
            def peaks(h, i, m):
                dve.wait_ge(scored, 2 * n_q * h + 2 * i + m + 1)
                nc.vector.reduce_max(peak[:, i % 2, m:m + 1], ps[:, m, 0:n_keys(i)], AX).then_inc(max_step, 1)
                dve.wait_ge(max_step, 4 * n_q * h + 4 * i + 2 * m + 1)
                nc.vector.tensor_scalar(neg_peak[:, i % 2, m:m + 1], peak[:, i % 2, m:m + 1], -K_SCALE, None,
                                        ALU.mult).then_inc(max_step, 1)

            def combine(h, i):
                n, c, e0 = n_keys(i), 2 * n_q * h + 2 * i, ex0[:, e0_buffer[i]]
                dve.wait_ge(exped, c + 4)
                nc.vector.reciprocal(recip[:, i % 2], total_e[:, i % 2]).then_inc(recip_step, 1)
                dve.wait_ge(recip_step, c + 1)
                nc.vector.tensor_tensor(recip[:, i % 2, 1:2], recip[:, i % 2, 1:2], e.NEG_LAM[:], ALU.mult).then_inc(recip_step, 1)
                dve.wait_ge(scaled1, n_q * h + i + 1)
                nc.vector.scalar_tensor_tensor(e0[:, 0:n], e0[:, 0:n], recip[:, i % 2, 0:1], ex1[:, i % 2, 0:n],
                                               ALU.mult, ALU.add).then_inc(combined, 1)

            def step(h, i, nxt):
                if nxt is not None:
                    peaks(*nxt, 0)
                combine(h, i)
                if nxt is not None:
                    peaks(*nxt, 1)

            dve.wait_ge(o_copied, 1)
            peaks(0, 0, 0)
            peaks(0, 0, 1)
            with dve.Fori(0, HEADS - 1) as h:
                for i in range(n_q):
                    step(h, i, after(h, i))
            for i in range(n_q):
                step(HEADS - 1, i, after(HEADS - 1, i) if i + 1 < n_q else None)
            for h in range(HEADS):
                dve.wait_ge(rstd_step, 2 * h + 2)
                nc.vector.scalar_tensor_tensor(o_all[:, h, 0:width], o_all[:, h, 0:width], e.DGN[:, h:h + 1],
                                               ex1[:, h % 2, 0:width], ALU.mult, ALU.mult).then_inc(normed, 1)
                dve.wait_ge(hi_made, h + 1)
                nc.vector.tensor_tensor(e.H_LO[:, 2 + h, 0:width], o_all[:, h, 0:width],
                                        e.H_HI[:, 2 + h, 0:width].bitcast(F32), ALU.subtract).then_inc(lo_made, 1)


def mlp_block(nc, e, layer, last_layer):
    width = SEQ if last_layer else T
    sides = [(0, 0, SEQ)] + ([] if last_layer else [(1, SEQ, T)])
    with ExitStack() as ctx:
        sem = lambda n: e.semaphore((f"{n}_f{layer}"))
        sb = lambda n, s, d=F32: ctx.enter_context(nc.sbuf_tensor(f"{n}_f{layer}", s, d))
        s = NormSemaphores(sem, "n2")
        slot_loaded = [sem("slot_loaded0"), sem("slot_loaded1")]
        w_hi_made, w_lo_made, out_done, out_added, x_loaded = map(
            sem, ("w_hi_made", "w_lo_made", "out_done", "out_added", "x_loaded"))
        up_done, up_relu, up_squared, g_hi_made, g_lo_made, down_done, down_added = map(
            sem, ("up_done", "up_relu", "up_squared", "g_hi_made", "g_lo_made", "down_done", "down_added"))
        stage, w_hi, w_lo = sb("stage", [P, 2, SLOT]), sb("w_hi", [P, 2, SLOT], R32), sb("w_lo", [P, 2, SLOT], R32)
        with ExitStack() as inner:
            tb = lambda n, s: inner.enter_context(nc.sbuf_tensor(f"{n}_f{layer}", s, F32))
            sq, acc, rstd, tmp = tb("sq", [P, 2, T]), tb("acc", [P, T]), tb("rstd", [P, T]), tb("tmp", [P, 3, T])
        g_hi, g_lo = sb("g_hi", [P, FF_CHUNK_TILES, T], R32), sb("g_lo", [P, FF_CHUNK_TILES, T], R32)
        hidden = sb("hidden", [P, 2, T])
        ps = ctx.enter_context(nc.psum_tensor(f"ps_f{layer}", [P, 2, 3 * 512], F32))
        b = NormBuffers(sq=sq, acc=acc, rstd=rstd, tmp=tmp, ps=ps)
        block = ctx.enter_context(nc.Block())
        slots = OUT_TILES + FF_CHUNKS * FF_SLOTS
        up0, down0 = OUT_TILES, OUT_TILES + FF_CHUNK_TILES

        @block.sync
        def _(sp):
            for u in range(2):
                sp.dma_start(stage[:, u], e.w_dram[layer, OUT0 + u]).then_inc(slot_loaded[u], 16)
            for k in range(KT):
                sp.dma_start(e.X[:, k, 0:width], (e.x_dram if layer == 0 else e.x_kept)[k][:, 0:width]).then_inc(x_loaded, 16)
            with sp.Fori(0, slots // 2 - 1) as i:
                for u in range(2):
                    sp.wait_ge(w_lo_made, 2 * i + u + 1)
                    sp.dma_start(stage[:, u], e.w_dram[layer, bass.ds(OUT0 + 2 + u + 2 * i, 1)].rearrange(
                        "a p c -> p (a c)")).then_inc(slot_loaded[u], 16)

        @block.scalar
        def _(act):
            def split(u, count):
                act.wait_ge(slot_loaded[u], count)
                nc.scalar.activation(w_hi[:, u], stage[:, u], ACT.Copy).then_inc(w_hi_made, 1)

            nc.scalar.activation(e.SCRAP[:, 0:1], e.UNIT[:, 0:1], ACT.Copy).then_inc(out_added, 2)
            split(0, 16)
            split(1, 16)
            with act.Fori(0, OUT_TILES // 2) as i:
                for u in range(2):
                    act.wait_ge(out_done, 2 * i + u + 1)
                    split(u, 16 * i + 32)
            act.wait_ge(out_added, OUT_TILES + 2)
            norm_act(nc, act, e, s, b, width)

            def split_after(n, c):
                split(n % 2, 16 * (n // 2 + 2) + 16 * (FF_SLOTS // 2) * c)

            def up(c, j):
                act.wait_ge(up_done, FF_CHUNK_TILES * c + j + 1)
                if j >= 2:
                    act.wait_ge(g_lo_made, FF_CHUNK_TILES * c + j - 1)
                nc.scalar.activation(hidden[:, j % 2, 0:width], ps[:, j % 2, 0:width], ACT.Relu).then_inc(up_relu, 1)
                act.wait_ge(up_relu, FF_CHUNK_TILES * c + j + 1)
                nc.scalar.activation(hidden[:, j % 2, 0:width], hidden[:, j % 2, 0:width], ACT.Square).then_inc(up_squared, 1)
                act.wait_ge(up_squared, FF_CHUNK_TILES * c + j + 1)
                nc.scalar.activation(g_hi[:, j, 0:width], hidden[:, j % 2, 0:width], ACT.Copy).then_inc(g_hi_made, 1)
                split_after(up0 + j, c)

            def down(c, j, more):
                act.wait_ge(down_done, KT * c + 2 * j + 2)
                if more:
                    split_after(down0 + j, c)

            with act.Fori(0, FF_CHUNKS - 1) as c:
                for j in range(FF_CHUNK_TILES):
                    up(c, j)
                for j in range(KT // 2):
                    down(c, j, True)
            for j in range(FF_CHUNK_TILES):
                up(FF_CHUNKS - 1, j)
            for j in range(KT // 2):
                down(FF_CHUNKS - 1, j, j < KT // 2 - 2)

        @block.tensor
        def _(pe):
            def product(u, j, x_hi, x_lo, first, n_k, ready, count):
                for k in range(n_k):
                    if ready is not None:
                        pe.wait_ge(ready, count + k + 1)
                    kk = slice((first + k) * P, (first + k + 1) * P)
                    for a, z in blocks(width):
                        last = mm3(nc, ps[:, u, a:z], w_hi[:, j, kk], w_lo[:, j, kk], x_hi[:, k, a:z],
                                   x_lo[:, k, a:z], k == 0, k == n_k - 1)
                return last

            with pe.Fori(0, OUT_TILES // 2) as i:
                for u in range(2):
                    pe.wait_ge(w_lo_made, 2 * i + u + 1)
                    pe.wait_ge(out_added, 2 * i + u + 1)
                    product(u, u, e.H_HI, e.H_LO, 0, KT, None, 0).then_inc(out_done, 1)
            norm_pe(nc, pe, e, s, b, width)
            with pe.Fori(0, FF_CHUNKS) as c:
                for j in range(FF_CHUNK_TILES):
                    pe.wait_ge(w_lo_made, up0 + 1 + j + FF_SLOTS * c)
                    if j < 2:
                        pe.wait_ge(down_added, KT * c + 1 + j)
                    else:
                        pe.wait_ge(up_relu, FF_CHUNK_TILES * c + j - 1)
                    product(j % 2, j % 2, e.H_HI, e.H_LO, 0, KT, s.lo, 0).then_inc(up_done, 1)
                for m in range(KT):
                    j = m // 2
                    pe.wait_ge(w_lo_made, down0 + 1 + j + FF_SLOTS * c)
                    if m < 2:
                        pe.wait_ge(up_relu, FF_CHUNK_TILES * c + 3 + m)
                    else:
                        pe.wait_ge(down_added, KT * c + 1 + m)
                    product(m % 2, j % 2, g_hi, g_lo, FF_CHUNK_TILES * (m % 2), FF_CHUNK_TILES, g_lo_made,
                            FF_CHUNK_TILES * c).then_inc(down_done, 1)

        @block.gpsimd
        def _(pool):
            norm_pool(nc, pool, e, s, b, width, e.GAIN2, 3)

        @block.vector
        def _(dve):
            def split_rest(u, count):
                dve.wait_ge(w_hi_made, count)
                nc.vector.tensor_tensor(w_lo[:, u], stage[:, u], w_hi[:, u].bitcast(F32),
                                        ALU.subtract).then_inc(w_lo_made, 1)

            def add_gated(u, x_of, gate_of, added):
                for n, (side, a, z) in enumerate(sides):
                    op = nc.vector.scalar_tensor_tensor(x_of(a, z), ps[:, u, a:z], gate_of(side), x_of(a, z),
                                                        ALU.mult, ALU.add)
                op.then_inc(added, 1)

            nc.vector.tensor_copy(e.SCRAP[:, 1:2], e.UNIT[:, 0:1]).then_inc(down_added, 2)
            split_rest(0, 1)
            split_rest(1, 2)
            dve.wait_ge(x_loaded, 16 * KT)
            with dve.Fori(0, OUT_TILES // 2) as i:
                for u in range(2):
                    dve.wait_ge(out_done, 2 * i + u + 1)
                    add_gated(u, lambda a, z: e.X[:, bass.ds(u + 2 * i, 1), a:z].rearrange("p k t -> p (k t)"),
                              lambda side: e.MOD[:, bass.ds(2 * (2 * KT + u) + side + 4 * i, 1)], out_added)
                    split_rest(u, 2 * i + u + 3)
            dve.wait_ge(out_added, OUT_TILES + 2)
            norm_dve(nc, dve, e, s, b, width)

            def up(c, j):
                dve.wait_ge(g_hi_made, FF_CHUNK_TILES * c + j + 1)
                nc.vector.tensor_tensor(g_lo[:, j, 0:width], hidden[:, j % 2, 0:width],
                                        g_hi[:, j, 0:width].bitcast(F32), ALU.subtract).then_inc(g_lo_made, 1)
                split_rest(j % 2, up0 + j + 3 + FF_SLOTS * c)

            def down(c, j, more):
                for m in (2 * j, 2 * j + 1):
                    dve.wait_ge(down_done, KT * c + m + 1)
                    dve.wait_ge(down_added, KT * c + 2)
                    add_gated(m % 2, lambda a, z: e.X[:, m, a:z],
                              lambda side: e.MOD[:, 2 * (5 * KT + m) + side:2 * (5 * KT + m) + side + 1], down_added)
                if more:
                    split_rest(j % 2, down0 + j + 3 + FF_SLOTS * c)

            with dve.Fori(0, FF_CHUNKS - 1) as c:
                for j in range(FF_CHUNK_TILES):
                    up(c, j)
                for j in range(KT // 2):
                    down(c, j, True)
            for j in range(FF_CHUNK_TILES):
                up(FF_CHUNKS - 1, j)
            for j in range(KT // 2):
                down(FF_CHUNKS - 1, j, j < KT // 2 - 2)


def final_block(nc, e):
    with ExitStack() as ctx:
        sem = lambda n: e.semaphore((f"{n}_final"))
        sb = lambda n, s, d=F32: ctx.enter_context(nc.sbuf_tensor(f"{n}_final", s, d))
        squared, summed, total, rstd_step, scaled, stored = map(
            sem, ("squared", "summed", "total", "rstd_step", "scaled", "stored"))
        sq, acc, rstd = sb("sq", [P, 2, SEQ]), sb("acc", [P, SEQ]), sb("rstd", [P, SEQ])
        ps = ctx.enter_context(nc.psum_tensor("ps_final", [P, SEQ], F32))
        block = ctx.enter_context(nc.Block())

        @block.sync
        def _(sp):
            for k in range(KT):
                sp.wait_ge(scaled, k + 1)
                sp.dma_start(e.out_dram[k], e.X[:, k, 0:SEQ]).then_inc(stored, 16)
            sp.wait_ge(stored, 16 * KT)

        @block.scalar
        def _(act):
            for k in range(KT):
                if k >= 2:
                    act.wait_ge(summed, k - 1)
                nc.scalar.activation(sq[:, k % 2], e.X[:, k, 0:SEQ], ACT.Square).then_inc(squared, 1)
            act.wait_ge(total, 1)
            nc.scalar.activation(rstd[:], ps[:], ACT.Ln, scale=1.0 / D_MODEL, bias=e.EPS[:]).then_inc(rstd_step, 1)
            act.wait_ge(rstd_step, 1)
            nc.scalar.activation(rstd[:], rstd[:], ACT.Exp, scale=-0.5).then_inc(rstd_step, 1)

        @block.tensor
        def _(pe):
            pe.wait_ge(summed, KT)
            for a, z in blocks(SEQ):
                last = nc.tensor.matmul(ps[:, a:z], e.ONES[:], acc[:, a:z], start=True, stop=True)
            last.then_inc(total, 1)

        @block.vector
        def _(dve):
            for k in range(KT):
                dve.wait_ge(squared, k + 1)
                if k == 0:
                    nc.vector.tensor_copy(acc[:], sq[:, 0]).then_inc(summed, 1)
                else:
                    dve.wait_ge(summed, k)
                    nc.vector.tensor_tensor(acc[:], acc[:], sq[:, k % 2], ALU.add).then_inc(summed, 1)
            dve.wait_ge(rstd_step, 2)
            for k in range(KT):
                nc.vector.scalar_tensor_tensor(e.X[:, k, 0:SEQ], e.X[:, k, 0:SEQ], sv(e, "final", k), rstd[:],
                                               ALU.mult, ALU.mult).then_inc(scaled, 1)


def build_program(nc, x_dram, cond_dram, id1_dram, sv_dram, w_dram, rope_dram, rt_dram, out_dram, layers=DEPTH):
    with ExitStack() as ctx:
        sb = lambda n, s, d=F32: ctx.enter_context(nc.sbuf_tensor(n, s, d))
        e = Shared()
        e.x_dram, e.cond_dram, e.id1_dram, e.sv_dram = x_dram, cond_dram, id1_dram, sv_dram
        e.w_dram, e.rope_dram, e.rt_dram, e.out_dram = w_dram, rope_dram, rt_dram, out_dram
        e.scratch = [nc.dram_tensor(f"projected{i}", (IN_TILES, P, T), F32).ap() for i in range(layers)]
        e.H_HI, e.H_LO = sb("h_hi", [P, KT, T], R32), sb("h_lo", [P, KT, T], R32)
        e.x_kept = nc.dram_tensor("x_kept", (KT, P, T), F32).ap()
        e.ID1, e.ONES, e.SV = sb("identity", [P, P]), sb("ones", [P, P]), sb("vectors", [P, SV_LEN])
        e.COND, e.MOD = sb("cond", [P, KT, 2]), sb("mod", [P, 2 * ADA_TILES])
        e.GAIN1, e.GAIN2 = sb("gain1", [P, KT, 2]), sb("gain2", [P, KT, 2])
        e.EPS, e.UNIT, e.SCRAP, e.POOL_SCRAP = sb("eps", [P, 1]), sb("unit", [P, 2]), sb("scrap", [P, 2]), sb("pool_scrap", [P, 2])
        e.LGA, e.LGP, e.CHUNK_DECAY = sb("lga", [P, 8]), sb("lgp", [P, 4]), sb("chunk_decay", [P, 4])
        e.K_DECAY, e.NEG_LAM, e.DGN = sb("k_decay", [P, 2, HEADS]), sb("neg_lam", [P, 1]), sb("dgn", [P, HEADS])
        e.IDENT = e.ID1[:]
        x_place = ExitStack()

        def place_x(n):
            e.X = x_place.enter_context(nc.sbuf_tensor(f"x{n}", [P, KT, T], F32))

        for layer in range(layers):
            last = layer == DEPTH - 1
            layer_semaphores = ExitStack()
            e.semaphore = lambda name: e.held.append(layer_semaphores.enter_context(nc.semaphore(name))) or e.held[-1]
            e.held = []
            if layer == 0:
                place_x(0)
            modulation_block(nc, e, layer)
            projection_block(nc, e, layer)
            x_place.close()
            with (nc.sbuf_tensor(f"rt{layer}", [P, RT_LEN], F32) as e.RT,
                  nc.sbuf_tensor(f"intra{layer}", [P, HEADS, P], F32) as e.INTRA,
                  nc.sbuf_tensor(f"q_decay{layer}", [P, 4, P], F32) as e.Q_DECAY):
                conv_norm_block(nc, e, layer)
                retention_block(nc, e, layer)
            attention_block(nc, e, layer, last)
            place_x(layer + 1)
            mlp_block(nc, e, layer, last)
            with nc.Block() as block:
                @block.sync
                def _(sp):
                    for s in e.held:
                        sp.sem_clear(s)
            layer_semaphores.close()
        e.semaphore = lambda name: ctx.enter_context(nc.semaphore(name))
        final_block(nc, e)
        x_place.close()


def rope_tables():
    f = np.float32
    half = DK // 2
    inv = f(ROPE_BASE) ** (-np.arange(0, DK, 2, dtype=f) / f(DK))
    inv_ax = f(ROPE_BASE) ** (-np.arange(0, half, 2, dtype=f) / f(half))
    pos = np.arange(SEQ)
    ret, ax = pos[:, None].astype(f) * inv[None, :], None
    rows, cols = (pos // GRID_W)[:, None].astype(f) * inv_ax, (pos % GRID_W)[:, None].astype(f) * inv_ax
    p = np.arange(P) % DK
    sign = np.where(p % 32 < 16, -1.0, 1.0).astype(f)[:, None]
    plain = ret[:, 16 * (p // 32) + p % 16].T
    axial = np.where(p[:, None] < 32, rows[:, p % 16].T, cols[:, p % 16].T)
    out = np.zeros((2, P, 2, T), f)
    out[:, :, 0] = 1.0
    for i, ang in enumerate((plain, axial)):
        out[i, :, 0, :SEQ] = np.cos(ang.astype(f))
        out[i, :, 1, :SEQ] = np.sin(ang.astype(f)) * sign
    return out


def retention_tables():
    f = np.float32
    s, c = np.arange(P)[:, None], np.arange(P)[None, :]
    one = np.ones((P, P))
    head = (s // DK == c // DK)
    tables = [np.maximum(c - s, 0), c >= s, np.maximum(s - c, 0), s >= c, (c + 1) * one, (P - c) * one, head, head / DK,
              P - 1 - s, s]
    return np.concatenate([t.astype(f) for t in tables], axis=1)


def columns(v):
    return v.reshape(-1, P).T


def kernel(**inputs):
    import concourse.bacc as bacc
    from concourse.bass_utils import run_bass_kernel_spmd

    a = {k: np.ascontiguousarray(v) for k, v in inputs.items()}
    x_t = np.concatenate([a["x"][0].T, a["ctx"][0].T], axis=1).reshape(KT, P, T)
    cond = np.stack([a["c"][0].reshape(KT, P).T, a["c_ctx"].reshape(KT, P).T], axis=-1)

    pair = np.arange(DK).reshape(2, 2, 16).transpose(1, 0, 2).reshape(-1)
    heads = (np.arange(HEADS)[:, None] * DK + pair).reshape(-1)
    width = HEADS * DK
    start = dict(rq=0, rk=width, rv=2 * width, rg=3 * width, dq=4 * width, dk=6 * width, dv=8 * width,
                 cv=10 * width, cg=11 * width)
    plain = np.arange(width)
    wide = np.arange(2 * width)
    order = np.concatenate([start["cv"] + plain, start["cg"] + plain, start["rq"] + heads, start["rk"] + heads,
                            start["rv"] + plain, start["rg"] + plain, start["dq"] + wide, start["dk"] + wide,
                            start["dv"] + wide])

    def slots(w):
        k, m = w.shape
        return w.reshape(k // P, P, m // P, P).transpose(2, 1, 0, 3).reshape(m // P, P, k)

    weights, vectors = [], []
    for i in range(DEPTH):
        parts = [slots(a["ada_w"][i]), slots(a["w_in"][i][:, order]), slots(a["w_out"][i])]
        up, rows = slots(a["mlp_w1"][i]), FF_CHUNK_TILES * P
        for c in range(FF_CHUNKS):
            parts.append(up[FF_CHUNK_TILES * c:FF_CHUNK_TILES * (c + 1)])
            down = slots(a["mlp_w2"][i][rows * c:rows * (c + 1)])
            parts.append(down.reshape(KT // 2, 2, P, rows).transpose(0, 2, 1, 3).reshape(KT // 2, P, SLOT))
        weights.append(np.concatenate(parts))
        decay = a["ret_log_decay"][i]
        vectors.append(np.concatenate([
            columns(a["norm1_w"][i]), columns(a["norm2_w"][i]), columns(a["ada_b"][i]), columns(a["ret_gn_w"][i]),
            columns(a["diff_gn_w"][i]),
            a["conv_w"][i].reshape(TAPS, CONV_TILES, P).transpose(2, 1, 0).reshape(P, CONV_TILES * TAPS),
            columns(a["conv_b"][i]), columns(a["conv_ln_w"][i]), columns(a["conv_ln_b"][i]),
            np.tile(decay.reshape(1, -1), (P, 1)),
            np.repeat(decay.reshape(2, 2, 2), DK, axis=2).reshape(4, P).T,
            np.tile(a["diff_lam"][i].reshape(1, -1), (P, 1)),
            columns(a["final_norm_w"])], axis=1))

    arrays = {"x_t": x_t, "cond_in": cond, "identity_in": np.eye(P, dtype=np.float32), "vectors_in": np.stack(vectors),
              "weights": np.stack(weights), "rope": rope_tables(), "retention": retention_tables()}
    arrays = {k: np.ascontiguousarray(v) for k, v in arrays.items()}
    nc = bacc.Bacc("TRN2", target_bir_lowering=False, num_devices=1)
    args = [nc.dram_tensor(k, v.shape, F32, kind="ExternalInput").ap() for k, v in arrays.items()]
    out = nc.dram_tensor("out_t", (KT, P, SEQ), F32, kind="ExternalOutput").ap()
    build_program(nc, *args, out)
    got = run_bass_kernel_spmd(nc, [arrays], core_ids=[0]).results[0]["out_t"]
    return np.ascontiguousarray(got.reshape(D_MODEL, SEQ).T)[None]
```

```python
import math
from contextlib import ExitStack


import numpy as np

import concourse.bass as bass
from concourse import mybir

class NormSemaphores:

    def __init__(self, sem, name):
        self.squared, self.summed, self.total = sem(f"{name}_squared"), sem(f"{name}_summed"), sem(f"{name}_total")
        self.psum_free, self.rstd = sem(f"{name}_psum_free"), sem(f"{name}_rstd")
        self.normed, self.shifted = sem(f"{name}_normed"), sem(f"{name}_shifted")
        self.hi, self.lo = sem(f"{name}_hi"), sem(f"{name}_lo")


class NormBuffers:
    def __init__(self, sq, acc, rstd, tmp, ps):
        self.sq, self.acc, self.rstd, self.tmp, self.ps = sq, acc, rstd, tmp, ps


class Shared:
    pass


F32 = mybir.dt.float32
R32 = mybir.dt.float32r
ACT = mybir.ActivationFunctionType
ALU = mybir.AluOpType
AX = mybir.AxisListType.X

P = 128
D_MODEL, SEQ, CTX, DEPTH = 1024, 1024, 256, 2
T = SEQ + CTX
KT = D_MODEL // P
N_MOD = 6
D_FF = 4 * D_MODEL
EPS = 1e-6
GRID_W = 64
ROPE_BASE = 10000.0
DK = 64
HEADS = 4
TAPS = 31
PAD = (TAPS - 1) // 2
CONV_TILES = 2
NCH = T // P
NCH_X = SEQ // P
SLOT = KT * P
K_SCALE = DK ** -0.5

ADA_TILES = N_MOD * KT
IN_TILES = 24
OUT_TILES = KT
FF_CHUNK_TILES = 4
FF_CHUNKS = D_FF // (FF_CHUNK_TILES * P)
IN0 = 0
OUT0 = IN0 + IN_TILES
FF0 = OUT0 + OUT_TILES
FF_SLOTS = FF_CHUNK_TILES + KT // 2
LAYER_SLOTS = FF0 + FF_CHUNKS * FF_SLOTS

CV, CG, RQ, RK, RV, RG, DQ, DKK, DV = 0, 2, 4, 6, 8, 10, 12, 16, 20
STORED0 = RQ

U_X0 = PAD
U_C0 = PAD + SEQ + PAD
U_LEN = U_C0 + CTX + PAD
Y_C0 = SEQ + PAD
Y_LEN = Y_C0 + CTX

SV_COLS = {}
_at = 0
for _name, _n in (("rgn", 2), ("dgn", 4), ("cw", CONV_TILES * TAPS),
                  ("cb", 2), ("clw", 2), ("clb", 2), ("lga", 8), ("lgp", 4), ("dlam", 4 * DK), ("final", KT)):
    SV_COLS[_name] = (_at, _at + _n)
    _at += _n
SV_LEN = _at
N1W, N2W, ADAB = 0, KT, 2 * KT
MV_LEN = 2 * KT + ADA_TILES
FIRST_TILES = 3 * KT
GROUP = 6
GROUP_COLS = GROUP * P
OWN_GROUPS, NEXT_GROUPS = (ADA_TILES - FIRST_TILES) // GROUP, ADA_TILES // GROUP

RT_RELF, RT_MASKF, RT_RELB, RT_MASKB, RT_QF, RT_QB, RT_BLK, RT_BLK64 = range(8)
RT_LEN = 8 * P + 2


def blocks(width):
    return [(a, min(a + 512, width)) for a in range(0, width, 512)]


def mm3(nc, out, w_hi, w_lo, x_hi, x_lo, start, stop):
    nc.tensor.matmul(out, w_hi, x_hi, start=start, stop=False)
    nc.tensor.matmul(out, w_hi, x_lo, start=False, stop=False)
    return nc.tensor.matmul(out, w_lo, x_hi, start=False, stop=stop)


def sv(e, name, a=0, n=1):
    lo, _ = SV_COLS[name]
    return e.SV[:, lo + a:lo + a + n]


def mod_tile(nc, ps, w, at, cond):
    for k in range(KT):
        last = nc.tensor.matmul(ps[:, bass.ds(2 * at, 2)], w[:, k * P:(k + 1) * P], cond[:, k], start=k == 0,
                                stop=k == KT - 1)
    return last


def add_bias(nc, e, layer, ps, first, n):
    bias = (e.MV[:, bass.ds(layer * MV_LEN + ADAB + first, n)].rearrange("p (k a) -> p k a", a=1)
            .to_broadcast([P, n, 2]))
    return nc.vector.tensor_tensor(e.MOD[:, bass.ds(2 * (ADA_TILES * layer + first), 2 * n)].rearrange("p (k a) -> p k a", a=2),
                                   ps[:, 0:2 * n].rearrange("p (k a) -> p k a", a=2), bias, ALU.add)


def make_gain(nc, e, layer, gain, w, scale):
    w_ap = e.MV[:, MV_LEN * layer + w:MV_LEN * layer + w + KT].rearrange("p (k a) -> p k a", a=1).to_broadcast([P, KT, 2])
    lo = 2 * (ADA_TILES * layer + KT * scale)
    return nc.vector.scalar_tensor_tensor(gain[:], e.MOD[:, lo:lo + 2 * KT].rearrange("p (k a) -> p k a", a=2), 1.0,
                                          w_ap, ALU.add, ALU.mult)


def modulation_block(nc, e):
    with ExitStack() as ctx:
        sem = lambda n: e.semaphore((f"{n}_m"))
        vectors_loaded, inputs_loaded, x_loaded = sem("vectors_loaded"), sem("inputs_loaded"), sem("x_loaded")
        slot_loaded = [sem(f"slot_loaded{n}") for n in range(2 * KT)]
        cond_ready, group_done, biased, gain_made = map(sem, ("cond_ready", "group_done", "biased", "gain_made"))
        stage = ctx.enter_context(nc.sbuf_tensor("ada_stage", [P, 2 * KT, SLOT], F32))
        ps = ctx.enter_context(nc.psum_tensor("ada_ps", [P, 3, 512], F32))
        block = ctx.enter_context(nc.Block())

        @block.sync
        def _(sp):
            sp.dma_start(e.COND[:], e.cond_dram).then_inc(inputs_loaded, 16)
            sp.dma_start(e.ID1[:], e.id1_dram).then_inc(inputs_loaded, 16)
            sp.dma_start(e.MV[:], e.mv_dram).then_inc(vectors_loaded, 16)
            for n in range(2 * KT):
                sp.dma_start(stage[:, n], e.ada_dram[n]).then_inc(slot_loaded[n], 16)
            for k in range(KT):
                sp.dma_start(e.X[:, k], e.x_dram[k]).then_inc(x_loaded, 16)
            for n in range(KT):
                sp.wait_ge(group_done, 1)
                sp.dma_start(stage[:, n], e.ada_dram[2 * KT + n]).then_inc(slot_loaded[n], 16)
            sp.wait_ge(x_loaded, 16 * KT)

        @block.scalar
        def _(act):
            act.wait_ge(inputs_loaded, 32)
            nc.scalar.activation(e.COND[:], e.COND[:], ACT.Silu).then_inc(cond_ready, 1)

        @block.tensor
        def _(pe):
            pe.wait_ge(cond_ready, 1)
            for g in range(3):
                for k in range(KT):
                    place = KT * (g % 2) + k
                    pe.wait_ge(slot_loaded[place], 16 * (g // 2 + 1))
                    last = mod_tile(nc, ps[:, g], stage[:, place], k, e.COND)
                last.then_inc(group_done, 1)

        @block.vector
        def _(dve):
            nc.vector.memset(e.EPS[:], EPS)
            nc.vector.memset(e.ONES[:], 1.0)
            nc.vector.memset(e.UNIT[:], 1.0)
            dve.wait_ge(vectors_loaded, 16)
            for g in range(3):
                dve.wait_ge(group_done, g + 1)
                add_bias(nc, e, 0, ps[:, g], KT * g, KT).then_inc(biased, 1)
            dve.wait_ge(biased, 3)
            make_gain(nc, e, 0, e.GAIN1, N1W, 1).then_inc(gain_made, 1)


def norm_act(nc, act, e, s, b, width):
    for k in range(KT):
        if k >= 2:
            act.wait_ge(s.summed, k - 1)
        nc.scalar.activation(b.sq[:, k % 2, 0:width], e.X[:, k, 0:width], ACT.Square).then_inc(s.squared, 1)
    act.wait_ge(s.total, 1)
    nc.scalar.activation(b.rstd[:, 0:width], b.ps[:, 0, 0:width], ACT.Ln, scale=1.0 / D_MODEL,
                         bias=e.EPS[:]).then_inc(s.psum_free, 2)
    act.wait_ge(s.psum_free, 2)
    nc.scalar.activation(b.rstd[:, 0:width], b.rstd[:, 0:width], ACT.Exp, scale=-0.5).then_inc(s.rstd, 1)
    per = 2 if width > SEQ else 1
    for k in range(KT):
        act.wait_ge(s.shifted, per * (k + 1))
        nc.scalar.activation(e.H_HI[:, k, 0:width], b.tmp[:, k % 3, 0:width], ACT.Copy).then_inc(s.hi, 1)


def norm_pe(nc, pe, e, s, b, width):
    pe.wait_ge(s.summed, KT)
    for a, z in blocks(width):
        last = nc.tensor.matmul(b.ps[:, 0, a:z], e.ONES[:], b.acc[:, a:z], start=True, stop=True)
    last.then_inc(s.total, 1)


def norm_dve(nc, dve, e, s, b, width):
    for k in range(KT):
        dve.wait_ge(s.squared, k + 1)
        if k == 0:
            nc.vector.tensor_copy(b.acc[:, 0:width], b.sq[:, 0, 0:width]).then_inc(s.summed, 1)
        else:
            dve.wait_ge(s.summed, k)
            nc.vector.tensor_tensor(b.acc[:, 0:width], b.acc[:, 0:width], b.sq[:, k % 2, 0:width],
                                    ALU.add).then_inc(s.summed, 1)
    dve.wait_ge(s.rstd, 1)
    for k in range(KT + 2):
        if k < KT:
            if k >= 3:
                dve.wait_ge(s.lo, k - 2)
            nc.vector.tensor_tensor(b.tmp[:, k % 3, 0:width], e.X[:, k, 0:width], b.rstd[:, 0:width],
                                    ALU.mult).then_inc(s.normed, 1)
        if k >= 2:
            j = k - 2
            dve.wait_ge(s.hi, j + 1)
            nc.vector.tensor_tensor(e.H_LO[:, j, 0:width], b.tmp[:, j % 3, 0:width],
                                    e.H_HI[:, j, 0:width].bitcast(F32), ALU.subtract).then_inc(s.lo, 1)


def norm_pool(nc, pool, e, s, b, width, layer, gain, shift):
    for k in range(KT):
        pool.wait_ge(s.normed, k + 1)
        for j, (a, z) in enumerate(((0, SEQ), (SEQ, width))):
            if z > a:
                sh = 2 * (ADA_TILES * layer + KT * shift + k) + j
                nc.gpsimd.tensor_scalar(b.tmp[:, k % 3, a:z], b.tmp[:, k % 3, a:z], gain[:, k, j:j + 1],
                                        e.MOD[:, sh:sh + 1], ALU.mult, ALU.add).then_inc(s.shifted, 1)


def projection_block(nc, e, layer):
    with ExitStack() as ctx:
        sem = lambda n: e.semaphore((f"{n}_p{layer}"))
        sb = lambda n, s, d=F32: ctx.enter_context(nc.sbuf_tensor(f"{n}_p{layer}", s, d))
        s = NormSemaphores(sem, "n1")
        slot_loaded = [sem("slot_loaded0"), sem("slot_loaded1")]
        w_hi_made, w_lo_made, tile_done = sem("w_hi_made"), sem("w_lo_made"), sem("tile_done")
        evacuated = s.psum_free
        vectors_loaded = sem("vectors_loaded")
        table_loaded, rope_step, cos_made = sem("table_loaded"), sem("rope_step"), sem("cos_made")
        stored = [sem("stored0"), sem("stored1")]
        margins_zeroed, gated, conv_step, conv_stored, x_stored = map(
            sem, ("margins_zeroed", "gated", "conv_step", "conv_stored", "x_stored"))

        stage, w_hi, w_lo = sb("stage", [P, 2, SLOT]), sb("w_hi", [P, 2, SLOT], R32), sb("w_lo", [P, 2, SLOT], R32)
        raw, rot, cosx, table = sb("raw", [P, 2, T]), sb("rot", [P, T]), sb("cosx", [P, T]), sb("table", [P, 2, T])
        with nc.sbuf_tensor(f"tmp_p{layer}", [P, 3, T], F32) as tmp:
            pass
        u_buf, y_buf = sb("u_buf", [P, CONV_TILES, U_LEN]), sb("y_buf", [P, CONV_TILES, Y_LEN])
        ps = ctx.enter_context(nc.psum_tensor(f"ps_p{layer}", [P, 2, 3 * 512], F32))
        b = NormBuffers(sq=raw, acc=rot, rstd=cosx, tmp=tmp, ps=ps)
        block = ctx.enter_context(nc.Block())
        scratch = e.scratch[layer]

        out_of_psum = lambda n: n + 3

        @block.sync
        def _(sp):
            for u in range(2):
                sp.dma_start(stage[:, u], e.w_dram[layer, IN0 + u]).then_inc(slot_loaded[u], 16)
            sp.dma_start(e.SV[:], e.sv_dram[layer]).then_inc(vectors_loaded, 16)
            sp.dma_start(table[:], e.rope_dram[0]).then_inc(table_loaded, 16)
            if layer > 0:
                for k in range(KT):
                    sp.dma_start(e.x_kept[k], e.X[:, k]).then_inc(x_stored, 16)

            def load(n, u):
                sp.wait_ge(w_lo_made, n + 1)
                sp.dma_start(stage[:, u], e.w_dram[layer, bass.ds(IN0 + 2 + n, 1)].rearrange(
                    "a p c -> p (a c)")).then_inc(slot_loaded[u], 16)

            def store(n, u):
                sp.dma_start(scratch[bass.ds(n, 1)].rearrange("a p c -> p (a c)"), raw[:, u]).then_inc(stored[u], 16)

            def store_conv(t):
                for (a, z), y in (((0, SEQ), 0), ((SEQ, T), Y_C0)):
                    sp.dma_start(scratch[t][:, a:z], y_buf[:, t, y:y + z - a]).then_inc(conv_stored, 16)

            for n in range(RQ):
                load(n, n % 2)
            for n in range(RQ, RV):
                load(n, n % 2)
                sp.wait_ge(rope_step, 3 * (n - RQ) + 3)
                store(n, n % 2)
            sp.dma_start(table[:], e.rope_dram[1]).then_inc(table_loaded, 16)
            for n in range(RV, DQ):
                load(n, n % 2)
                sp.wait_ge(evacuated, out_of_psum(n))
                store(n, n % 2)
            sp.wait_ge(conv_step, TAPS)
            store_conv(0)
            with sp.Fori(0, (DV - DQ) // 2) as i:
                for u in range(2):
                    load(DQ + u + 2 * i, u)
                    sp.wait_ge(rope_step, 3 * (RV - RQ) + 3 * u + 3 + 6 * i)
                    store(DQ + u + 2 * i, u)
            for n in range(DV, IN_TILES):
                if n < IN_TILES - 2:
                    load(n, n % 2)
                sp.wait_ge(evacuated, out_of_psum(n))
                store(n, n % 2)
            sp.wait_ge(conv_step, 2 * TAPS)
            store_conv(1)
            for u in range(2):
                sp.wait_ge(stored[u], 16 * (IN_TILES - STORED0) // 2)
            sp.wait_ge(conv_stored, 16 * 4)
            if layer > 0:
                sp.wait_ge(x_stored, 16 * KT)

        @block.scalar
        def _(act):
            def split(n, u):
                nc.scalar.activation(w_hi[:, u], stage[:, u], ACT.Copy).then_inc(w_hi_made, 1)

            for u in range(2):
                act.wait_ge(slot_loaded[u], 16)
                split(u, u)
            norm_act(nc, act, e, s, b, T)

            def tile(n, u, func, loads=True, load_count=None):
                act.wait_ge(tile_done, n + 1)
                nc.scalar.activation(raw[:, u], ps[:, u, 0:T], func).then_inc(evacuated, 1)
                if loads:
                    act.wait_ge(slot_loaded[u], load_count)
                    split(n + 2, u)

            loads_of = lambda n: 16 * (n // 2 + 2)
            act.wait_ge(margins_zeroed, 2)
            for n in range(CV, CG):
                act.wait_ge(tile_done, n + 1)
                nc.scalar.activation(u_buf[:, n - CV, U_X0:U_X0 + SEQ], ps[:, n % 2, 0:SEQ], ACT.Copy)
                nc.scalar.activation(u_buf[:, n - CV, U_C0:U_C0 + CTX], ps[:, n % 2, SEQ:T], ACT.Copy).then_inc(evacuated, 1)
                act.wait_ge(slot_loaded[n % 2], loads_of(n))
                split(n + 2, n % 2)
            for n in range(CG, RQ):
                tile(n, n % 2, ACT.Sigmoid, True, loads_of(n))
            for n in range(RQ, DQ):
                if n < RQ + 2:
                    act.wait_ge(gated, n - RQ + 1)
                else:
                    act.wait_ge(stored[n % 2], 16 * ((n - STORED0) // 2))
                tile(n, n % 2, ACT.Silu if n >= RG else ACT.Copy, True, loads_of(n))
            with act.Fori(0, (DV - DQ) // 2) as i:
                for u in range(2):
                    act.wait_ge(stored[u], 16 * ((DQ - STORED0) // 2) + 16 * i)
                    tile(DQ + u + 2 * i, u, ACT.Copy, True, loads_of(DQ) + 16 * i)
            for n in range(DV, IN_TILES):
                act.wait_ge(stored[n % 2], 16 * ((n - STORED0) // 2))
                tile(n, n % 2, ACT.Copy, n < IN_TILES - 2, loads_of(n))

        @block.tensor
        def _(pe):
            norm_pe(nc, pe, e, s, b, T)
            with pe.Fori(0, IN_TILES // 2) as i:
                for u in range(2):
                    pe.wait_ge(w_lo_made, 2 * i + u + 1)
                    pe.wait_ge(evacuated, 2 * i + u + 1)
                    for k in range(KT):
                        pe.wait_ge(s.lo, k + 1)
                        kk = slice(k * P, (k + 1) * P)
                        for a, z in blocks(T):
                            last = mm3(nc, ps[:, u, a:z], w_hi[:, u, kk], w_lo[:, u, kk], e.H_HI[:, k, a:z],
                                       e.H_LO[:, k, a:z], k == 0, k == KT - 1)
                    last.then_inc(tile_done, 1)

        @block.gpsimd
        def _(pool):
            norm_pool(nc, pool, e, s, b, T, layer, e.GAIN1, 0)

            def rope_cos(n, r, u):
                pool.wait_ge(evacuated, out_of_psum(n))
                nc.gpsimd.tensor_tensor(cosx[:], raw[:, u], table[:, 0], ALU.mult).then_inc(cos_made, 1)

            pool.wait_ge(table_loaded, 16)
            for n in range(RQ, RV):
                if n > RQ:
                    pool.wait_ge(rope_step, 3 * (n - RQ))
                rope_cos(n, n - RQ, n % 2)
            pool.wait_ge(table_loaded, 32)
            with pool.Fori(0, (DV - DQ) // 2) as i:
                for u in range(2):
                    pool.wait_ge(rope_step, 3 * (RV - RQ) + 3 * u + 6 * i)
                    rope_cos(DQ + u + 2 * i, 0, u)

        @block.vector
        def _(dve):
            def split_rest(n, u):
                dve.wait_ge(w_hi_made, n + 1)
                nc.vector.tensor_tensor(w_lo[:, u], stage[:, u], w_hi[:, u].bitcast(F32),
                                        ALU.subtract).then_inc(w_lo_made, 1)

            split_rest(0, 0)
            split_rest(1, 1)
            norm_dve(nc, dve, e, s, b, T)
            dve.wait_ge(s.lo, KT)
            nc.vector.memset(u_buf[:, :, 0:PAD], 0.0)
            nc.vector.memset(u_buf[:, :, U_X0 + SEQ:U_C0], 0.0).then_inc(margins_zeroed, 1)
            nc.vector.memset(u_buf[:, :, U_C0 + CTX:U_LEN], 0.0).then_inc(margins_zeroed, 1)

            swap = [(p + 16) % 32 for p in range(32)]

            def rope(n, r3, u, cos_count, tables):
                dve.wait_ge(table_loaded, tables)
                dve.wait_ge(evacuated, out_of_psum(n))
                nc.vector.tensor_copy(e.SCRAP[:, 1:2], e.UNIT[:, 0:1])
                nc.vector.stream_shuffle(rot[:], raw[:, u], swap).then_inc(rope_step, 1)
                dve.wait_ge(rope_step, r3 + 1)
                nc.vector.tensor_tensor(rot[:], rot[:], table[:, 1], ALU.mult).then_inc(rope_step, 1)
                dve.wait_ge(cos_made, cos_count)
                dve.wait_ge(rope_step, r3 + 2)
                nc.vector.tensor_tensor(raw[:, u], rot[:], cosx[:], ALU.add).then_inc(rope_step, 1)

            w0, b0 = SV_COLS["cw"][0], SV_COLS["cb"][0]

            def tap(t, j, weight, count):
                dve.wait_ge(conv_step, count)
                nc.vector.scalar_tensor_tensor(y_buf[:, t], u_buf[:, t, bass.ds(j, Y_LEN)], e.SV[:, bass.ds(weight, 1)],
                                               y_buf[:, t], ALU.mult, ALU.add).then_inc(conv_step, 1)

            def first_tap(t):
                nc.vector.tensor_scalar(y_buf[:, t], u_buf[:, t, 0:Y_LEN], e.SV[:, w0 + t * TAPS:w0 + t * TAPS + 1],
                                        e.SV[:, b0 + t:b0 + t + 1], ALU.mult, ALU.add).then_inc(conv_step, 1)

            for n in range(CV, CG):
                split_rest(n + 2, n % 2)
            for n in range(CG, RQ):
                t = n - CG
                dve.wait_ge(evacuated, out_of_psum(n))
                for c0, a, z in ((U_X0, 0, SEQ), (U_C0, SEQ, T)):
                    g = nc.vector.tensor_tensor(u_buf[:, t, c0:c0 + z - a], u_buf[:, t, c0:c0 + z - a],
                                                raw[:, n % 2, a:z], ALU.mult)
                g.then_inc(gated, 1)
                split_rest(n + 2, n % 2)
            dve.wait_ge(gated, 2)
            dve.wait_ge(vectors_loaded, 16)
            taps_done = 0
            for n in range(RQ, DQ):
                if n < RV:
                    rope(n, 3 * (n - RQ), n % 2, n - RQ + 1, 16)
                split_rest(n + 2, n % 2)
                for _ in range(4):
                    if taps_done == 0:
                        first_tap(0)
                        taps_done = 1
                    elif taps_done < TAPS:
                        tap(0, taps_done, w0 + taps_done, taps_done)
                        taps_done += 1
            first_tap(1)
            with dve.Fori(0, (DV - DQ) // 2) as i:
                for u in range(2):
                    rope(DQ + u + 2 * i, 3 * (RV - RQ) + 3 * u + 6 * i, u, RV - RQ + 1 + u + 2 * i, 32)
                    split_rest(DQ + 2 + u + 2 * i, u)
                    for j in range(3):
                        q = 3 * u + j + 1
                        tap(1, 6 * i + q, w0 + TAPS + q + 6 * i, TAPS + q + 6 * i)
            for n in range(DV, IN_TILES):
                if n < IN_TILES - 2:
                    split_rest(n + 2, n % 2)
                for _ in range(2):
                    j = 1 + 3 * (DV - DQ) + 2 * (n - DV) + _
                    if j < TAPS:
                        tap(1, j, w0 + TAPS + j, TAPS + j)


def conv_norm_block(nc, e, layer):
    lam_init = 0.8 - 0.6 * math.exp(-0.3 * layer)
    with ExitStack() as ctx:
        sem = lambda n: e.semaphore((f"{n}_c{layer}"))
        sb = lambda n, s, d=F32: ctx.enter_context(nc.sbuf_tensor(f"{n}_c{layer}", s, d))
        loaded, tables_loaded, summed, centered, squared, varied, rstd_step, scaled, silu_step, hi_made, done = map(
            sem, ("loaded", "tables_loaded", "summed", "centered", "squared", "varied", "rstd_step", "scaled",
                  "silu_step", "hi_made", "done"))
        pa, pv = sem("prep_act"), sem("prep_dve")
        y, sq, rstd = sb("y", [P, 2, T]), sb("sq", [P, 2, T]), sb("rstd", [P, T])
        ef, eb = sb("ef", [P, HEADS, P]), sb("eb", [P, HEADS, P])
        lam_prod, lam_sum = sb("lam_prod", [P, 2, DK]), sb("lam_sum", [P, 4])
        ps = ctx.enter_context(nc.psum_tensor(f"ps_c{layer}", [P, 2, 3 * 512], F32))
        block = ctx.enter_context(nc.Block())
        rt = lambda i: e.RT[:, i * P:(i + 1) * P]

        @block.sync
        def _(sp):
            sp.dma_start(e.RT[:], e.rt_dram).then_inc(tables_loaded, 16)
            for t in range(CONV_TILES):
                sp.dma_start(y[:, t], e.scratch[layer][t]).then_inc(loaded, 16)

        @block.tensor
        def _(pe):
            pe.wait_ge(loaded, 32)
            for a, z in blocks(T):
                for t in range(CONV_TILES):
                    last = nc.tensor.matmul(ps[:, 0, a:z], e.ONES[:], y[:, t, a:z], start=t == 0, stop=t == 1)
            last.then_inc(summed, 1)
            pe.wait_ge(squared, 2)
            for a, z in blocks(T):
                for t in range(CONV_TILES):
                    last = nc.tensor.matmul(ps[:, 1, a:z], e.ONES[:], sq[:, t, a:z], start=t == 0, stop=t == 1)
            last.then_inc(varied, 1)

        @block.scalar
        def _(act):
            act.wait_ge(tables_loaded, 16)
            nc.scalar.activation(e.LGA[:], sv(e, "lga", 0, 8), ACT.Exp).then_inc(pa, 1)
            nc.scalar.activation(e.LGP[:], sv(e, "lgp", 0, 4), ACT.Exp).then_inc(pa, 1)
            act.wait_ge(pa, 2)
            nc.scalar.activation(e.LGA[:], e.LGA[:], ACT.Copy, scale=-1.0).then_inc(pa, 1)
            nc.scalar.activation(e.LGP[:], e.LGP[:], ACT.Copy, scale=-1.0).then_inc(pa, 1)
            act.wait_ge(pa, 4)
            nc.scalar.activation(e.CHUNK_DECAY[:], e.LGP[:], ACT.Exp, scale=float(P)).then_inc(pa, 1)
            for d in range(2):
                for p in range(2):
                    nc.scalar.activation(e.Q_DECAY[:, 2 * d + p], rt(RT_QF + d), ACT.Exp,
                                         scale=e.LGP[:, 2 * d + p:2 * d + p + 1]).then_inc(pa, 1)
                nc.scalar.activation(e.K_DECAY[:, d], e.LGA[:, 4 * d:4 * d + 4], ACT.Exp,
                                     scale=e.RT[:, 8 * P + d:8 * P + d + 1]).then_inc(pa, 1)
            act.wait_ge(pa, 11)
            nc.scalar.activation(e.K_DECAY[:], e.K_DECAY[:], ACT.Copy, scale=K_SCALE).then_inc(pa, 1)
            for h in range(HEADS):
                nc.scalar.activation(ef[:, h], rt(RT_RELF), ACT.Exp, scale=e.LGA[:, h:h + 1]).then_inc(pa, 1)
                nc.scalar.activation(eb[:, h], rt(RT_RELB), ACT.Exp, scale=e.LGA[:, 4 + h:5 + h]).then_inc(pa, 1)
            act.wait_ge(pv, 4)
            nc.scalar.activation(lam_sum[:, 2:4], lam_sum[:, 0:2], ACT.Exp).then_inc(pa, 1)
            for t in range(CONV_TILES):
                act.wait_ge(centered, t + 1)
                nc.scalar.activation(sq[:, t], y[:, t], ACT.Square).then_inc(squared, 1)
            act.wait_ge(varied, 1)
            nc.scalar.activation(rstd[:], ps[:, 1, 0:T], ACT.Ln, scale=1.0 / (CONV_TILES * P),
                                 bias=e.EPS[:]).then_inc(rstd_step, 1)
            act.wait_ge(rstd_step, 1)
            nc.scalar.activation(rstd[:], rstd[:], ACT.Exp, scale=-0.5).then_inc(rstd_step, 1)
            for t in range(CONV_TILES):
                act.wait_ge(scaled, t + 1)
                nc.scalar.activation(y[:, t], y[:, t], ACT.Silu, scale=sv(e, "clw", t), bias=sv(e, "clb", t)).then_inc(silu_step, 1)
                act.wait_ge(silu_step, t + 1)
                nc.scalar.activation(e.H_HI[:, 6 + t], y[:, t], ACT.Copy).then_inc(hi_made, 1)

        @block.vector
        def _(dve):
            for j in range(2):
                nc.vector.tensor_tensor(lam_prod[:, j], sv(e, "dlam", 2 * j * DK, DK), sv(e, "dlam", (2 * j + 1) * DK, DK),
                                        ALU.mult).then_inc(pv, 1)
            for j in range(2):
                dve.wait_ge(pv, j + 1)
                nc.vector.reduce_sum(lam_sum[:, j:j + 1], lam_prod[:, j], AX).then_inc(pv, 1)
            dve.wait_ge(pa, 20)
            for h in range(HEADS):
                nc.vector.scalar_tensor_tensor(ef[:, h], ef[:, h], K_SCALE, rt(RT_MASKF), ALU.mult, ALU.mult).then_inc(pv, 1)
                nc.vector.scalar_tensor_tensor(eb[:, h], eb[:, h], K_SCALE, rt(RT_MASKB), ALU.mult, ALU.mult).then_inc(pv, 1)
            dve.wait_ge(pv, 12)
            nc.vector.tensor_tensor(e.INTRA[:], ef[:], eb[:], ALU.add).then_inc(pv, 1)
            dve.wait_ge(pa, 21)
            nc.vector.tensor_tensor(e.NEG_LAM[:], lam_sum[:, 3:4], lam_sum[:, 2:3], ALU.subtract).then_inc(pv, 1)
            dve.wait_ge(pv, 14)
            nc.vector.tensor_scalar(e.NEG_LAM[:], e.NEG_LAM[:], -lam_init, None, ALU.add).then_inc(pv, 1)
            nc.vector.tensor_scalar(e.DGN[:], sv(e, "dgn", 0, 4), 1.0 - lam_init, None, ALU.mult).then_inc(pv, 1)
            dve.wait_ge(summed, 1)
            for t in range(CONV_TILES):
                nc.vector.scalar_tensor_tensor(y[:, t], ps[:, 0, 0:T], -1.0 / (CONV_TILES * P), y[:, t], ALU.mult,
                                               ALU.add).then_inc(centered, 1)
            dve.wait_ge(rstd_step, 2)
            for t in range(CONV_TILES):
                dve.wait_ge(squared, t + 1)
                dve.wait_ge(centered, t + 1)
                nc.vector.tensor_tensor(y[:, t], y[:, t], rstd[:], ALU.mult).then_inc(scaled, 1)
            for t in range(CONV_TILES):
                dve.wait_ge(hi_made, t + 1)
                nc.vector.tensor_tensor(e.H_LO[:, 6 + t], y[:, t], e.H_HI[:, 6 + t].bitcast(F32),
                                        ALU.subtract).then_inc(done, 1)


def retention_block(nc, e, layer):
    with ExitStack() as ctx:
        sem = lambda n: e.semaphore((f"{n}_r{layer}"))
        sb = lambda n, s, d=F32: ctx.enter_context(nc.sbuf_tensor(f"{n}_r{layer}", s, d))
        loaded, transposed, tok_made, kd_f, kd_b, q_f, q_b, kv_made, kv_masked, state_step, scored, decayed = map(
            sem, ("loaded", "transposed", "tok_made", "kd_f", "kd_b", "q_f", "q_b", "kv_made", "kv_masked",
                  "state_step", "scored", "decayed"))
        out_made, out_copied, mean_made, centered, squared, var_made, rstd_step, scaled, hi_made, pair_done = map(
            sem, ("out_made", "out_copied", "mean_made", "centered", "squared", "var_made", "rstd_step", "scaled",
                  "hi_made", "pair_done"))
        q, k, v, g = (sb(n, [P, T]) for n in "qkvg")
        ktok, vtok = sb("ktok", [P, NCH, P]), sb("vtok", [P, NCH, P])
        kd, qd = sb("kd", [P, 2, NCH, P]), sb("qd", [P, 2, NCH, P])
        state, prob = sb("state", [P, 2, NCH, P]), sb("prob", [P, 2, NCH, P])
        o, o2 = q, k
        ps = ctx.enter_context(nc.psum_tensor(f"ps_r{layer}", [P, 2, 3 * 512], F32))
        block = ctx.enter_context(nc.Block())
        scratch = e.scratch[layer]
        chunk = lambda n: slice(n * P, (n + 1) * P)
        chunks = lambda ap: ap.rearrange("p (n c) -> p n c", c=P)
        orders = ([NCH_X, NCH_X + 1] + list(range(NCH_X)), list(range(NCH))[::-1])

        @block.sync
        def _(sp):
            for p in range(2):
                if p:
                    sp.wait_ge(loaded, 64 * p)
                    sp.wait_ge(pair_done, p)
                for buf, n in ((k, RK), (v, RV), (q, RQ), (g, RG)):
                    sp.dma_start(buf[:], scratch[n + p]).then_inc(loaded, 16)

        @block.tensor
        def _(pe):
            with pe.Fori(0, 2) as p:
                pe.wait_ge(loaded, 64 * p + 64)
                for j, src in enumerate((k, v)):
                    for n in range(NCH):
                        last = nc.tensor.transpose(ps[:, j, chunk(n)], src[:, chunk(n)], e.IDENT)
                    last.then_inc(transposed, 1)
                pe.wait_ge(tok_made, 2 * p + 2)
                for j, ready in enumerate((kd_f, kd_b)):
                    pe.wait_ge(ready, p + 1)
                    for n in range(NCH):
                        last = nc.tensor.matmul(ps[:, j, chunk(n)], kd[:, j, n], vtok[:, n], start=True, stop=True)
                    last.then_inc(kv_made, 1)
                for j in range(2):
                    pe.wait_ge(kv_masked, 2 * p + j + 1)
                    rows = slice(64 * j, 64 * j + 64)
                    for n in range(NCH):
                        last = nc.tensor.matmul(ps[:, j, chunk(n)], k[rows, chunk(n)], q[rows, chunk(n)], start=True, stop=True)
                    last.then_inc(scored, 1)
                pe.wait_ge(decayed, 2 * p + 2)
                pe.wait_ge(q_f, p + 1)
                pe.wait_ge(q_b, p + 1)
                for n in range(NCH):
                    nc.tensor.matmul(ps[:, 0, chunk(n)], state[:, 0, n], qd[:, 0, n], start=True, stop=False)
                    nc.tensor.matmul(ps[:, 0, chunk(n)], state[:, 1, n], qd[:, 1, n], start=False, stop=True)
                    for j in range(2):
                        last = nc.tensor.matmul(ps[64 * j:64 * j + 64, 0, chunk(n)], vtok[:, n, 64 * j:64 * j + 64],
                                                prob[:, j, n], start=False, stop=True, skip_group_check=True)
                last.then_inc(out_made, 1)
                pe.wait_ge(out_copied, p + 1)
                for a, z in blocks(T):
                    last = nc.tensor.matmul(ps[:, 1, a:z], e.RT[:, RT_BLK64 * P:(RT_BLK64 + 1) * P], o[:, a:z], start=True, stop=True)
                last.then_inc(mean_made, 1)
                pe.wait_ge(squared, p + 1)
                for a, z in blocks(T):
                    last = nc.tensor.matmul(ps[:, 0, a:z], e.RT[:, RT_BLK64 * P:(RT_BLK64 + 1) * P], o2[:, a:z], start=True, stop=True)
                last.then_inc(var_made, 1)

        @block.scalar
        def _(act):
            with act.Fori(0, 2) as p:
                for j, dst in enumerate((ktok, vtok)):
                    act.wait_ge(transposed, 2 * p + j + 1)
                    nc.scalar.activation(dst[:].rearrange("p n c -> p (n c)"), ps[:, j, 0:T], ACT.Copy).then_inc(tok_made, 1)
                act.wait_ge(out_made, p + 1)
                nc.scalar.activation(o[:], ps[:, 0, 0:T], ACT.Copy).then_inc(out_copied, 1)
                act.wait_ge(centered, p + 1)
                nc.scalar.activation(o2[:], o[:], ACT.Square).then_inc(squared, 1)
                act.wait_ge(var_made, p + 1)
                nc.scalar.activation(o2[:], ps[:, 0, 0:T], ACT.Ln, bias=e.EPS[:]).then_inc(rstd_step, 1)
                act.wait_ge(rstd_step, 2 * p + 1)
                nc.scalar.activation(o2[:], o2[:], ACT.Exp, scale=-0.5).then_inc(rstd_step, 1)
                act.wait_ge(scaled, 2 * p + 2)
                nc.scalar.activation(e.H_HI[:, bass.ds(p, 1)].rearrange("p a t -> p (a t)"), o[:], ACT.Copy).then_inc(hi_made, 1)

        def k_decay(j, p):
            return (e.K_DECAY[:, j, bass.ds(2 * p, 2)].rearrange("p (a h b) -> p a h b", a=1, b=1)
                    .to_broadcast([P, NCH, 2, DK]))

        def by_head(ap):
            return ap.rearrange("p n (h d) -> p n h d", h=2)

        def q_decay(j, p):
            return e.Q_DECAY[:, bass.ds(2 * j + p, 1)].to_broadcast([P, NCH, P])

        @block.gpsimd
        def _(pool):
            with pool.Fori(0, 2) as p:
                pool.wait_ge(loaded, 64 * p + 64)
                nc.gpsimd.tensor_tensor(qd[:, 1], chunks(q[:]), q_decay(1, p), ALU.mult).then_inc(q_b, 1)
                pool.wait_ge(tok_made, 2 * p + 1)
                nc.gpsimd.tensor_tensor(by_head(kd[:, 1]), by_head(ktok[:]), k_decay(1, p), ALU.mult).then_inc(kd_b, 1)

        @block.vector
        def _(dve):
            with dve.Fori(0, 2) as p:
                dve.wait_ge(loaded, 64 * p + 64)
                nc.vector.tensor_tensor(qd[:, 0], chunks(q[:]), q_decay(0, p), ALU.mult).then_inc(q_f, 1)
                dve.wait_ge(tok_made, 2 * p + 1)
                nc.vector.tensor_tensor(by_head(kd[:, 0]), by_head(ktok[:]), k_decay(0, p), ALU.mult).then_inc(kd_f, 1)
                for j in range(2):
                    first = nc.vector.memset(state[:, j, orders[j][0]], 0.0)
                first.then_inc(state_step, 1)
                mask = e.RT[:, RT_BLK * P:(RT_BLK + 1) * P].rearrange("p (a c) -> p a c", a=1).to_broadcast([P, NCH, P])
                for j in range(2):
                    dve.wait_ge(kv_made, 2 * p + j + 1)
                    nc.vector.tensor_tensor(prob[:, j], chunks(ps[:, j, 0:T]), mask, ALU.mult).then_inc(kv_masked, 1)
                dve.wait_ge(kv_masked, 2 * p + 2)
                for a, z in zip(range(NCH - 1), range(1, NCH)):
                    for j in range(2):
                        dve.wait_ge(state_step, (2 * (NCH - 1) + 1) * p + (2 * a + j if a else 1))
                        nc.vector.scalar_tensor_tensor(
                            state[:, j, orders[j][z]], state[:, j, orders[j][a]], e.CHUNK_DECAY[:, bass.ds(2 * j + p, 1)],
                            prob[:, j, orders[j][a]], ALU.mult, ALU.add).then_inc(state_step, 1)
                dve.wait_ge(state_step, (2 * (NCH - 1) + 1) * (p + 1))
                for j in range(2):
                    dve.wait_ge(scored, 2 * p + j + 1)
                    nc.vector.tensor_tensor(prob[:, j], chunks(ps[:, j, 0:T]),
                                            e.INTRA[:, bass.ds(2 * p + j, 1)].to_broadcast([P, NCH, P]),
                                            ALU.mult).then_inc(decayed, 1)
                dve.wait_ge(mean_made, p + 1)
                nc.vector.tensor_tensor(o[:], o[:], ps[:, 1, 0:T], ALU.subtract).then_inc(centered, 1)
                dve.wait_ge(rstd_step, 2 * p + 2)
                dve.wait_ge(centered, p + 1)
                nc.vector.tensor_tensor(o[:], o[:], o2[:], ALU.mult).then_inc(scaled, 1)
                dve.wait_ge(scaled, 2 * p + 1)
                gw = SV_COLS["rgn"][0]
                nc.vector.scalar_tensor_tensor(o[:], o[:], e.SV[:, bass.ds(gw + p, 1)], g[:], ALU.mult, ALU.mult).then_inc(scaled, 1)
                dve.wait_ge(hi_made, p + 1)
                nc.vector.tensor_tensor(e.H_LO[:, bass.ds(p, 1)].rearrange("p a t -> p (a t)"), o[:],
                                        e.H_HI[:, bass.ds(p, 1)].rearrange("p a t -> p (a t)").bitcast(F32),
                                        ALU.subtract).then_inc(pair_done, 1)


def attention_block(nc, e, layer, last_layer):
    n_q = NCH_X if last_layer else NCH
    width = n_q * P
    keys_of = lambda i: (0, T) if i < NCH_X else (SEQ, T)
    n_keys = lambda i: keys_of(i)[1] - keys_of(i)[0]
    in_fours = lambda n: [list(range(a, min(a + 4, n))) for a in range(0, n, 4)]
    rounds_of = lambda i: in_fours(n_keys(i) // P)
    v_rounds = in_fours(NCH)
    first_round = [len(v_rounds)]
    for i in range(n_q):
        first_round.append(first_round[-1] + len(rounds_of(i)))
    per_head = first_round[-1]
    AHEAD = 3
    RING = 4 if n_q % 4 == 0 else 5
    assert NCH_X % 4 == 0 and n_q % RING == 0

    with ExitStack() as ctx:
        sem = lambda n: e.semaphore(f"{n}_a{layer}")
        sb = lambda n, s, d=F32: ctx.enter_context(nc.sbuf_tensor(f"{n}_a{layer}", s, d))
        v_loaded, qk_loaded, scored, max_step, exped, recip_step, scaled1, combined = map(
            sem, ("v_loaded", "qk_loaded", "scored", "max_step", "exped", "recip_step", "scaled1", "combined"))
        transposed, t_copied, av_made, o_copied = map(sem, ("transposed", "t_copied", "av_made", "o_copied"))
        squared, total, rstd_step, normed, hi_made, lo_made = map(
            sem, ("squared", "total", "rstd_step", "normed", "hi_made", "lo_made"))
        hi_split, k_lo_split, q_lo_split = map(sem, ("hi_split", "k_lo_split", "q_lo_split"))
        v, q_twice, k_twice = sb("v", [P, T]), sb("q_twice", [P, 2, T]), sb("k_twice", [P, 2, T])
        q_parts, k_hi, k_lo = (sb(n, [P, 2, T], R32) for n in ("q_parts", "k_hi", "k_lo"))
        vtok, at = sb("vtok", [P, NCH, P]), sb("at", [P, NCH, P])
        ex0, ex1, ex0_ctx = sb("ex0", [P, 4, T]), sb("ex1", [P, 2, T]), sb("ex0_ctx", [P, 2, CTX])
        exp0_of = lambda i: ex0[:, i % 4] if i < NCH_X else ex0_ctx[:, i - NCH_X]
        o_all = sb("o_all", [P, HEADS, T])
        peak, neg_peak, total_e, recip = (sb(n, [P, RING, 2]) for n in ("peak", "neg_peak", "total_e", "recip"))
        ps = ctx.enter_context(nc.psum_tensor(f"ps_a{layer}", [P, 2, 3 * 512], F32))
        ps_t = ctx.enter_context(nc.psum_tensor(f"ps_t{layer}", [P, 512], F32))
        ps_o = ctx.enter_context(nc.psum_tensor(f"ps_o{layer}", [P, 512], F32))
        block = ctx.enter_context(nc.Block())
        scratch = e.scratch[layer]
        chunk = lambda n: slice(n * P, (n + 1) * P)

        def after(h, i, n, last_head=False):
            if i + n < n_q:
                return (h, i + n)
            return None if last_head else (h + 1, i + n - n_q)

        @block.sync
        def _(sp):
            def load_v(h):
                sp.dma_start(v[:], scratch[bass.ds(DV + h, 1)].rearrange("a p c -> p (a c)")).then_inc(v_loaded, 16)

            def load_qk(h):
                for m in range(2):
                    for buf, n in ((k_twice, DKK), (q_twice, DQ)):
                        for half in range(2):
                            sp.dma_start(buf[64 * half:64 * half + 64, m], scratch[bass.ds(n + h, 1), 64 * m:64 * m + 64].rearrange(
                                "a p c -> p (a c)")).then_inc(qk_loaded, 16)

            load_qk(0)
            load_v(0)
            with sp.Fori(0, HEADS - 1) as h:
                sp.wait_ge(qk_loaded, 128 * h + 128)
                sp.wait_ge(k_lo_split, 2 * h + 2)
                sp.wait_ge(q_lo_split, 2 * h + 2)
                load_qk(h + 1)
                sp.wait_ge(v_loaded, 16 * h + 16)
                sp.wait_ge(transposed, per_head * h + len(v_rounds))
                load_v(h + 1)

        @block.tensor
        def _(pe):
            def transposes(h, r, src, ids):
                pe.wait_ge(t_copied, per_head * h + r + 1)
                for n in ids:
                    t = nc.tensor.transpose(ps_t[:, (n - ids[0]) * P:(n - ids[0] + 1) * P], src[:, chunk(n)], e.IDENT)
                t.then_inc(transposed, 1)

            def scores(h, i, m):
                a0, z0 = keys_of(i)
                if i == 0:
                    pe.wait_ge(k_lo_split, 2 * h + m + 1)
                    pe.wait_ge(q_lo_split, 2 * h + m + 1)
                pe.wait_ge(exped, 2 * n_q * h + 2 * i + m + 1)
                for a, z in blocks(z0 - a0):
                    nc.tensor.matmul(ps[:, m, a:z], q_parts[:, m, chunk(i)], k_hi[:, m, a0 + a:a0 + z], start=True, stop=False)
                    t = nc.tensor.matmul(ps[:, m, a:z], q_parts[:, m, chunk(i)], k_lo[:, m, a0 + a:a0 + z], start=False, stop=True)
                t.then_inc(scored, 1)

            def values(h, i, r, ids):
                pe.wait_ge(t_copied, per_head * h + first_round[i] + r + 2)
                for n in ids:
                    t = nc.tensor.matmul(ps_o[:, 0:P], vtok[:, keys_of(i)[0] // P + n], at[:, n], start=n == 0,
                                         stop=n == n_keys(i) // P - 1)
                return t

            def v_transposes(h):
                pe.wait_ge(v_loaded, 16 * h + 16)
                for r, ids in enumerate(v_rounds):
                    transposes(h, r, v, ids)

            def step(nxt, prev):
                if nxt is not None:
                    scores(*nxt, 0)
                h, i = prev
                rounds = rounds_of(i)
                pe.wait_ge(combined, n_q * h + i + 1)
                transposes(h, first_round[i], exp0_of(i), rounds[0])
                if nxt is not None:
                    scores(*nxt, 1)
                if len(rounds) > 1:
                    transposes(h, first_round[i] + 1, exp0_of(i), rounds[1])
                pe.wait_ge(o_copied, n_q * h + i + 1)
                for r, ids in enumerate(rounds):
                    t = values(h, i, r, ids)
                    if r + 2 < len(rounds):
                        transposes(h, first_round[i] + r + 2, exp0_of(i), rounds[r + 2])
                t.then_inc(av_made, 1)

            v_transposes(0)
            for i in range(AHEAD):
                for m in range(2):
                    scores(0, i, m)
            with pe.Fori(0, HEADS - 1) as h:
                for i in range(n_q):
                    step(after(h, i, AHEAD), (h, i))
                v_transposes(h + 1)
            for i in range(n_q):
                step(after(HEADS - 1, i, AHEAD, True), (HEADS - 1, i))
            for h in range(HEADS):
                pe.wait_ge(squared, h + 1)
                if h >= 2:
                    pe.wait_ge(rstd_step, 2 * (h - 2) + 1)
                for a, z in blocks(width):
                    t = nc.tensor.matmul(ps[:, h % 2, a:z], e.ONES[:], ex0[:, h % 2, a:z], start=True, stop=True)
                t.then_inc(total, 1)

        @block.scalar
        def _(act):
            def copy_round(h, r, dst):
                act.wait_ge(transposed, per_head * h + r + 1)
                nc.scalar.activation(dst.rearrange("p n c -> p (n c)"), ps_t[:, 0:dst.shape[1] * P],
                                     ACT.Copy).then_inc(t_copied, 1)

            def exp(h, i, m):
                n, dst = n_keys(i), ex1[:, i % 2] if m else exp0_of(i)
                act.wait_ge(max_step, 4 * n_q * h + 4 * i + 2 * m + 2)
                nc.scalar.activation(dst[:, 0:n], ps[:, m, 0:n], ACT.Exp, bias=neg_peak[:, i % RING, m:m + 1],
                                     scale=K_SCALE, accum_out=total_e[:, i % RING, m:m + 1]).then_inc(exped, 1)

            def v_copies(h):
                for r, ids in enumerate(v_rounds):
                    copy_round(h, r, vtok[:, ids[0]:ids[-1] + 1])

            def split_hi(h, m, after_scores=True):
                if m == 0:
                    act.wait_ge(qk_loaded, 128 * h + 128)
                if after_scores:
                    act.wait_ge(scored, 2 * n_q * h + m - 1)
                nc.scalar.activation(k_hi[:, m], k_twice[:, m], ACT.Copy).then_inc(hi_split, 1)
                nc.scalar.activation(q_parts[:, m], q_twice[:, m], ACT.Copy).then_inc(hi_split, 1)

            def step(nxt, prev, split=None):
                h, i = prev
                for r, ids in enumerate(rounds_of(i)):
                    copy_round(h, first_round[i] + r, at[:, ids[0]:ids[-1] + 1])
                    if r == 0 and split is not None:
                        split_hi(split, 1)
                    if r == 0 and nxt is not None:
                        exp(*nxt, 0)
                if nxt is not None:
                    exp(*nxt, 1)
                act.wait_ge(av_made, n_q * h + i + 1)
                nc.scalar.activation(o_all[:, bass.ds(h, 1), chunk(i)].rearrange("p a t -> p (a t)"), ps_o[:, 0:P],
                                     ACT.Copy).then_inc(o_copied, 1)

            nc.scalar.activation(neg_peak[:, 0], e.UNIT[:, 0:2], ACT.Copy).then_inc(exped, 2)
            nc.scalar.activation(neg_peak[:, 1], e.UNIT[:, 0:2], ACT.Copy).then_inc(t_copied, 1)
            nc.scalar.activation(recip[:, 0], e.UNIT[:, 0:2], ACT.Copy).then_inc(o_copied, 1)
            for m in range(2):
                split_hi(0, m, False)
            v_copies(0)
            for i in range(AHEAD):
                for m in range(2):
                    exp(0, i, m)
            with act.Fori(0, HEADS - 1) as h:
                for i in range(n_q):
                    step(after(h, i, AHEAD), (h, i), h + 1 if i == n_q - AHEAD else None)
                    if i == n_q - AHEAD - 1:
                        split_hi(h + 1, 0)
                v_copies(h + 1)
            for i in range(n_q):
                step(after(HEADS - 1, i, AHEAD, True), (HEADS - 1, i))
            act.wait_ge(o_copied, n_q * HEADS + 1)

            def square(h):
                if h >= 2:
                    act.wait_ge(total, h - 1)
                nc.scalar.activation(ex0[:, h % 2, 0:width], o_all[:, h, 0:width], ACT.Square).then_inc(squared, 1)

            square(0)
            square(1)
            for h in range(HEADS):
                act.wait_ge(total, h + 1)
                if h >= 2:
                    act.wait_ge(normed, h - 1)
                nc.scalar.activation(ex1[:, h % 2, 0:width], ps[:, h % 2, 0:width], ACT.Ln, scale=1.0 / P,
                                     bias=e.EPS[:]).then_inc(rstd_step, 1)
                act.wait_ge(rstd_step, 2 * h + 1)
                nc.scalar.activation(ex1[:, h % 2, 0:width], ex1[:, h % 2, 0:width], ACT.Exp, scale=-0.5).then_inc(rstd_step, 1)
                if h + 2 < HEADS:
                    square(h + 2)
                act.wait_ge(normed, h + 1)
                nc.scalar.activation(e.H_HI[:, 2 + h, 0:width], o_all[:, h, 0:width], ACT.Copy).then_inc(hi_made, 1)

        @block.gpsimd
        def _(pool):
            def split_k_lo(h, m):
                pool.wait_ge(hi_split, 4 * h + 2 * m + 1)
                nc.gpsimd.tensor_tensor(k_lo[:, m], k_twice[:, m], k_hi[:, m].bitcast(F32),
                                        ALU.subtract).then_inc(k_lo_split, 1)

            def scale_tiles(h, next_head):
                for i in range(n_q):
                    n = n_keys(i)
                    pool.wait_ge(recip_step, 2 * n_q * h + 2 * i + 2)
                    nc.gpsimd.tensor_tensor(e.POOL_SCRAP[:], e.UNIT[:], e.UNIT[:], ALU.mult)
                    nc.gpsimd.tensor_scalar(ex1[:, i % 2, 0:n], ex1[:, i % 2, 0:n], recip[:, i % RING, 1:2], 1.0,
                                            ALU.mult, ALU.mult).then_inc(scaled1, 1)
                    if next_head is not None and i >= n_q - 2:
                        split_k_lo(next_head, i - (n_q - 2))

            for m in range(2):
                split_k_lo(0, m)
            with pool.Fori(0, HEADS - 1) as h:
                scale_tiles(h, h + 1)
            scale_tiles(HEADS - 1, None)

        @block.vector
        def _(dve):
            def split_q_lo(h, m):
                dve.wait_ge(hi_split, 4 * h + 2 * m + 2)
                low = slice(64, P)
                nc.vector.tensor_tensor(q_parts[low, m], q_twice[low, m], q_parts[low, m].bitcast(F32),
                                        ALU.subtract).then_inc(q_lo_split, 1)

            def peaks(h, i, m):
                dve.wait_ge(scored, 2 * n_q * h + 2 * i + m + 1)
                nc.vector.reduce_max(peak[:, i % RING, m:m + 1], ps[:, m, 0:n_keys(i)], AX).then_inc(max_step, 1)
                dve.wait_ge(max_step, 4 * n_q * h + 4 * i + 2 * m + 1)
                nc.vector.tensor_scalar(neg_peak[:, i % RING, m:m + 1], peak[:, i % RING, m:m + 1], -K_SCALE, None,
                                        ALU.mult).then_inc(max_step, 1)

            def reciprocals(h, i):
                c = 2 * n_q * h + 2 * i
                dve.wait_ge(exped, c + 4)
                nc.vector.reciprocal(recip[:, i % RING], total_e[:, i % RING]).then_inc(recip_step, 1)
                dve.wait_ge(recip_step, c + 1)
                nc.vector.tensor_tensor(recip[:, i % RING, 1:2], recip[:, i % RING, 1:2], e.NEG_LAM[:], ALU.mult).then_inc(recip_step, 1)

            def combine(h, i):
                n, e0 = n_keys(i), exp0_of(i)
                dve.wait_ge(recip_step, 2 * n_q * h + 2 * i + 2)
                dve.wait_ge(scaled1, n_q * h + i + 1)
                nc.vector.scalar_tensor_tensor(e0[:, 0:n], e0[:, 0:n], recip[:, i % RING, 0:1], ex1[:, i % 2, 0:n],
                                               ALU.mult, ALU.add).then_inc(combined, 1)

            def step(h, i, last_head=False):
                nxt, following = after(h, i, 1, last_head), after(h, i, 2, last_head)
                combine(h, i)
                if nxt is not None:
                    reciprocals(*nxt)
                if following is not None:
                    if following[1] == 0:
                        for m in range(2):
                            split_q_lo(following[0], m)
                    for m in range(2):
                        peaks(*following, m)

            dve.wait_ge(o_copied, 1)
            for m in range(2):
                split_q_lo(0, m)
            peaks(0, 0, 0)
            peaks(0, 0, 1)
            reciprocals(0, 0)
            peaks(0, 1, 0)
            peaks(0, 1, 1)
            with dve.Fori(0, HEADS - 1) as h:
                for i in range(n_q):
                    step(h, i)
            for i in range(n_q):
                step(HEADS - 1, i, True)
            for h in range(HEADS):
                dve.wait_ge(rstd_step, 2 * h + 2)
                nc.vector.scalar_tensor_tensor(o_all[:, h, 0:width], o_all[:, h, 0:width], e.DGN[:, h:h + 1],
                                               ex1[:, h % 2, 0:width], ALU.mult, ALU.mult).then_inc(normed, 1)
                dve.wait_ge(hi_made, h + 1)
                nc.vector.tensor_tensor(e.H_LO[:, 2 + h, 0:width], o_all[:, h, 0:width],
                                        e.H_HI[:, 2 + h, 0:width].bitcast(F32), ALU.subtract).then_inc(lo_made, 1)


def mlp_block(nc, e, layer, last_layer):
    width = SEQ if last_layer else T
    sides = [(0, 0, SEQ)] + ([] if last_layer else [(1, SEQ, T)])
    with ExitStack() as ctx:
        sem = lambda n: e.semaphore((f"{n}_f{layer}"))
        sb = lambda n, s, d=F32: ctx.enter_context(nc.sbuf_tensor(f"{n}_f{layer}", s, d))
        s = NormSemaphores(sem, "n2")
        slot_loaded = [sem("slot_loaded0"), sem("slot_loaded1")]
        w_hi_made, w_lo_made, out_done, out_added, x_loaded = map(
            sem, ("w_hi_made", "w_lo_made", "out_done", "out_added", "x_loaded"))
        up_done, up_relu, up_squared, g_hi_made, g_lo_made, down_done, down_added = map(
            sem, ("up_done", "up_relu", "up_squared", "g_hi_made", "g_lo_made", "down_done", "down_added"))
        stage, w_hi, w_lo = sb("stage", [P, 2, SLOT]), sb("w_hi", [P, 2, SLOT], R32), sb("w_lo", [P, 2, SLOT], R32)
        with ExitStack() as inner:
            tb = lambda n, s: inner.enter_context(nc.sbuf_tensor(f"{n}_f{layer}", s, F32))
            sq, acc, rstd, tmp = tb("sq", [P, 2, T]), tb("acc", [P, T]), tb("rstd", [P, T]), tb("tmp", [P, 3, T])
            own_stage = tb("own_stage", [P, 4, GROUP_COLS])
        g_hi, g_lo = sb("g_hi", [P, FF_CHUNK_TILES, T], R32), sb("g_lo", [P, FF_CHUNK_TILES, T], R32)
        hidden = sb("hidden", [P, 2, T])
        ps = ctx.enter_context(nc.psum_tensor(f"ps_f{layer}", [P, 2, 3 * 512], F32))
        b = NormBuffers(sq=sq, acc=acc, rstd=rstd, tmp=tmp, ps=ps)
        block = ctx.enter_context(nc.Block())
        side, own = not last_layer, layer == 0
        if side:
            side_loaded, unit_added, group_reduced, side_biased, gain_made = map(
                sem, ("side_loaded", "unit_added", "group_reduced", "side_biased", "gain_made"))
            side_stage, side_acc = sb("side_stage", [P, GROUP_COLS]), sb("side_acc", [P, 2, GROUP_COLS])
            side_ps = ctx.enter_context(nc.psum_tensor(f"side_ps_f{layer}", [P, 512], F32))
            own_groups = OWN_GROUPS if own else 0
            own_loaded = [sem(f"own_loaded{n}") for n in range(4)] if own else None
        slots = OUT_TILES + FF_CHUNKS * FF_SLOTS
        up0, down0 = OUT_TILES, OUT_TILES + FF_CHUNK_TILES

        @block.sync
        def _(sp):
            for u in range(2):
                sp.dma_start(stage[:, u], e.w_dram[layer, OUT0 + u]).then_inc(slot_loaded[u], 16)
            def load(n, u, i):
                sp.wait_ge(w_lo_made, n + u - 1 + 2 * i)
                sp.dma_start(stage[:, u], e.w_dram[layer, bass.ds(OUT0 + n + u + 2 * i, 1)].rearrange(
                    "a p c -> p (a c)")).then_inc(slot_loaded[u], 16)

            def chunk_load(c, n):
                load(OUT_TILES + n - n % 2, n % 2, FF_SLOTS // 2 * c)

            def own_load(n, i):
                if i is not None:
                    sp.wait_ge(unit_added, 2 * (n - 4) + 2 + 2 * KT * i)
                    sp.dma_start(own_stage[:, n % 4], e.units_dram[bass.ds(n + KT * i, 1)].rearrange(
                        "a p c -> p (a c)")).then_inc(own_loaded[n % 4], 16)
                else:
                    sp.dma_start(own_stage[:, n % 4], e.units_dram[n]).then_inc(own_loaded[n % 4], 16)

            def side_load(c, n):
                if side:
                    if n > 0:
                        sp.wait_ge(unit_added, 2 * KT * own_groups + 2 * n + 2 * KT * c)
                    sp.dma_start(side_stage[:], e.units_dram[bass.ds(KT * OWN_GROUPS + n + KT * c, 1)].rearrange(
                        "a p c -> p (a c)")).then_inc(side_loaded, 16)

            if own:
                for n in range(4):
                    own_load(n, None)
            for k in range(KT):
                sp.dma_start(e.X[:, k, 0:width], (e.x_dram if layer == 0 else e.x_kept)[k][:, 0:width]).then_inc(x_loaded, 16)
            with sp.Fori(0, OUT_TILES // 2 - 1) as i:
                for u in range(2):
                    load(2, u, i)
                    if own:
                        for r in range(4):
                            own_load(4 + 4 * u + r, i)
            for u in range(2):
                load(OUT_TILES, u, 0)
                if own and u == 0:
                    for r in range(4):
                        own_load(4 + r + KT * (OWN_GROUPS - 1), 0)
            for n in range(2, FF_SLOTS // 2):
                chunk_load(0, n)
            side_load(0, 0)

            def chunk(c, more):
                for j in range(FF_CHUNK_TILES):
                    chunk_load(c, FF_SLOTS // 2 + j)
                    side_load(c, 2 * j + 1)
                    if j < FF_CHUNK_TILES - 1:
                        side_load(c, 2 * j + 2)
                if more:
                    for n in range(FF_SLOTS // 2):
                        chunk_load(c + 1, n)
                    side_load_first(c + 1)

            def side_load_first(c):
                if side:
                    sp.wait_ge(unit_added, 2 * KT * own_groups + 2 * KT * c)
                    side_load(c, 0)

            with sp.Fori(0, FF_CHUNKS - 1) as c:
                chunk(c, True)
            chunk(FF_CHUNKS - 1, False)

        @block.scalar
        def _(act):
            def split(u, count):
                act.wait_ge(slot_loaded[u], count)
                nc.scalar.activation(w_hi[:, u], stage[:, u], ACT.Copy).then_inc(w_hi_made, 1)

            nc.scalar.activation(e.SCRAP[:, 0:1], e.UNIT[:, 0:1], ACT.Copy).then_inc(out_added, 2)
            split(0, 16)
            split(1, 16)
            with act.Fori(0, OUT_TILES // 2) as i:
                for u in range(2):
                    act.wait_ge(out_done, 2 * i + u + 1)
                    split(u, 16 * i + 32)
            act.wait_ge(out_added, OUT_TILES + 2)
            norm_act(nc, act, e, s, b, width)

            def split_after(n, c):
                split(n % 2, 16 * (n // 2 + 2) + 16 * (FF_SLOTS // 2) * c)

            def up(c, j):
                act.wait_ge(up_done, FF_CHUNK_TILES * c + j + 1)
                if j >= 2:
                    act.wait_ge(g_lo_made, FF_CHUNK_TILES * c + j - 1)
                nc.scalar.activation(hidden[:, j % 2, 0:width], ps[:, j % 2, 0:width], ACT.Relu).then_inc(up_relu, 1)
                act.wait_ge(up_relu, FF_CHUNK_TILES * c + j + 1)
                nc.scalar.activation(hidden[:, j % 2, 0:width], hidden[:, j % 2, 0:width], ACT.Square).then_inc(up_squared, 1)
                act.wait_ge(up_squared, FF_CHUNK_TILES * c + j + 1)
                nc.scalar.activation(g_hi[:, j, 0:width], hidden[:, j % 2, 0:width], ACT.Copy).then_inc(g_hi_made, 1)
                split_after(up0 + j, c)

            def down(c, j, more):
                act.wait_ge(down_done, KT * c + 2 * j + 2)
                if more:
                    split_after(down0 + j, c)

            with act.Fori(0, FF_CHUNKS - 1) as c:
                for j in range(FF_CHUNK_TILES):
                    up(c, j)
                for j in range(KT // 2):
                    down(c, j, True)
            for j in range(FF_CHUNK_TILES):
                up(FF_CHUNKS - 1, j)
            for j in range(KT // 2):
                down(FF_CHUNKS - 1, j, j < KT // 2 - 2)

        @block.tensor
        def _(pe):
            def product(u, j, x_hi, x_lo, first, n_k, ready, count):
                for k in range(n_k):
                    if ready is not None:
                        pe.wait_ge(ready, count + k + 1)
                    kk = slice((first + k) * P, (first + k + 1) * P)
                    for a, z in blocks(width):
                        last = mm3(nc, ps[:, u, a:z], w_hi[:, j, kk], w_lo[:, j, kk], x_hi[:, k, a:z],
                                   x_lo[:, k, a:z], k == 0, k == n_k - 1)
                return last

            def side_reduce(g):
                if side:
                    pe.wait_ge(side_biased, g + 1)
                    pe.wait_ge(unit_added, 2 * KT * g + 2 * KT)
                    for m in range(GROUP):
                        for v in range(2):
                            t = nc.tensor.matmul(side_ps[:, 2 * m + v:2 * m + v + 1], side_acc[:, v, m * P:(m + 1) * P],
                                                 e.ONES[:, 0:1], start=True, stop=True)
                    t.then_inc(group_reduced, 1)

            with pe.Fori(0, OUT_TILES // 2) as i:
                for u in range(2):
                    pe.wait_ge(w_lo_made, 2 * i + u + 1)
                    pe.wait_ge(out_added, 2 * i + u + 1)
                    product(u, u, e.H_HI, e.H_LO, 0, KT, None, 0).then_inc(out_done, 1)
                if own:
                    side_reduce(i)
            norm_pe(nc, pe, e, s, b, width)
            with pe.Fori(0, FF_CHUNKS) as c:
                for j in range(FF_CHUNK_TILES):
                    pe.wait_ge(w_lo_made, up0 + 1 + j + FF_SLOTS * c)
                    if j < 2:
                        pe.wait_ge(down_added, KT * c + 1 + j)
                    else:
                        pe.wait_ge(up_relu, FF_CHUNK_TILES * c + j - 1)
                    product(j % 2, j % 2, e.H_HI, e.H_LO, 0, KT, s.lo, 0).then_inc(up_done, 1)
                for m in range(KT):
                    j = m // 2
                    pe.wait_ge(w_lo_made, down0 + 1 + j + FF_SLOTS * c)
                    if m < 2:
                        pe.wait_ge(up_relu, FF_CHUNK_TILES * c + 3 + m)
                    else:
                        pe.wait_ge(down_added, KT * c + 1 + m)
                    product(m % 2, j % 2, g_hi, g_lo, FF_CHUNK_TILES * (m % 2), FF_CHUNK_TILES, g_lo_made,
                            FF_CHUNK_TILES * c).then_inc(down_done, 1)
                    if m == 3 and side:
                        side_reduce(own_groups + c)

        @block.gpsimd
        def _(pool):
            norm_pool(nc, pool, e, s, b, width, layer, e.GAIN2, 3)

        @block.vector
        def _(dve):
            def split_rest(u, count):
                dve.wait_ge(w_hi_made, count)
                nc.vector.tensor_tensor(w_lo[:, u], stage[:, u], w_hi[:, u].bitcast(F32),
                                        ALU.subtract).then_inc(w_lo_made, 1)

            def add_gated(u, x_of, gate_of, added):
                for n, (side, a, z) in enumerate(sides):
                    op = nc.vector.scalar_tensor_tensor(x_of(a, z), ps[:, u, a:z], gate_of(side), x_of(a, z),
                                                        ALU.mult, ALU.add)
                op.then_inc(added, 1)

            def unit(n, g, place):
                for v in range(2):
                    c = e.COND[:, n, v:v + 1]
                    if n == 0:
                        if v == 0:
                            dve.wait_ge(group_reduced, g)
                        nc.vector.tensor_scalar(side_acc[:, v], place, c, None, ALU.mult).then_inc(unit_added, 1)
                    else:
                        dve.wait_ge(unit_added, 2 * KT * g + 2 * n + v - 1)
                        nc.vector.scalar_tensor_tensor(side_acc[:, v], place, c, side_acc[:, v], ALU.mult,
                                                       ALU.add).then_inc(unit_added, 1)

            def own_units(i, u):
                if own:
                    for n in range(4 * u, 4 * u + 4):
                        dve.wait_ge(own_loaded[n % 4], 16 * (n // 4 + 1) + 32 * i)
                        unit(n, i, own_stage[:, n % 4])

            def chunk_units(c, j):
                if side:
                    for n in (2 * j, 2 * j + 1):
                        dve.wait_ge(side_loaded, 16 * (n + 1) + 16 * KT * c)
                        unit(n, own_groups + c, side_stage[:])

            def group_bias(g, of_layer, first):
                dve.wait_ge(group_reduced, g + 1)
                add_bias(nc, e, of_layer, side_ps, first, GROUP).then_inc(side_biased, 1)

            nc.vector.tensor_copy(e.SCRAP[:, 1:2], e.UNIT[:, 0:1]).then_inc(down_added, 2)
            if side:
                nc.vector.tensor_copy(e.SCRAP[:, 2:3], e.UNIT[:, 0:1]).then_inc(side_biased, 1)
            split_rest(0, 1)
            split_rest(1, 2)
            dve.wait_ge(x_loaded, 16 * KT)
            with dve.Fori(0, OUT_TILES // 2) as i:
                for u in range(2):
                    own_units(i, u)
                    dve.wait_ge(out_done, 2 * i + u + 1)
                    add_gated(u, lambda a, z: e.X[:, bass.ds(u + 2 * i, 1), a:z].rearrange("p k t -> p (k t)"),
                              lambda side: e.MOD[:, bass.ds(2 * (ADA_TILES * layer + 2 * KT + u) + side + 4 * i, 1)], out_added)
                    split_rest(u, 2 * i + u + 3)
                if own:
                    group_bias(i, layer, FIRST_TILES + GROUP * i)
            if own:
                dve.wait_ge(side_biased, OWN_GROUPS + 1)
                make_gain(nc, e, layer, e.GAIN2, N2W, 4).then_inc(gain_made, 1)
            dve.wait_ge(out_added, OUT_TILES + 2)
            norm_dve(nc, dve, e, s, b, width)

            def up(c, j):
                dve.wait_ge(g_hi_made, FF_CHUNK_TILES * c + j + 1)
                nc.vector.tensor_tensor(g_lo[:, j, 0:width], hidden[:, j % 2, 0:width],
                                        g_hi[:, j, 0:width].bitcast(F32), ALU.subtract).then_inc(g_lo_made, 1)
                split_rest(j % 2, up0 + j + 3 + FF_SLOTS * c)
                chunk_units(c, j)

            def down(c, j, more):
                for m in (2 * j, 2 * j + 1):
                    dve.wait_ge(down_done, KT * c + m + 1)
                    dve.wait_ge(down_added, KT * c + 2)
                    add_gated(m % 2, lambda a, z: e.X[:, m, a:z],
                              lambda side: e.MOD[:, bass.ds(2 * (ADA_TILES * layer + 5 * KT + m) + side, 1)], down_added)
                if more:
                    split_rest(j % 2, down0 + j + 3 + FF_SLOTS * c)
                if side and j == 2:
                    group_bias(own_groups + c, layer + 1, GROUP * c)

            with dve.Fori(0, FF_CHUNKS - 1) as c:
                for j in range(FF_CHUNK_TILES):
                    up(c, j)
                for j in range(KT // 2):
                    down(c, j, True)
            for j in range(FF_CHUNK_TILES):
                up(FF_CHUNKS - 1, j)
            for j in range(KT // 2):
                down(FF_CHUNKS - 1, j, j < KT // 2 - 2)
            if side:
                dve.wait_ge(side_biased, own_groups + FF_CHUNKS + 1)
                make_gain(nc, e, layer + 1, e.GAIN1, N1W, 1).then_inc(gain_made, 1)
                dve.wait_ge(s.shifted, 2 * KT)
                make_gain(nc, e, layer + 1, e.GAIN2, N2W, 4).then_inc(gain_made, 1)


def final_block(nc, e):
    with ExitStack() as ctx:
        sem = lambda n: e.semaphore((f"{n}_final"))
        sb = lambda n, s, d=F32: ctx.enter_context(nc.sbuf_tensor(f"{n}_final", s, d))
        squared, summed, total, rstd_step, scaled, stored = map(
            sem, ("squared", "summed", "total", "rstd_step", "scaled", "stored"))
        sq, acc, rstd = sb("sq", [P, 2, SEQ]), sb("acc", [P, SEQ]), sb("rstd", [P, SEQ])
        ps = ctx.enter_context(nc.psum_tensor("ps_final", [P, SEQ], F32))
        block = ctx.enter_context(nc.Block())

        @block.sync
        def _(sp):
            for k in range(KT):
                sp.wait_ge(scaled, k + 1)
                sp.dma_start(e.out_dram[k], e.X[:, k, 0:SEQ]).then_inc(stored, 16)
            sp.wait_ge(stored, 16 * KT)

        @block.scalar
        def _(act):
            for k in range(KT):
                if k >= 2:
                    act.wait_ge(summed, k - 1)
                nc.scalar.activation(sq[:, k % 2], e.X[:, k, 0:SEQ], ACT.Square).then_inc(squared, 1)
            act.wait_ge(total, 1)
            nc.scalar.activation(rstd[:], ps[:], ACT.Ln, scale=1.0 / D_MODEL, bias=e.EPS[:]).then_inc(rstd_step, 1)
            act.wait_ge(rstd_step, 1)
            nc.scalar.activation(rstd[:], rstd[:], ACT.Exp, scale=-0.5).then_inc(rstd_step, 1)

        @block.tensor
        def _(pe):
            pe.wait_ge(summed, KT)
            for a, z in blocks(SEQ):
                last = nc.tensor.matmul(ps[:, a:z], e.ONES[:], acc[:, a:z], start=True, stop=True)
            last.then_inc(total, 1)

        @block.vector
        def _(dve):
            for k in range(KT):
                dve.wait_ge(squared, k + 1)
                if k == 0:
                    nc.vector.tensor_copy(acc[:], sq[:, 0]).then_inc(summed, 1)
                else:
                    dve.wait_ge(summed, k)
                    nc.vector.tensor_tensor(acc[:], acc[:], sq[:, k % 2], ALU.add).then_inc(summed, 1)
            dve.wait_ge(rstd_step, 2)
            for k in range(KT):
                nc.vector.scalar_tensor_tensor(e.X[:, k, 0:SEQ], e.X[:, k, 0:SEQ], sv(e, "final", k), rstd[:],
                                               ALU.mult, ALU.mult).then_inc(scaled, 1)


def build_program(nc, x_dram, cond_dram, id1_dram, sv_dram, mv_dram, ada_dram, units_dram, w_dram, rope_dram, rt_dram, out_dram, layers=DEPTH):
    with ExitStack() as ctx:
        sb = lambda n, s, d=F32: ctx.enter_context(nc.sbuf_tensor(n, s, d))
        e = Shared()
        e.x_dram, e.cond_dram, e.id1_dram, e.sv_dram = x_dram, cond_dram, id1_dram, sv_dram
        e.mv_dram, e.ada_dram, e.units_dram, e.w_dram, e.rope_dram, e.rt_dram, e.out_dram = mv_dram, ada_dram, units_dram, w_dram, rope_dram, rt_dram, out_dram
        e.scratch = [nc.dram_tensor(f"projected{i}", (IN_TILES, P, T), F32).ap() for i in range(layers)]
        e.H_HI, e.H_LO = sb("h_hi", [P, KT, T], R32), sb("h_lo", [P, KT, T], R32)
        e.x_kept = nc.dram_tensor("x_kept", (KT, P, T), F32).ap()
        e.ID1, e.ONES, e.SV = sb("identity", [P, P]), sb("ones", [P, P]), sb("vectors", [P, SV_LEN])
        e.COND, e.MOD = sb("cond", [P, KT, 2]), sb("mod", [P, 2 * ADA_TILES * DEPTH])
        e.MV = sb("modulation_vectors", [P, MV_LEN * DEPTH])
        e.GAIN1, e.GAIN2 = sb("gain1", [P, KT, 2]), sb("gain2", [P, KT, 2])
        e.EPS, e.UNIT, e.SCRAP, e.POOL_SCRAP = sb("eps", [P, 1]), sb("unit", [P, 2]), sb("scrap", [P, 4]), sb("pool_scrap", [P, 2])
        e.LGA, e.LGP, e.CHUNK_DECAY = sb("lga", [P, 8]), sb("lgp", [P, 4]), sb("chunk_decay", [P, 4])
        e.K_DECAY, e.NEG_LAM, e.DGN = sb("k_decay", [P, 2, HEADS]), sb("neg_lam", [P, 1]), sb("dgn", [P, HEADS])
        e.IDENT = e.ID1[:]
        x_place = ExitStack()

        def place_x(n):
            e.X = x_place.enter_context(nc.sbuf_tensor(f"x{n}", [P, KT, T], F32))

        for layer in range(layers):
            last = layer == DEPTH - 1
            layer_semaphores = ExitStack()
            e.semaphore = lambda name: e.held.append(layer_semaphores.enter_context(nc.semaphore(name))) or e.held[-1]
            e.held = []
            if layer == 0:
                place_x(0)
                modulation_block(nc, e)
            projection_block(nc, e, layer)
            x_place.close()
            with (nc.sbuf_tensor(f"rt{layer}", [P, RT_LEN], F32) as e.RT,
                  nc.sbuf_tensor(f"intra{layer}", [P, HEADS, P], F32) as e.INTRA,
                  nc.sbuf_tensor(f"q_decay{layer}", [P, 4, P], F32) as e.Q_DECAY):
                conv_norm_block(nc, e, layer)
                retention_block(nc, e, layer)
            attention_block(nc, e, layer, last)
            place_x(layer + 1)
            mlp_block(nc, e, layer, last)
            with nc.Block() as block:
                @block.sync
                def _(sp):
                    for s in e.held:
                        sp.sem_clear(s)
            layer_semaphores.close()
        e.semaphore = lambda name: ctx.enter_context(nc.semaphore(name))
        final_block(nc, e)
        x_place.close()


def rope_tables():
    f = np.float32
    half = DK // 2
    inv = f(ROPE_BASE) ** (-np.arange(0, DK, 2, dtype=f) / f(DK))
    inv_ax = f(ROPE_BASE) ** (-np.arange(0, half, 2, dtype=f) / f(half))
    pos = np.arange(SEQ)
    ret, ax = pos[:, None].astype(f) * inv[None, :], None
    rows, cols = (pos // GRID_W)[:, None].astype(f) * inv_ax, (pos % GRID_W)[:, None].astype(f) * inv_ax
    p = np.arange(P) % DK
    sign = np.where(p % 32 < 16, -1.0, 1.0).astype(f)[:, None]
    plain = ret[:, 16 * (p // 32) + p % 16].T
    axial = np.where(p[:, None] < 32, rows[:, p % 16].T, cols[:, p % 16].T)
    out = np.zeros((2, P, 2, T), f)
    out[:, :, 0] = 1.0
    for i, ang in enumerate((plain, axial)):
        out[i, :, 0, :SEQ] = np.cos(ang.astype(f))
        out[i, :, 1, :SEQ] = np.sin(ang.astype(f)) * sign
    return out


def retention_tables():
    f = np.float32
    s, c = np.arange(P)[:, None], np.arange(P)[None, :]
    one = np.ones((P, P))
    head = (s // DK == c // DK)
    tables = [np.maximum(c - s, 0), c >= s, np.maximum(s - c, 0), s >= c, (c + 1) * one, (P - c) * one, head, head / DK,
              P - 1 - s, s]
    return np.concatenate([t.astype(f) for t in tables], axis=1)


def columns(v):
    return v.reshape(-1, P).T


def kernel(**inputs):
    import concourse.bacc as bacc
    from concourse.bass_utils import run_bass_kernel_spmd

    a = {k: np.ascontiguousarray(v) for k, v in inputs.items()}
    x_t = np.concatenate([a["x"][0].T, a["ctx"][0].T], axis=1).reshape(KT, P, T)
    cond = np.stack([a["c"][0].reshape(KT, P).T, a["c_ctx"].reshape(KT, P).T], axis=-1)

    pair = np.arange(DK).reshape(2, 2, 16).transpose(1, 0, 2).reshape(-1)
    heads = (np.arange(HEADS)[:, None] * DK + pair).reshape(-1)
    width = HEADS * DK
    start = dict(rq=0, rk=width, rv=2 * width, rg=3 * width, dq=4 * width, dk=6 * width, dv=8 * width,
                 cv=10 * width, cg=11 * width)
    plain = np.arange(width)
    wide = np.arange(2 * width)
    order = np.concatenate([start["cv"] + plain, start["cg"] + plain, start["rq"] + heads, start["rk"] + heads,
                            start["rv"] + plain, start["rg"] + plain, start["dq"] + wide, start["dk"] + wide,
                            start["dv"] + wide])

    def slots(w):
        k, m = w.shape
        return w.reshape(k // P, P, m // P, P).transpose(2, 1, 0, 3).reshape(m // P, P, k)

    def units(w):
        k, m = w.shape
        return w.reshape(KT, P, m // GROUP_COLS, GROUP_COLS).transpose(2, 0, 1, 3).reshape(-1, P, GROUP_COLS)

    weights, vectors, mod_vectors = [], [], []
    for i in range(DEPTH):
        parts = [slots(a["w_in"][i][:, order]), slots(a["w_out"][i])]
        up, rows = slots(a["mlp_w1"][i]), FF_CHUNK_TILES * P
        for c in range(FF_CHUNKS):
            parts.append(up[FF_CHUNK_TILES * c:FF_CHUNK_TILES * (c + 1)])
            down = slots(a["mlp_w2"][i][rows * c:rows * (c + 1)])
            parts.append(down.reshape(KT // 2, 2, P, rows).transpose(0, 2, 1, 3).reshape(KT // 2, P, SLOT))
        weights.append(np.concatenate(parts))
        decay = a["ret_log_decay"][i]
        mod_vectors.append(np.concatenate([columns(a["norm1_w"][i]), columns(a["norm2_w"][i]), columns(a["ada_b"][i])], axis=1))
        vectors.append(np.concatenate([
            columns(a["ret_gn_w"][i]),
            columns(a["diff_gn_w"][i]),
            a["conv_w"][i].reshape(TAPS, CONV_TILES, P).transpose(2, 1, 0).reshape(P, CONV_TILES * TAPS),
            columns(a["conv_b"][i]), columns(a["conv_ln_w"][i]), columns(a["conv_ln_b"][i]),
            np.tile(decay.reshape(1, -1), (P, 1)),
            np.repeat(decay.reshape(2, 2, 2), DK, axis=2).reshape(4, P).T,
            np.tile(a["diff_lam"][i].reshape(1, -1), (P, 1)),
            columns(a["final_norm_w"])], axis=1))

    arrays = {"x_t": x_t, "cond_in": cond, "identity_in": np.eye(P, dtype=np.float32), "vectors_in": np.stack(vectors),
              "mod_vectors_in": np.concatenate(mod_vectors, axis=1),
              "modulation_first": slots(a["ada_w"][0])[:FIRST_TILES],
              "modulation_units": np.concatenate([units(a["ada_w"][0][:, FIRST_TILES * P:])]
                                                 + [units(a["ada_w"][i]) for i in range(1, DEPTH)]),
              "weights": np.stack(weights), "rope": rope_tables(), "retention": retention_tables()}
    arrays = {k: np.ascontiguousarray(v) for k, v in arrays.items()}
    nc = bacc.Bacc("TRN2", target_bir_lowering=False, num_devices=1)
    args = [nc.dram_tensor(k, v.shape, F32, kind="ExternalInput").ap() for k, v in arrays.items()]
    out = nc.dram_tensor("out_t", (KT, P, SEQ), F32, kind="ExternalOutput").ap()
    build_program(nc, *args, out)
    got = run_bass_kernel_spmd(nc, [arrays], core_ids=[0]).results[0]["out_t"]
    return np.ascontiguousarray(got.reshape(D_MODEL, SEQ).T)[None]
```

```python
import math
from contextlib import ExitStack

import numpy as np

import concourse.bass as bass
from concourse import mybir


class NormSemaphores:

    def __init__(self, sem, name):
        self.squared, self.summed, self.total = sem(f"{name}_squared"), sem(f"{name}_summed"), sem(f"{name}_total")
        self.psum_free, self.rstd = sem(f"{name}_psum_free"), sem(f"{name}_rstd")
        self.normed, self.shifted = sem(f"{name}_normed"), sem(f"{name}_shifted")
        self.hi, self.lo = sem(f"{name}_hi"), sem(f"{name}_lo")


class NormBuffers:
    def __init__(self, sq, acc, rstd, tmp, ps):
        self.sq, self.acc, self.rstd, self.tmp, self.ps = sq, acc, rstd, tmp, ps


class Shared:
    pass


F32 = mybir.dt.float32
R32 = mybir.dt.float32r
ACT = mybir.ActivationFunctionType
ALU = mybir.AluOpType
AX = mybir.AxisListType.X

P = 128
D_MODEL, SEQ, CTX, DEPTH = 1024, 1024, 256, 2
T = SEQ + CTX
KT = D_MODEL // P
N_MOD = 6
D_FF = 4 * D_MODEL
EPS = 1e-6
GRID_W = 64
ROPE_BASE = 10000.0
DK = 64
HEADS = 4
TAPS = 31
PAD = (TAPS - 1) // 2
CONV_TILES = 2
NCH = T // P
NCH_X = SEQ // P
SLOT = KT * P
K_SCALE = DK ** -0.5

ADA_TILES = N_MOD * KT
IN_TILES = 24
OUT_TILES = KT
FF_CHUNK_TILES = 4
FF_CHUNKS = D_FF // (FF_CHUNK_TILES * P)
IN0 = 0
OUT0 = IN0 + IN_TILES
FF0 = OUT0 + OUT_TILES
FF_SLOTS = FF_CHUNK_TILES + KT // 2
LAYER_SLOTS = FF0 + FF_CHUNKS * FF_SLOTS

CV, CG, RQ, RK, RV, RG, DQ, DKK, DV = 0, 2, 4, 6, 8, 10, 12, 16, 20
STORED0 = RQ

U_X0 = PAD
U_C0 = PAD + SEQ + PAD
U_LEN = U_C0 + CTX + PAD
Y_C0 = SEQ + PAD
Y_LEN = Y_C0 + CTX

SV_COLS = {}
_at = 0
for _name, _n in (("rgn", 2), ("dgn", 4), ("cw", CONV_TILES * TAPS),
                  ("cb", 2), ("clw", 2), ("clb", 2), ("lga", 8), ("lgp", 4), ("dlam", 4 * DK), ("final", KT)):
    SV_COLS[_name] = (_at, _at + _n)
    _at += _n
SV_LEN = _at
N1W, N2W, ADAB = 0, KT, 2 * KT
MV_LEN = 2 * KT + ADA_TILES
FIRST_TILES = 3 * KT
MOD_PLACES = 14
GROUP = 6
GROUP_COLS = GROUP * P
OWN_GROUPS, NEXT_GROUPS = (ADA_TILES - FIRST_TILES) // GROUP, ADA_TILES // GROUP

RT_RELF, RT_MASKF, RT_RELB, RT_MASKB, RT_QF, RT_QB, RT_BLK, RT_BLK64 = range(8)
RT_LEN = 8 * P + 2


def blocks(width):
    return [(a, min(a + 512, width)) for a in range(0, width, 512)]


def mm3(nc, out, w_hi, w_lo, x_hi, x_lo, start, stop):
    nc.tensor.matmul(out, w_hi, x_hi, start=start, stop=False)
    nc.tensor.matmul(out, w_hi, x_lo, start=False, stop=False)
    return nc.tensor.matmul(out, w_lo, x_hi, start=False, stop=stop)


def first_products(nc, pe, ps, w_hi, w_lo, e, width, ready, done):
    for k in range(KT):
        pe.wait_ge(ready, k + 1)
        kk = slice(k * P, (k + 1) * P)
        for u in range(2):
            for a, z in blocks(width):
                last = mm3(nc, ps[:, u, a:z], w_hi[:, u, kk], w_lo[:, u, kk], e.H_HI[:, k, a:z], e.H_LO[:, k, a:z],
                           k == 0, k == KT - 1)
            if k == KT - 1:
                last.then_inc(done, 1)


def sv(e, name, a=0, n=1):
    lo, _ = SV_COLS[name]
    return e.SV[:, lo + a:lo + a + n]


def mod_tile(nc, ps, w, at, cond):
    for k in range(KT):
        last = nc.tensor.matmul(ps[:, bass.ds(2 * at, 2)], w[:, k * P:(k + 1) * P], cond[:, k], start=k == 0,
                                stop=k == KT - 1)
    return last


def add_bias(nc, e, layer, ps, first, n):
    bias = (e.MV[:, bass.ds(layer * MV_LEN + ADAB + first, n)].rearrange("p (k a) -> p k a", a=1)
            .to_broadcast([P, n, 2]))
    return nc.vector.tensor_tensor(e.MOD[:, bass.ds(2 * (ADA_TILES * layer + first), 2 * n)].rearrange("p (k a) -> p k a", a=2),
                                   ps[:, 0:2 * n].rearrange("p (k a) -> p k a", a=2), bias, ALU.add)


def make_gain(nc, e, layer, gain, w, scale):
    w_ap = e.MV[:, MV_LEN * layer + w:MV_LEN * layer + w + KT].rearrange("p (k a) -> p k a", a=1).to_broadcast([P, KT, 2])
    lo = 2 * (ADA_TILES * layer + KT * scale)
    return nc.vector.scalar_tensor_tensor(gain[:], e.MOD[:, lo:lo + 2 * KT].rearrange("p (k a) -> p k a", a=2), 1.0,
                                          w_ap, ALU.add, ALU.mult)


def modulation_block(nc, e):
    with ExitStack() as ctx:
        sem = lambda n: e.semaphore((f"{n}_m"))
        vectors_loaded, inputs_loaded, x_loaded = sem("vectors_loaded"), sem("inputs_loaded"), [sem(f"x_loaded{k}") for k in range(KT // 2)]
        slot_loaded = [sem(f"slot_loaded{n}") for n in range(MOD_PLACES)]
        cond_ready, tile_done, biased, gain_made = map(sem, ("cond_ready", "tile_done", "biased", "gain_made"))
        s = e.first_norm = NormSemaphores(sem, "n1")
        stage = ctx.enter_context(nc.sbuf_tensor("ada_stage", [P, MOD_PLACES, SLOT], F32))
        sq = ctx.enter_context(nc.sbuf_tensor("sq_m", [P, 2, T], F32))
        ps = ctx.enter_context(nc.psum_tensor("ada_ps", [P, 3, 512], F32))
        norm_ps = ctx.enter_context(nc.psum_tensor("norm_ps_m", [P, 1, 3 * 512], F32))
        b = NormBuffers(sq=sq, acc=e.RSTD_ACC, rstd=e.FIRST_RSTD, tmp=None, ps=norm_ps)
        block = ctx.enter_context(nc.Block())

        @block.sync
        def _(sp):
            sp.dma_start(e.COND[:], e.cond_dram).then_inc(inputs_loaded, 16)
            sp.dma_start(e.ID1[:], e.id1_dram).then_inc(inputs_loaded, 16)
            sp.dma_start(e.MV[:], e.mv_dram).then_inc(vectors_loaded, 16)
            for n in range(KT):
                sp.dma_start(stage[:, n], e.ada_dram[n]).then_inc(slot_loaded[n], 16)
            for k in range(KT):
                sp.dma_start(e.X[:, k], e.x_dram[k]).then_inc(x_loaded[k // 2], 16)
            for n in range(KT, FIRST_TILES):
                if n >= MOD_PLACES:
                    sp.wait_ge(tile_done, n - MOD_PLACES + 1)
                sp.dma_start(stage[:, n % MOD_PLACES], e.ada_dram[n]).then_inc(slot_loaded[n % MOD_PLACES], 16)

        @block.scalar
        def _(act):
            act.wait_ge(inputs_loaded, 32)
            nc.scalar.activation(e.COND[:], e.COND[:], ACT.Silu).then_inc(cond_ready, 1)
            for k in range(KT):
                act.wait_ge(x_loaded[k // 2], 32)
                square_tile(nc, act, s, b, e.X[:, k], k % 2, k)
            inverse_rms(nc, act, e, s, b, T)

        @block.tensor
        def _(pe):
            pe.wait_ge(cond_ready, 1)
            for n in range(FIRST_TILES):
                pe.wait_ge(slot_loaded[n % MOD_PLACES], 16 * (n // MOD_PLACES + 1))
                mod_tile(nc, ps[:, n // KT], stage[:, n % MOD_PLACES], n % KT, e.COND).then_inc(tile_done, 1)
                if n == 2 * KT - 1:
                    norm_pe(nc, pe, e, s, b, T)

        @block.vector
        def _(dve):
            nc.vector.memset(e.EPS[:], EPS)
            nc.vector.memset(e.ONES[:], 1.0)
            nc.vector.memset(e.UNIT[:], 1.0)
            clear_sum(nc, s, b)
            for k in range(KT):
                add_square(nc, dve, s, b, T, k % 2, k)
            dve.wait_ge(vectors_loaded, 16)
            for g in range(3):
                dve.wait_ge(tile_done, KT * (g + 1))
                add_bias(nc, e, 0, ps[:, g], KT * g, KT).then_inc(biased, 1)
            dve.wait_ge(biased, 3)
            make_gain(nc, e, 0, e.GAIN1, N1W, 1).then_inc(gain_made, 1)


def square_tile(nc, act, s, b, x, u, summed):
    act.wait_ge(s.summed, summed)
    nc.scalar.activation(b.sq[:, u, 0:x.shape[-1]], x, ACT.Square).then_inc(s.squared, 1)


def clear_sum(nc, s, b):
    nc.vector.memset(b.acc[:], 0.0).then_inc(s.summed, 1)


def add_square(nc, dve, s, b, width, u, k):
    dve.wait_ge(s.squared, k + 1)
    dve.wait_ge(s.summed, k + 1)
    nc.vector.tensor_tensor(b.acc[:, 0:width], b.acc[:, 0:width], b.sq[:, u, 0:width], ALU.add).then_inc(s.summed, 1)


def inverse_rms(nc, act, e, s, b, width):
    act.wait_ge(s.total, 1)
    nc.scalar.activation(b.rstd[:, 0:width], b.ps[:, 0, 0:width], ACT.Ln, scale=1.0 / D_MODEL,
                         bias=e.EPS[:]).then_inc(s.psum_free, 2)
    act.wait_ge(s.psum_free, 2)
    nc.scalar.activation(b.rstd[:, 0:width], b.rstd[:, 0:width], ACT.Exp, scale=-0.5).then_inc(s.rstd, 1)


def norm_hi(nc, act, e, s, b, width):
    per = 2 if width > SEQ else 1
    for k in range(KT):
        act.wait_ge(s.shifted, per * (k + 1))
        nc.scalar.activation(e.H_HI[:, k, 0:width], b.tmp[:, k % 3, 0:width], ACT.Copy).then_inc(s.hi, 1)


def norm_pe(nc, pe, e, s, b, width):
    pe.wait_ge(s.summed, KT + 1)
    for a, z in blocks(width):
        last = nc.tensor.matmul(b.ps[:, 0, a:z], e.ONES[:], b.acc[:, a:z], start=True, stop=True)
    last.then_inc(s.total, 1)


def norm_dve(nc, dve, e, s, b, width):
    for k in range(KT + 2):
        if k < KT:
            if k >= 3:
                dve.wait_ge(s.lo, k - 2)
            nc.vector.tensor_tensor(b.tmp[:, k % 3, 0:width], e.X[:, k, 0:width], b.rstd[:, 0:width],
                                    ALU.mult).then_inc(s.normed, 1)
        if k >= 2:
            j = k - 2
            dve.wait_ge(s.hi, j + 1)
            nc.vector.tensor_tensor(e.H_LO[:, j, 0:width], b.tmp[:, j % 3, 0:width],
                                    e.H_HI[:, j, 0:width].bitcast(F32), ALU.subtract).then_inc(s.lo, 1)


def norm_pool(nc, pool, e, s, b, width, layer, gain, shift):
    for k in range(KT):
        pool.wait_ge(s.normed, k + 1)
        for j, (a, z) in enumerate(((0, SEQ), (SEQ, width))):
            if z > a:
                sh = 2 * (ADA_TILES * layer + KT * shift + k) + j
                nc.gpsimd.tensor_scalar(b.tmp[:, k % 3, a:z], b.tmp[:, k % 3, a:z], gain[:, k, j:j + 1],
                                        e.MOD[:, sh:sh + 1], ALU.mult, ALU.add).then_inc(s.shifted, 1)


def projection_block(nc, e, layer, last_layer):
    columns_of = lambda n: SEQ if last_layer and not (RK <= n < RG or n >= DKK) else T
    pairs = range(IN_TILES // 2)
    starts = [i for i in pairs if i == 0 or columns_of(2 * i) != columns_of(2 * i - 2)] + [len(pairs)]
    stretches = lambda first, end: [(max(a, first), min(z, end)) for a, z in zip(starts, starts[1:])
                                    if max(a, first) < min(z, end)]
    with ExitStack() as ctx:
        sem = lambda n: e.semaphore((f"{n}_p{layer}"))
        sb = lambda n, s, d=F32: ctx.enter_context(nc.sbuf_tensor(f"{n}_p{layer}", s, d))
        s = NormSemaphores(sem, "n1") if layer else e.first_norm
        slot_loaded = [sem("slot_loaded0"), sem("slot_loaded1")]
        w_hi_made, w_lo_made, tile_done = sem("w_hi_made"), sem("w_lo_made"), sem("tile_done")
        evacuated = s.psum_free
        vectors_loaded = sem("vectors_loaded")
        table_loaded, rope_step, cos_made = sem("table_loaded"), sem("rope_step"), sem("cos_made")
        stored = [sem("stored0"), sem("stored1")]
        margins_zeroed, gated, conv_step, conv_stored, x_stored = map(
            sem, ("margins_zeroed", "gated", "conv_step", "conv_stored", "x_stored"))

        stage, w_hi, w_lo = sb("stage", [P, 2, SLOT]), sb("w_hi", [P, 2, SLOT], R32), sb("w_lo", [P, 2, SLOT], R32)
        raw, rot, cosx, table = sb("raw", [P, 2, T]), sb("rot", [P, T]), sb("cosx", [P, T]), sb("table", [P, 2, T])
        with nc.sbuf_tensor(f"tmp_p{layer}", [P, 3, T], F32) as tmp:
            pass
        u_buf, y_buf = sb("u_buf", [P, CONV_TILES, U_LEN]), sb("y_buf", [P, CONV_TILES, Y_LEN])
        ps = ctx.enter_context(nc.psum_tensor(f"ps_p{layer}", [P, 2, 3 * 512], F32))
        b = NormBuffers(sq=raw, acc=rot, rstd=cosx if layer else e.FIRST_RSTD, tmp=tmp, ps=ps)
        block = ctx.enter_context(nc.Block())
        scratch = e.scratch[layer]

        out_of_psum = lambda n: n + 3

        @block.sync
        def _(sp):
            for u in range(2):
                sp.dma_start(stage[:, u], e.w_dram[layer, IN0 + u]).then_inc(slot_loaded[u], 16)
            sp.dma_start(e.SV[:], e.sv_dram[layer]).then_inc(vectors_loaded, 16)
            sp.dma_start(table[:], e.rope_dram[0]).then_inc(table_loaded, 16)
            if layer > 0:
                for k in range(KT):
                    sp.dma_start(e.x_kept[k], e.X[:, k]).then_inc(x_stored, 16)

            def load(n, u):
                sp.wait_ge(w_lo_made, n + 1)
                sp.dma_start(stage[:, u], e.w_dram[layer, bass.ds(IN0 + 2 + n, 1)].rearrange(
                    "a p c -> p (a c)")).then_inc(slot_loaded[u], 16)

            def store(n, u):
                sp.dma_start(scratch[bass.ds(n, 1)].rearrange("a p c -> p (a c)"), raw[:, u]).then_inc(stored[u], 16)

            def store_conv(t):
                for (a, z), y in (((0, SEQ), 0), ((SEQ, T), Y_C0)):
                    sp.dma_start(scratch[t][:, a:z], y_buf[:, t, y:y + z - a]).then_inc(conv_stored, 16)

            for n in range(RQ):
                load(n, n % 2)
            for n in range(RQ, RV):
                load(n, n % 2)
                sp.wait_ge(rope_step, 3 * (n - RQ) + 3)
                store(n, n % 2)
            sp.dma_start(table[:], e.rope_dram[1]).then_inc(table_loaded, 16)
            for n in range(RV, DQ):
                load(n, n % 2)
                sp.wait_ge(evacuated, out_of_psum(n))
                store(n, n % 2)
            sp.wait_ge(conv_step, TAPS)
            store_conv(0)
            with sp.Fori(0, (DV - DQ) // 2) as i:
                for u in range(2):
                    load(DQ + u + 2 * i, u)
                    sp.wait_ge(rope_step, 3 * (RV - RQ) + 3 * u + 3 + 6 * i)
                    store(DQ + u + 2 * i, u)
            for n in range(DV, IN_TILES):
                if n < IN_TILES - 2:
                    load(n, n % 2)
                sp.wait_ge(evacuated, out_of_psum(n))
                store(n, n % 2)
            sp.wait_ge(conv_step, 2 * TAPS)
            store_conv(1)
            for u in range(2):
                sp.wait_ge(stored[u], 16 * (IN_TILES - STORED0) // 2)
            sp.wait_ge(conv_stored, 16 * 4)
            if layer > 0:
                sp.wait_ge(x_stored, 16 * KT)

        @block.scalar
        def _(act):
            def split(n, u):
                nc.scalar.activation(w_hi[:, u], stage[:, u], ACT.Copy).then_inc(w_hi_made, 1)

            for u in range(2):
                act.wait_ge(slot_loaded[u], 16)
                split(u, u)
            if layer > 0:
                for k in range(KT):
                    square_tile(nc, act, s, b, e.X[:, k], k % 2, k)
                inverse_rms(nc, act, e, s, b, T)
            norm_hi(nc, act, e, s, b, T)

            def tile(n, u, func, width, loads=True, load_count=None):
                act.wait_ge(tile_done, n + 1)
                nc.scalar.activation(raw[:, u, 0:width], ps[:, u, 0:width], func).then_inc(evacuated, 1)
                if loads:
                    act.wait_ge(slot_loaded[u], load_count)
                    split(n + 2, u)

            loads_of = lambda n: 16 * (n // 2 + 2)
            act.wait_ge(margins_zeroed, 2)
            for n in range(CV, CG):
                act.wait_ge(tile_done, n + 1)
                if columns_of(n) == T:
                    nc.scalar.activation(u_buf[:, n - CV, U_C0:U_C0 + CTX], ps[:, n % 2, SEQ:T], ACT.Copy)
                nc.scalar.activation(u_buf[:, n - CV, U_X0:U_X0 + SEQ], ps[:, n % 2, 0:SEQ], ACT.Copy).then_inc(evacuated, 1)
                act.wait_ge(slot_loaded[n % 2], loads_of(n))
                split(n + 2, n % 2)
            for n in range(CG, RQ):
                tile(n, n % 2, ACT.Sigmoid, columns_of(n), True, loads_of(n))
            for n in range(RQ, DQ):
                if n < RQ + 2:
                    act.wait_ge(gated, n - RQ + 1)
                else:
                    act.wait_ge(stored[n % 2], 16 * ((n - STORED0) // 2))
                tile(n, n % 2, ACT.Silu if n >= RG else ACT.Copy, columns_of(n), True, loads_of(n))
            for first, end in stretches(DQ // 2, DV // 2):
                with act.Fori(first - DQ // 2, end - DQ // 2) as i:
                    for u in range(2):
                        act.wait_ge(stored[u], 16 * ((DQ - STORED0) // 2) + 16 * i)
                        tile(DQ + u + 2 * i, u, ACT.Copy, columns_of(2 * first), True, loads_of(DQ) + 16 * i)
            for n in range(DV, IN_TILES):
                act.wait_ge(stored[n % 2], 16 * ((n - STORED0) // 2))
                tile(n, n % 2, ACT.Copy, columns_of(n), n < IN_TILES - 2, loads_of(n))

        @block.tensor
        def _(pe):
            if layer > 0:
                norm_pe(nc, pe, e, s, b, T)
            def pair(i, width):
                for u in range(2):
                    pe.wait_ge(w_lo_made, 2 * i + u + 1)
                    pe.wait_ge(evacuated, 2 * i + u + 1)
                    for k in range(KT):
                        kk = slice(k * P, (k + 1) * P)
                        for a, z in blocks(width):
                            last = mm3(nc, ps[:, u, a:z], w_hi[:, u, kk], w_lo[:, u, kk], e.H_HI[:, k, a:z],
                                       e.H_LO[:, k, a:z], k == 0, k == KT - 1)
                    last.then_inc(tile_done, 1)

            pe.wait_ge(w_lo_made, 2)
            pe.wait_ge(evacuated, 2)
            first_products(nc, pe, ps, w_hi, w_lo, e, columns_of(0), s.lo, tile_done)
            for first, end in stretches(1, IN_TILES // 2):
                with pe.Fori(first, end) as i:
                    pair(i, columns_of(2 * first))

        @block.gpsimd
        def _(pool):
            norm_pool(nc, pool, e, s, b, T, layer, e.GAIN1, 0)

            def rope_cos(n, r, u):
                pool.wait_ge(evacuated, out_of_psum(n))
                nc.gpsimd.tensor_tensor(cosx[:], raw[:, u], table[:, 0], ALU.mult).then_inc(cos_made, 1)

            pool.wait_ge(table_loaded, 16)
            for n in range(RQ, RV):
                if n > RQ:
                    pool.wait_ge(rope_step, 3 * (n - RQ))
                rope_cos(n, n - RQ, n % 2)
            pool.wait_ge(table_loaded, 32)
            with pool.Fori(0, (DV - DQ) // 2) as i:
                for u in range(2):
                    pool.wait_ge(rope_step, 3 * (RV - RQ) + 3 * u + 6 * i)
                    rope_cos(DQ + u + 2 * i, 0, u)

        @block.vector
        def _(dve):
            def split_rest(n, u):
                dve.wait_ge(w_hi_made, n + 1)
                nc.vector.tensor_tensor(w_lo[:, u], stage[:, u], w_hi[:, u].bitcast(F32),
                                        ALU.subtract).then_inc(w_lo_made, 1)

            split_rest(0, 0)
            split_rest(1, 1)
            if layer > 0:
                clear_sum(nc, s, b)
                for k in range(KT):
                    add_square(nc, dve, s, b, T, k % 2, k)
                dve.wait_ge(s.rstd, 1)
            norm_dve(nc, dve, e, s, b, T)
            dve.wait_ge(s.lo, KT)
            nc.vector.memset(u_buf[:, :, 0:PAD], 0.0)
            nc.vector.memset(u_buf[:, :, U_X0 + SEQ:U_C0], 0.0).then_inc(margins_zeroed, 1)
            nc.vector.memset(u_buf[:, :, U_C0 + (0 if last_layer else CTX):U_LEN], 0.0).then_inc(margins_zeroed, 1)

            swap = [(p + 16) % 32 for p in range(32)]

            def rope(n, r3, u, cos_count, tables):
                dve.wait_ge(table_loaded, tables)
                dve.wait_ge(evacuated, out_of_psum(n))
                nc.vector.tensor_copy(e.SCRAP[:, 1:2], e.UNIT[:, 0:1])
                nc.vector.stream_shuffle(rot[:], raw[:, u], swap).then_inc(rope_step, 1)
                dve.wait_ge(rope_step, r3 + 1)
                nc.vector.tensor_tensor(rot[:], rot[:], table[:, 1], ALU.mult).then_inc(rope_step, 1)
                dve.wait_ge(cos_made, cos_count)
                dve.wait_ge(rope_step, r3 + 2)
                nc.vector.tensor_tensor(raw[:, u], rot[:], cosx[:], ALU.add).then_inc(rope_step, 1)

            w0, b0 = SV_COLS["cw"][0], SV_COLS["cb"][0]

            def tap(t, j, weight, count):
                dve.wait_ge(conv_step, count)
                nc.vector.scalar_tensor_tensor(y_buf[:, t], u_buf[:, t, bass.ds(j, Y_LEN)], e.SV[:, bass.ds(weight, 1)],
                                               y_buf[:, t], ALU.mult, ALU.add).then_inc(conv_step, 1)

            def first_tap(t):
                nc.vector.tensor_scalar(y_buf[:, t], u_buf[:, t, 0:Y_LEN], e.SV[:, w0 + t * TAPS:w0 + t * TAPS + 1],
                                        e.SV[:, b0 + t:b0 + t + 1], ALU.mult, ALU.add).then_inc(conv_step, 1)

            for n in range(CV, CG):
                split_rest(n + 2, n % 2)
            for n in range(CG, RQ):
                t = n - CG
                dve.wait_ge(evacuated, out_of_psum(n))
                for c0, a, z in ((U_X0, 0, SEQ), (U_C0, SEQ, T)):
                    g = nc.vector.tensor_tensor(u_buf[:, t, c0:c0 + z - a], u_buf[:, t, c0:c0 + z - a],
                                                raw[:, n % 2, a:z], ALU.mult)
                g.then_inc(gated, 1)
                split_rest(n + 2, n % 2)
            dve.wait_ge(gated, 2)
            dve.wait_ge(vectors_loaded, 16)
            taps_done = 0
            for n in range(RQ, DQ):
                if n < RV:
                    rope(n, 3 * (n - RQ), n % 2, n - RQ + 1, 16)
                split_rest(n + 2, n % 2)
                for _ in range(4):
                    if taps_done == 0:
                        first_tap(0)
                        taps_done = 1
                    elif taps_done < TAPS:
                        tap(0, taps_done, w0 + taps_done, taps_done)
                        taps_done += 1
            first_tap(1)
            with dve.Fori(0, (DV - DQ) // 2) as i:
                for u in range(2):
                    rope(DQ + u + 2 * i, 3 * (RV - RQ) + 3 * u + 6 * i, u, RV - RQ + 1 + u + 2 * i, 32)
                    split_rest(DQ + 2 + u + 2 * i, u)
                    for j in range(3):
                        q = 3 * u + j + 1
                        tap(1, 6 * i + q, w0 + TAPS + q + 6 * i, TAPS + q + 6 * i)
            for n in range(DV, IN_TILES):
                if n < IN_TILES - 2:
                    split_rest(n + 2, n % 2)
                for _ in range(2):
                    j = 1 + 3 * (DV - DQ) + 2 * (n - DV) + _
                    if j < TAPS:
                        tap(1, j, w0 + TAPS + j, TAPS + j)


def retention_block(nc, e, layer):
    lam_init = 0.8 - 0.6 * math.exp(-0.3 * layer)
    with ExitStack() as ctx:
        sem = lambda n: e.semaphore((f"{n}_r{layer}"))
        sb = lambda n, s, d=F32: ctx.enter_context(nc.sbuf_tensor(f"{n}_r{layer}", s, d))
        y_loaded, tables_loaded, c_summed, c_centered, c_squared, c_varied, c_rstd, c_scaled, c_silu, c_hi, c_lo = map(
            sem, ("y_loaded", "tables_loaded", "c_summed", "c_centered", "c_squared", "c_varied", "c_rstd", "c_scaled",
                  "c_silu", "c_hi", "c_lo"))
        pa, pv = sem("prep_act"), sem("prep_dve")
        k_in, v_in, q_in, g_in = ([sem(f"{n}_in{p}") for p in range(2)] for n in "kvqg")
        transposed, tok_made, kd_f, kd_b, q_f, q_b, kv_made, kv_masked, state_step, scored, decayed = map(
            sem, ("transposed", "tok_made", "kd_f", "kd_b", "q_f", "q_b", "kv_made", "kv_masked", "state_step",
                  "scored", "decayed"))
        out_made, out_copied, mean_made, centered, squared, var_made, rstd_step, scaled, hi_made, lo_made = map(
            sem, ("out_made", "out_copied", "mean_made", "centered", "squared", "var_made", "rstd_step", "scaled",
                  "hi_made", "lo_made"))
        q, k, v, g = (sb(n, [P, 2, T]) for n in "qkvg")
        ktok, vtok = sb("ktok", [P, NCH, P]), sb("vtok", [P, 2, NCH, P])
        kd, qd = sb("kd", [P, 2, NCH, P]), sb("qd", [P, 2, NCH, P])
        state, prob = sb("state", [P, 2, NCH, P]), sb("prob", [P, 2, NCH, P])
        y, rstd = e.K_TWICE, e.V_HEAD
        ef, eb = (e.Q_TWICE0[:, j * HEADS * P:(j + 1) * HEADS * P].rearrange("p (h c) -> p h c", h=HEADS) for j in range(2))
        e.qk_loaded = [e.semaphore(f"qk_loaded{m}_a{layer}") for m in range(2)]
        e.v_loaded = e.semaphore(f"v_loaded_a{layer}")
        lam_prod, lam_sum = sb("lam_prod", [P, 2, DK]), sb("lam_sum", [P, 4])
        y_sq = prob[:].rearrange("p j n c -> p j (n c)")
        o, o2 = q, k
        ps = ctx.enter_context(nc.psum_tensor(f"ps_r{layer}", [P, 2, 3 * 512], F32))
        block = ctx.enter_context(nc.Block())
        scratch = e.scratch[layer]
        rt = lambda i: e.RT[:, i * P:(i + 1) * P]
        chunk = lambda n: slice(n * P, (n + 1) * P)
        chunks = lambda ap: ap.rearrange("p (n c) -> p n c", c=P)
        orders = ([NCH_X, NCH_X + 1] + list(range(NCH_X)), list(range(NCH))[::-1])
        steps_per_pair = 2 * (NCH - 1) + 1
        KV_SET = ((0, 1), (1, 1))
        SCORE_SET = ((0, 1), (1, 0))
        OUT_SET, MEAN_SET, VAR_SET = (0, 1), (0, 0), (0, 1)

        @block.sync
        def _(sp):
            sp.dma_start(e.RT[:], e.rt_dram).then_inc(tables_loaded, 16)
            for t in range(CONV_TILES):
                sp.dma_start(y[:, t], e.scratch[layer][t]).then_inc(y_loaded, 16)
            sp.wait_ge(y_loaded, 16 * CONV_TILES)
            for p in range(2):
                for buf, n, loaded in ((k, RK, k_in), (v, RV, v_in), (q, RQ, q_in)):
                    sp.dma_start(buf[:, p], scratch[n + p]).then_inc(loaded[p], 16)
            for p in range(2):
                sp.dma_start(g[:, p], scratch[RG + p]).then_inc(g_in[p], 16)
            sp.wait_ge(c_lo, 2)
            for half in range(2):
                sp.dma_start(e.K_TWICE[64 * half:64 * half + 64, 0], scratch[DKK, 0:64]).then_inc(e.qk_loaded[0], 16)
            sp.wait_ge(pv, 13)
            for half in range(2):
                sp.dma_start(e.Q_TWICE0[64 * half:64 * half + 64], scratch[DQ, 0:64]).then_inc(e.qk_loaded[0], 16)
            sp.dma_start(e.V_HEAD[:], scratch[DV]).then_inc(e.v_loaded, 16)

        @block.tensor
        def _(pe):
            def ones_product(lhs, src, at, done, pieces=1):
                for a, z in blocks(T):
                    for t in range(pieces):
                        last = nc.tensor.matmul(ps[:, at, a:z], lhs, src[t][:, a:z], start=t == 0, stop=t == pieces - 1)
                last.then_inc(done, 1)

            def transposes(p, j, src, loaded, at):
                pe.wait_ge(loaded[p], 16)
                for n in range(NCH):
                    last = nc.tensor.transpose(ps[:, at, chunk(n)], src[:, p, chunk(n)], e.IDENT)
                last.then_inc(transposed, 1)

            def chunk_sums(p, j):
                pe.wait_ge((kd_f, kd_b)[j], p + 1)
                for n in range(NCH):
                    last = nc.tensor.matmul(ps[:, KV_SET[p][j], chunk(n)], kd[:, j, n], vtok[:, p, n], start=True, stop=True)
                last.then_inc(kv_made, 1)

            def scores(p, j):
                pe.wait_ge(q_in[p], 16)
                rows = slice(64 * j, 64 * j + 64)
                for n in range(NCH):
                    last = nc.tensor.matmul(ps[:, SCORE_SET[p][j], chunk(n)], k[rows, p, chunk(n)], q[rows, p, chunk(n)],
                                            start=True, stop=True)
                last.then_inc(scored, 1)

            def output(p):
                at = OUT_SET[p]
                pe.wait_ge(decayed, 2 * p + 2)
                pe.wait_ge(state_step, steps_per_pair * (p + 1))
                pe.wait_ge(q_f, p + 1)
                pe.wait_ge(q_b, p + 1)
                for n in range(NCH):
                    nc.tensor.matmul(ps[:, at, chunk(n)], state[:, 0, n], qd[:, 0, n], start=True, stop=False)
                    nc.tensor.matmul(ps[:, at, chunk(n)], state[:, 1, n], qd[:, 1, n], start=False, stop=True)
                    for j in range(2):
                        last = nc.tensor.matmul(ps[64 * j:64 * j + 64, at, chunk(n)], vtok[:, p, n, 64 * j:64 * j + 64],
                                                prob[:, j, n], start=False, stop=True, skip_group_check=True)
                last.then_inc(out_made, 1)

            pe.wait_ge(tables_loaded, 16)
            pe.wait_ge(y_loaded, 32)
            ones_product(e.ONES[:], [y[:, t] for t in range(2)], 0, c_summed, 2)
            transposes(0, 0, k, k_in, 1)
            pe.wait_ge(c_centered, 2)
            transposes(0, 1, v, v_in, 0)
            pe.wait_ge(tok_made, 1)
            pe.wait_ge(c_squared, 2)
            ones_product(e.ONES[:], [y_sq[:, t] for t in range(2)], 1, c_varied, 2)
            pe.wait_ge(tok_made, 2)
            chunk_sums(0, 0)
            pe.wait_ge(c_rstd, 1)
            chunk_sums(0, 1)
            for j in range(2):
                pe.wait_ge(kv_masked, j + 1)
                scores(0, j)
            for j, (src, loaded) in enumerate(((k, k_in), (v, v_in))):
                pe.wait_ge(decayed, j + 1)
                transposes(1, j, src, loaded, j)
            pe.wait_ge(tok_made, 3)
            output(0)
            pe.wait_ge(tok_made, 4)
            chunk_sums(1, 0)
            pe.wait_ge(out_copied, 1)
            ones_product(rt(RT_BLK64), [o[:, 0]], MEAN_SET[0], mean_made)
            pe.wait_ge(kv_masked, 3)
            chunk_sums(1, 1)
            pe.wait_ge(centered, 1)
            pe.wait_ge(squared, 1)
            ones_product(rt(RT_BLK64), [o2[:, 0]], VAR_SET[0], var_made)
            pe.wait_ge(kv_masked, 4)
            scores(1, 0)
            pe.wait_ge(rstd_step, 1)
            scores(1, 1)
            output(1)
            pe.wait_ge(out_copied, 2)
            ones_product(rt(RT_BLK64), [o[:, 1]], MEAN_SET[1], mean_made)
            pe.wait_ge(squared, 2)
            ones_product(rt(RT_BLK64), [o2[:, 1]], VAR_SET[1], var_made)

        @block.scalar
        def _(act):
            nc.scalar.activation(e.LGA[:], sv(e, "lga", 0, 8), ACT.Exp).then_inc(pa, 1)
            nc.scalar.activation(e.LGP[:], sv(e, "lgp", 0, 4), ACT.Exp).then_inc(pa, 1)
            act.wait_ge(pa, 2)
            nc.scalar.activation(e.LGA[:], e.LGA[:], ACT.Copy, scale=-1.0).then_inc(pa, 1)
            nc.scalar.activation(e.LGP[:], e.LGP[:], ACT.Copy, scale=-1.0).then_inc(pa, 1)
            act.wait_ge(pa, 4)
            act.wait_ge(tables_loaded, 16)
            nc.scalar.activation(e.CHUNK_DECAY[:], e.LGP[:], ACT.Exp, scale=float(P)).then_inc(pa, 1)
            for d in range(2):
                for p in range(2):
                    nc.scalar.activation(e.Q_DECAY[:, 2 * d + p], rt(RT_QF + d), ACT.Exp,
                                         scale=e.LGP[:, 2 * d + p:2 * d + p + 1]).then_inc(pa, 1)
                nc.scalar.activation(e.K_DECAY[:, d], e.LGA[:, 4 * d:4 * d + 4], ACT.Exp,
                                     scale=e.RT[:, 8 * P + d:8 * P + d + 1]).then_inc(pa, 1)
            act.wait_ge(pa, 11)
            nc.scalar.activation(e.K_DECAY[:], e.K_DECAY[:], ACT.Copy, scale=K_SCALE).then_inc(pa, 1)
            for h in range(HEADS):
                nc.scalar.activation(ef[:, h], rt(RT_RELF), ACT.Exp, scale=e.LGA[:, h:h + 1]).then_inc(pa, 1)
                nc.scalar.activation(eb[:, h], rt(RT_RELB), ACT.Exp, scale=e.LGA[:, 4 + h:5 + h]).then_inc(pa, 1)
            act.wait_ge(pv, 4)
            nc.scalar.activation(lam_sum[:, 2:4], lam_sum[:, 0:2], ACT.Exp).then_inc(pa, 1)

            def token_major(p, j, dst, at):
                act.wait_ge(transposed, 2 * p + j + 1)
                nc.scalar.activation(dst.rearrange("p n c -> p (n c)"), ps[:, at, 0:T], ACT.Copy).then_inc(tok_made, 1)

            def copy_out(p):
                act.wait_ge(out_made, p + 1)
                nc.scalar.activation(o[:, p], ps[:, OUT_SET[p], 0:T], ACT.Copy).then_inc(out_copied, 1)

            def square(p):
                act.wait_ge(centered, p + 1)
                nc.scalar.activation(o2[:, p], o[:, p], ACT.Square).then_inc(squared, 1)

            def inverse_rms(p):
                act.wait_ge(var_made, p + 1)
                nc.scalar.activation(o2[:, p], ps[:, VAR_SET[p], 0:T], ACT.Ln, bias=e.EPS[:]).then_inc(rstd_step, 1)
                act.wait_ge(rstd_step, 2 * p + 1)
                nc.scalar.activation(o2[:, p], o2[:, p], ACT.Exp, scale=-0.5).then_inc(rstd_step, 1)

            def hi(p):
                act.wait_ge(scaled, 2 * p + 2)
                nc.scalar.activation(e.H_HI[:, p], o[:, p], ACT.Copy).then_inc(hi_made, 1)

            token_major(0, 0, ktok[:], 1)
            for t in range(CONV_TILES):
                act.wait_ge(c_centered, t + 1)
                nc.scalar.activation(y_sq[:, t], y[:, t], ACT.Square).then_inc(c_squared, 1)
            token_major(0, 1, vtok[:, 0], 0)
            act.wait_ge(c_varied, 1)
            nc.scalar.activation(rstd[:], ps[:, 1, 0:T], ACT.Ln, scale=1.0 / (CONV_TILES * P),
                                 bias=e.EPS[:]).then_inc(c_rstd, 1)
            act.wait_ge(c_rstd, 1)
            nc.scalar.activation(rstd[:], rstd[:], ACT.Exp, scale=-0.5).then_inc(c_rstd, 1)
            for t in range(CONV_TILES):
                act.wait_ge(c_scaled, t + 1)
                nc.scalar.activation(y[:, t], y[:, t], ACT.Silu, scale=sv(e, "clw", t), bias=sv(e, "clb", t)).then_inc(c_silu, 1)
            for t in range(CONV_TILES):
                act.wait_ge(c_silu, t + 1)
                nc.scalar.activation(e.H_HI[:, 6 + t], y[:, t], ACT.Copy).then_inc(c_hi, 1)
            token_major(1, 0, ktok[:], 0)
            token_major(1, 1, vtok[:, 1], 1)
            copy_out(0)
            square(0)
            inverse_rms(0)
            hi(0)
            copy_out(1)
            square(1)
            inverse_rms(1)
            hi(1)

        def k_decay(j, p):
            return (e.K_DECAY[:, j, 2 * p:2 * p + 2].rearrange("p (a h b) -> p a h b", a=1, b=1)
                    .to_broadcast([P, NCH, 2, DK]))

        def by_head(ap):
            return ap.rearrange("p n (h d) -> p n h d", h=2)

        def q_decay(j, p):
            return e.Q_DECAY[:, 2 * j + p:2 * j + p + 1].to_broadcast([P, NCH, P])

        @block.gpsimd
        def _(pool):
            for p in range(2):
                if p:
                    pool.wait_ge(kv_made, 2)
                pool.wait_ge(pa, 12)
                pool.wait_ge(tok_made, 2 * p + 1)
                nc.gpsimd.tensor_tensor(by_head(kd[:, 1]), by_head(ktok[:]), k_decay(1, p), ALU.mult).then_inc(kd_b, 1)
                if p:
                    pool.wait_ge(out_made, 1)
                pool.wait_ge(q_in[p], 16)
                nc.gpsimd.tensor_tensor(qd[:, 1], chunks(q[:, p]), q_decay(1, p), ALU.mult).then_inc(q_b, 1)

        @block.vector
        def _(dve):
            for j in range(2):
                nc.vector.tensor_tensor(lam_prod[:, j], sv(e, "dlam", 2 * j * DK, DK), sv(e, "dlam", (2 * j + 1) * DK, DK),
                                        ALU.mult).then_inc(pv, 1)
            for j in range(2):
                dve.wait_ge(pv, j + 1)
                nc.vector.reduce_sum(lam_sum[:, j:j + 1], lam_prod[:, j], AX).then_inc(pv, 1)

            def decays():
                dve.wait_ge(pa, 20)
                for h in range(HEADS):
                    nc.vector.scalar_tensor_tensor(ef[:, h], ef[:, h], K_SCALE, rt(RT_MASKF), ALU.mult, ALU.mult).then_inc(pv, 1)
                    nc.vector.scalar_tensor_tensor(eb[:, h], eb[:, h], K_SCALE, rt(RT_MASKB), ALU.mult, ALU.mult).then_inc(pv, 1)
                dve.wait_ge(pv, 12)
                nc.vector.tensor_tensor(e.INTRA[:], ef, eb, ALU.add).then_inc(pv, 1)
                dve.wait_ge(pa, 21)
                nc.vector.tensor_tensor(e.NEG_LAM[:], lam_sum[:, 3:4], lam_sum[:, 2:3], ALU.subtract).then_inc(pv, 1)
                dve.wait_ge(pv, 14)
                nc.vector.tensor_scalar(e.NEG_LAM[:], e.NEG_LAM[:], -lam_init, None, ALU.add).then_inc(pv, 1)
                nc.vector.tensor_scalar(e.DGN[:], sv(e, "dgn", 0, 4), 1.0 - lam_init, None, ALU.mult).then_inc(pv, 1)

            def forward_keys(p):
                dve.wait_ge(pa, 12)
                dve.wait_ge(tok_made, 2 * p + 1)
                nc.vector.tensor_tensor(by_head(kd[:, 0]), by_head(ktok[:]), k_decay(0, p), ALU.mult).then_inc(kd_f, 1)

            def forward_queries(p):
                dve.wait_ge(q_in[p], 16)
                nc.vector.tensor_tensor(qd[:, 0], chunks(q[:, p]), q_decay(0, p), ALU.mult).then_inc(q_f, 1)

            mask = e.RT[:, RT_BLK * P:(RT_BLK + 1) * P].rearrange("p (a c) -> p a c", a=1).to_broadcast([P, NCH, P])

            def own_blocks(p, j):
                dve.wait_ge(kv_made, 2 * p + j + 1)
                nc.vector.tensor_tensor(prob[:, j], chunks(ps[:, KV_SET[p][j], 0:T]), mask, ALU.mult).then_inc(kv_masked, 1)

            def states(p):
                for j in range(2):
                    first = nc.vector.memset(state[:, j, orders[j][0]], 0.0)
                first.then_inc(state_step, 1)
                dve.wait_ge(kv_masked, 2 * p + 2)
                for a, z in zip(range(NCH - 1), range(1, NCH)):
                    for j in range(2):
                        dve.wait_ge(state_step, steps_per_pair * p + (2 * a + j if a else 1))
                        nc.vector.scalar_tensor_tensor(
                            state[:, j, orders[j][z]], state[:, j, orders[j][a]], e.CHUNK_DECAY[:, 2 * j + p:2 * j + p + 1],
                            prob[:, j, orders[j][a]], ALU.mult, ALU.add).then_inc(state_step, 1)
                dve.wait_ge(state_step, steps_per_pair * (p + 1))

            def decayed_scores(p, j):
                dve.wait_ge(scored, 2 * p + j + 1)
                nc.vector.tensor_tensor(prob[:, j], chunks(ps[:, SCORE_SET[p][j], 0:T]),
                                        e.INTRA[:, 2 * p + j:2 * p + j + 1].to_broadcast([P, NCH, P]),
                                        ALU.mult).then_inc(decayed, 1)

            def center(p):
                dve.wait_ge(mean_made, p + 1)
                nc.vector.tensor_tensor(o[:, p], o[:, p], ps[:, MEAN_SET[p], 0:T], ALU.subtract).then_inc(centered, 1)

            def scale_and_gate(p):
                dve.wait_ge(rstd_step, 2 * p + 2)
                nc.vector.tensor_tensor(o[:, p], o[:, p], o2[:, p], ALU.mult).then_inc(scaled, 1)
                dve.wait_ge(scaled, 2 * p + 1)
                dve.wait_ge(g_in[p], 16)
                nc.vector.scalar_tensor_tensor(o[:, p], o[:, p], sv(e, "rgn", p), g[:, p], ALU.mult, ALU.mult).then_inc(scaled, 1)

            def rest(p):
                dve.wait_ge(hi_made, p + 1)
                nc.vector.tensor_tensor(e.H_LO[:, p], o[:, p], e.H_HI[:, p].bitcast(F32), ALU.subtract).then_inc(lo_made, 1)

            dve.wait_ge(c_summed, 1)
            for t in range(CONV_TILES):
                nc.vector.scalar_tensor_tensor(y[:, t], ps[:, 0, 0:T], -1.0 / (CONV_TILES * P), y[:, t], ALU.mult,
                                               ALU.add).then_inc(c_centered, 1)
            forward_keys(0)
            forward_queries(0)
            decays()
            own_blocks(0, 0)
            dve.wait_ge(c_rstd, 2)
            dve.wait_ge(c_squared, 2)
            dve.wait_ge(c_centered, 2)
            for t in range(CONV_TILES):
                nc.vector.tensor_tensor(y[:, t], y[:, t], rstd[:], ALU.mult).then_inc(c_scaled, 1)
            own_blocks(0, 1)
            states(0)
            for j in range(2):
                decayed_scores(0, j)
            for t in range(CONV_TILES):
                dve.wait_ge(c_hi, t + 1)
                nc.vector.tensor_tensor(e.H_LO[:, 6 + t], y[:, t], e.H_HI[:, 6 + t].bitcast(F32),
                                        ALU.subtract).then_inc(c_lo, 1)
            forward_keys(1)
            dve.wait_ge(out_made, 1)
            own_blocks(1, 0)
            center(0)
            forward_queries(1)
            own_blocks(1, 1)
            states(1)
            scale_and_gate(0)
            for j in range(2):
                decayed_scores(1, j)
            rest(0)
            center(1)
            dve.wait_ge(centered, 2)
            scale_and_gate(1)
            rest(1)


def attention_block(nc, e, layer, last_layer):
    n_q = NCH_X if last_layer else NCH
    width = n_q * P
    keys_of = lambda i: (0, T) if i < NCH_X else (SEQ, T)
    n_keys = lambda i: keys_of(i)[1] - keys_of(i)[0]
    in_fours = lambda n: [list(range(a, min(a + 4, n))) for a in range(0, n, 4)]
    rounds_of = lambda i: in_fours(n_keys(i) // P)
    v_rounds = in_fours(NCH)
    first_round = [len(v_rounds)]
    for i in range(n_q):
        first_round.append(first_round[-1] + len(rounds_of(i)))
    per_head = first_round[-1]
    AHEAD = 3
    RING = 4 if n_q % 4 == 0 else 5
    assert NCH_X % 4 == 0 and n_q % RING == 0

    with ExitStack() as ctx:
        sem = lambda n: e.semaphore(f"{n}_a{layer}")
        sb = lambda n, s, d=F32: ctx.enter_context(nc.sbuf_tensor(f"{n}_a{layer}", s, d))
        scored, max_step, exped, recip_step, scaled1, combined = map(
            sem, ("scored", "max_step", "exped", "recip_step", "scaled1", "combined"))
        transposed, t_copied, av_made, o_copied = map(sem, ("transposed", "t_copied", "av_made", "o_copied"))
        squared, total, rstd_step, normed, hi_made, lo_made = map(
            sem, ("squared", "total", "rstd_step", "normed", "hi_made", "lo_made"))
        qk_loaded, v_loaded = e.qk_loaded, e.v_loaded
        hi_split, k_lo_split, q_lo_split = map(sem, ("hi_split", "k_lo_split", "q_lo_split"))
        v, k_twice = e.V_HEAD, e.K_TWICE
        q_twice = (e.Q_TWICE0, sb("q_twice1", [P, T]))
        q_parts, k_hi, k_lo = (sb(n, [P, 2, T], R32) for n in ("q_parts", "k_hi", "k_lo"))
        vtok, at = sb("vtok", [P, NCH, P]), sb("at", [P, NCH, P])
        ex0, ex1, ex0_ctx = sb("ex0", [P, 4, T]), sb("ex1", [P, 2, T]), sb("ex0_ctx", [P, 2, CTX])
        exp0_of = lambda i: ex0[:, i % 4] if i < NCH_X else ex0_ctx[:, i - NCH_X]
        o_all = sb("o_all", [P, HEADS, T])
        peak, neg_peak, total_e, recip = (sb(n, [P, RING, 2]) for n in ("peak", "neg_peak", "total_e", "recip"))
        ps = ctx.enter_context(nc.psum_tensor(f"ps_a{layer}", [P, 2, 3 * 512], F32))
        ps_t = ctx.enter_context(nc.psum_tensor(f"ps_t{layer}", [P, 512], F32))
        ps_o = ctx.enter_context(nc.psum_tensor(f"ps_o{layer}", [P, 512], F32))
        squared_before, log_made, hi_copied = sem("squared_before"), sem("log_made"), sem("hi_copied")
        o_squares = [k_twice[:, 0], k_twice[:, 1], q_twice[0], q_twice[1]]
        rstd_of = [ex1[:, 0], ex1[:, 1], ex0[:, 0], ex0[:, 1]]
        HI_BY_ACT = 2
        block = ctx.enter_context(nc.Block())
        scratch = e.scratch[layer]
        chunk = lambda n: slice(n * P, (n + 1) * P)

        def after(h, i, n, last_head=False):
            if i + n < n_q:
                return (h, i + n)
            return None if last_head else (h + 1, i + n - n_q)

        @block.sync
        def _(sp):
            def load_v(h):
                sp.dma_start(v[:], scratch[bass.ds(DV + h, 1)].rearrange("a p c -> p (a c)")).then_inc(v_loaded, 16)

            def qk_moves(h, m):
                return [(buf[64 * half:64 * half + 64], scratch[bass.ds(n + h, 1), 64 * m:64 * m + 64].rearrange("a p c -> p (a c)"))
                        for buf, n in ((k_twice[:, m], DKK), (q_twice[m], DQ)) for half in range(2)]

            def load_qk(moves, m):
                for dst, src in moves:
                    sp.dma_start(dst, src).then_inc(qk_loaded[m], 16)

            load_qk(qk_moves(0, 1), 1)
            with sp.Fori(0, HEADS - 1) as h:
                moves = [qk_moves(h + 1, m) for m in range(2)]
                for m in range(2):
                    sp.wait_ge(k_lo_split, 2 * h + m + 1)
                    sp.wait_ge(q_lo_split, 2 * h + m + 1)
                    sp.wait_ge(qk_loaded[m], 64 * h + 64)
                    load_qk(moves[m], m)
                sp.wait_ge(v_loaded, 16 * h + 16)
                sp.wait_ge(transposed, per_head * h + len(v_rounds))
                load_v(h + 1)

        @block.tensor
        def _(pe):
            def transposes(h, r, src, ids):
                pe.wait_ge(t_copied, per_head * h + r + 1)
                for n in ids:
                    t = nc.tensor.transpose(ps_t[:, (n - ids[0]) * P:(n - ids[0] + 1) * P], src[:, chunk(n)], e.IDENT)
                t.then_inc(transposed, 1)

            def scores(h, i, m):
                a0, z0 = keys_of(i)
                if i == 0:
                    pe.wait_ge(k_lo_split, 2 * h + m + 1)
                    pe.wait_ge(q_lo_split, 2 * h + m + 1)
                pe.wait_ge(exped, 2 * n_q * h + 2 * i + m + 1)
                for a, z in blocks(z0 - a0):
                    nc.tensor.matmul(ps[:, m, a:z], q_parts[:, m, chunk(i)], k_hi[:, m, a0 + a:a0 + z], start=True, stop=False)
                    t = nc.tensor.matmul(ps[:, m, a:z], q_parts[:, m, chunk(i)], k_lo[:, m, a0 + a:a0 + z], start=False, stop=True)
                t.then_inc(scored, 1)

            def values(h, i, r, ids):
                pe.wait_ge(t_copied, per_head * h + first_round[i] + r + 2)
                for n in ids:
                    t = nc.tensor.matmul(ps_o[:, 0:P], vtok[:, keys_of(i)[0] // P + n], at[:, n], start=n == 0,
                                         stop=n == n_keys(i) // P - 1)
                return t

            def v_transposes(h):
                pe.wait_ge(v_loaded, 16 * h + 16)
                for r, ids in enumerate(v_rounds):
                    transposes(h, r, v, ids)

            def step(nxt, prev):
                first_tile = nxt is not None and nxt[1] == 0
                if nxt is not None and not first_tile:
                    scores(*nxt, 0)
                h, i = prev
                rounds = rounds_of(i)
                pe.wait_ge(combined, n_q * h + i + 1)
                transposes(h, first_round[i], exp0_of(i), rounds[0])
                if nxt is not None and not first_tile:
                    scores(*nxt, 1)
                if len(rounds) > 1:
                    transposes(h, first_round[i] + 1, exp0_of(i), rounds[1])
                pe.wait_ge(o_copied, n_q * h + i + 1)
                for r, ids in enumerate(rounds):
                    t = values(h, i, r, ids)
                    if r + 2 < len(rounds):
                        transposes(h, first_round[i] + r + 2, exp0_of(i), rounds[r + 2])
                t.then_inc(av_made, 1)
                if first_tile:
                    for m in range(2):
                        scores(*nxt, m)

            v_transposes(0)
            for i in range(AHEAD):
                for m in range(2):
                    scores(0, i, m)
            with pe.Fori(0, HEADS - 1) as h:
                for i in range(n_q):
                    step(after(h, i, AHEAD), (h, i))
                v_transposes(h + 1)
            for i in range(n_q):
                step(after(HEADS - 1, i, AHEAD, True), (HEADS - 1, i))
            for h in range(HEADS):
                if h < HEADS - 1:
                    pe.wait_ge(squared_before, h + 1)
                else:
                    pe.wait_ge(squared, 1)
                if h >= 2:
                    pe.wait_ge(log_made, h - 1)
                for a, z in blocks(width):
                    t = nc.tensor.matmul(ps[:, h % 2, a:z], e.ONES[:], o_squares[h][:, a:z], start=True, stop=True)
                t.then_inc(total, 1)

        @block.scalar
        def _(act):
            def copy_round(h, r, dst):
                act.wait_ge(transposed, per_head * h + r + 1)
                nc.scalar.activation(dst.rearrange("p n c -> p (n c)"), ps_t[:, 0:dst.shape[1] * P],
                                     ACT.Copy).then_inc(t_copied, 1)

            def exp(h, i, m):
                n, dst = n_keys(i), ex1[:, i % 2] if m else exp0_of(i)
                act.wait_ge(max_step, 4 * n_q * h + 4 * i + 2 * m + 2)
                nc.scalar.activation(dst[:, 0:n], ps[:, m, 0:n], ACT.Exp, bias=neg_peak[:, i % RING, m:m + 1],
                                     scale=K_SCALE, accum_out=total_e[:, i % RING, m:m + 1]).then_inc(exped, 1)

            def v_copies(h):
                for r, ids in enumerate(v_rounds):
                    copy_round(h, r, vtok[:, ids[0]:ids[-1] + 1])

            def split_hi(h, m, after_scores=True):
                act.wait_ge(qk_loaded[m], 64 * h + 64)
                if after_scores:
                    act.wait_ge(scored, 2 * n_q * h + m - 1)
                nc.scalar.activation(k_hi[:, m], k_twice[:, m], ACT.Copy).then_inc(hi_split, 1)
                nc.scalar.activation(q_parts[:, m], q_twice[m][:], ACT.Copy).then_inc(hi_split, 1)

            def step(nxt, prev):
                h, i = prev
                first_tile = nxt is not None and nxt[1] == 0
                rounds = rounds_of(i)
                for r, ids in enumerate(rounds):
                    copy_round(h, first_round[i] + r, at[:, ids[0]:ids[-1] + 1])
                    if r == min(1, len(rounds) - 1):
                        if first_tile:
                            split_hi(nxt[0], 1)
                        elif nxt is not None:
                            exp(*nxt, 0)
                if nxt is not None and not first_tile:
                    exp(*nxt, 1)
                act.wait_ge(av_made, n_q * h + i + 1)
                nc.scalar.activation(o_all[:, bass.ds(h, 1), chunk(i)].rearrange("p a t -> p (a t)"), ps_o[:, 0:P],
                                     ACT.Copy).then_inc(o_copied, 1)
                if first_tile:
                    for m in range(2):
                        exp(*nxt, m)

            nc.scalar.activation(neg_peak[:, 0], e.UNIT[:, 0:2], ACT.Copy).then_inc(exped, 2)
            nc.scalar.activation(neg_peak[:, 1], e.UNIT[:, 0:2], ACT.Copy).then_inc(t_copied, 1)
            nc.scalar.activation(recip[:, 0], e.UNIT[:, 0:2], ACT.Copy).then_inc(o_copied, 1)
            for m in range(2):
                split_hi(0, m, False)
            v_copies(0)
            for i in range(AHEAD):
                for m in range(2):
                    exp(0, i, m)
            with act.Fori(0, HEADS - 1) as h:
                for i in range(n_q):
                    step(after(h, i, AHEAD), (h, i))
                    if i == n_q - AHEAD - 1:
                        split_hi(h + 1, 0)
                v_copies(h + 1)
            for i in range(n_q):
                step(after(HEADS - 1, i, AHEAD, True), (HEADS - 1, i))
            act.wait_ge(o_copied, n_q * HEADS + 1)

            act.wait_ge(q_lo_split, 2 * HEADS)
            nc.scalar.preload_act_table_set("natural_log_exp_and_others")
            nc.scalar.activation(o_squares[-1][:, 0:width], o_all[:, HEADS - 1, 0:width], ACT.Square).then_inc(squared, 1)

            def log(h):
                act.wait_ge(total, h + 1)
                nc.scalar.activation(rstd_of[h][:, 0:width], ps[:, h % 2, 0:width], ACT.Ln, scale=1.0 / P,
                                     bias=e.EPS[:]).then_inc(log_made, 1)

            def exp_of_log(h):
                act.wait_ge(log_made, h + 1)
                nc.scalar.activation(rstd_of[h][:, 0:width], rstd_of[h][:, 0:width], ACT.Exp, scale=-0.5).then_inc(rstd_step, 1)

            log(0)
            exp_of_log(0)
            for h in range(1, HEADS):
                log(h)
                exp_of_log(h)
                if h <= HI_BY_ACT:
                    act.wait_ge(normed, h)
                    nc.scalar.activation(e.H_HI[:, 1 + h, 0:width], o_all[:, h - 1, 0:width], ACT.Copy).then_inc(hi_made, 1)

        @block.gpsimd
        def _(pool):
            def split_k_lo(h, m):
                pool.wait_ge(hi_split, 4 * h + 2 * m + 1)
                nc.gpsimd.tensor_tensor(k_lo[:, m], k_twice[:, m], k_hi[:, m].bitcast(F32),
                                        ALU.subtract).then_inc(k_lo_split, 1)

            def square(h):
                pool.wait_ge(o_copied, n_q * (h + 1) + 1)
                pool.wait_ge(q_lo_split, 2 * HEADS)
                nc.gpsimd.tensor_tensor(o_squares[h][:, 0:width], o_all[:, h, 0:width], o_all[:, h, 0:width],
                                        ALU.mult).then_inc(squared_before, 1)

            def scale_tiles(h, next_head):
                for i in range(n_q):
                    n = n_keys(i)
                    pool.wait_ge(recip_step, 2 * n_q * h + 2 * i + 2)
                    nc.gpsimd.tensor_tensor(e.POOL_SCRAP[:], e.UNIT[:], e.UNIT[:], ALU.mult)
                    nc.gpsimd.tensor_scalar(ex1[:, i % 2, 0:n], ex1[:, i % 2, 0:n], recip[:, i % RING, 1:2], 1.0,
                                            ALU.mult, ALU.mult).then_inc(scaled1, 1)
                    if next_head is not None and i == n_q - 2:
                        for m in range(2):
                            split_k_lo(next_head, m)
                    if next_head is None and 1 <= i < HEADS:
                        square(i - 1)

            for m in range(2):
                split_k_lo(0, m)
            with pool.Fori(0, HEADS - 1) as h:
                scale_tiles(h, h + 1)
            scale_tiles(HEADS - 1, None)

        @block.vector
        def _(dve):
            def split_q_lo(h, m):
                dve.wait_ge(hi_split, 4 * h + 2 * m + 2)
                low = slice(64, P)
                nc.vector.tensor_tensor(q_parts[low, m], q_twice[m][low], q_parts[low, m].bitcast(F32),
                                        ALU.subtract).then_inc(q_lo_split, 1)

            def peaks(h, i, m):
                dve.wait_ge(scored, 2 * n_q * h + 2 * i + m + 1)
                nc.vector.reduce_max(peak[:, i % RING, m:m + 1], ps[:, m, 0:n_keys(i)], AX).then_inc(max_step, 1)
                dve.wait_ge(max_step, 4 * n_q * h + 4 * i + 2 * m + 1)
                nc.vector.tensor_scalar(neg_peak[:, i % RING, m:m + 1], peak[:, i % RING, m:m + 1], -K_SCALE, None,
                                        ALU.mult).then_inc(max_step, 1)

            def reciprocals(h, i):
                c = 2 * n_q * h + 2 * i
                dve.wait_ge(exped, c + 4)
                nc.vector.reciprocal(recip[:, i % RING], total_e[:, i % RING]).then_inc(recip_step, 1)
                dve.wait_ge(recip_step, c + 1)
                nc.vector.tensor_tensor(recip[:, i % RING, 1:2], recip[:, i % RING, 1:2], e.NEG_LAM[:], ALU.mult).then_inc(recip_step, 1)

            def combine(h, i):
                n, e0 = n_keys(i), exp0_of(i)
                dve.wait_ge(recip_step, 2 * n_q * h + 2 * i + 2)
                dve.wait_ge(scaled1, n_q * h + i + 1)
                nc.vector.scalar_tensor_tensor(e0[:, 0:n], e0[:, 0:n], recip[:, i % RING, 0:1], ex1[:, i % 2, 0:n],
                                               ALU.mult, ALU.add).then_inc(combined, 1)

            def step(h, i, last_head=False):
                nxt, following = after(h, i, 1, last_head), after(h, i, 2, last_head)
                combine(h, i)
                if nxt is not None:
                    reciprocals(*nxt)
                if following is not None:
                    if following[1] == 0:
                        for m in range(2):
                            split_q_lo(following[0], m)
                    for m in range(2):
                        peaks(*following, m)

            dve.wait_ge(o_copied, 1)
            for m in range(2):
                split_q_lo(0, m)
            peaks(0, 0, 0)
            peaks(0, 0, 1)
            reciprocals(0, 0)
            peaks(0, 1, 0)
            peaks(0, 1, 1)
            with dve.Fori(0, HEADS - 1) as h:
                for i in range(n_q):
                    step(h, i)
            for i in range(n_q):
                step(HEADS - 1, i, True)
            def rest(h):
                dve.wait_ge(*((hi_made, h + 1) if h < HI_BY_ACT else (hi_copied, h + 1 - HI_BY_ACT)))
                nc.vector.tensor_tensor(e.H_LO[:, 2 + h, 0:width], o_all[:, h, 0:width],
                                        e.H_HI[:, 2 + h, 0:width].bitcast(F32), ALU.subtract).then_inc(lo_made, 1)

            for h in range(HEADS):
                dve.wait_ge(rstd_step, h + 1)
                nc.vector.scalar_tensor_tensor(o_all[:, h, 0:width], o_all[:, h, 0:width], e.DGN[:, h:h + 1],
                                               rstd_of[h][:, 0:width], ALU.mult, ALU.mult).then_inc(normed, 1)
                if h >= HI_BY_ACT:
                    dve.wait_ge(normed, h + 1)
                    nc.vector.tensor_copy(e.H_HI[:, 2 + h, 0:width], o_all[:, h, 0:width]).then_inc(hi_copied, 1)
                if h > 0:
                    rest(h - 1)
            rest(HEADS - 1)


def mlp_block(nc, e, layer, last_layer):
    width = SEQ if last_layer else T
    sides = [(0, 0, SEQ)] + ([] if last_layer else [(1, SEQ, T)])
    with ExitStack() as ctx:
        sem = lambda n: e.semaphore((f"{n}_f{layer}"))
        sb = lambda n, s, d=F32: ctx.enter_context(nc.sbuf_tensor(f"{n}_f{layer}", s, d))
        s = NormSemaphores(sem, "n2")
        slot_loaded = [sem("slot_loaded0"), sem("slot_loaded1")]
        x_loaded = [sem("x_loaded0"), sem("x_loaded1")]
        w_hi_made, w_lo_made, out_done, out_added = map(
            sem, ("w_hi_made", "w_lo_made", "out_done", "out_added"))
        up_done, up_relu, up_squared, g_hi_made, g_lo_made, down_done, down_added = map(
            sem, ("up_done", "up_relu", "up_squared", "g_hi_made", "g_lo_made", "down_done", "down_added"))
        stage, w_hi, w_lo = sb("stage", [P, 2, SLOT]), sb("w_hi", [P, 2, SLOT], R32), sb("w_lo", [P, 2, SLOT], R32)
        with ExitStack() as inner:
            tb = lambda n, s: inner.enter_context(nc.sbuf_tensor(f"{n}_f{layer}", s, F32))
            sq, acc, rstd, tmp = tb("sq", [P, 2, T]), tb("acc", [P, T]), tb("rstd", [P, T]), tb("tmp", [P, 3, T])
            own_stage = tb("own_stage", [P, 4, GROUP_COLS])
        g_hi, g_lo = sb("g_hi", [P, FF_CHUNK_TILES, T], R32), sb("g_lo", [P, FF_CHUNK_TILES, T], R32)
        hidden = sb("hidden", [P, 2, T])
        ps = ctx.enter_context(nc.psum_tensor(f"ps_f{layer}", [P, 2, 3 * 512], F32))
        b = NormBuffers(sq=sq, acc=acc, rstd=rstd, tmp=tmp, ps=ps)
        block = ctx.enter_context(nc.Block())
        side, own = not last_layer, layer == 0
        if side:
            side_loaded, unit_added, group_reduced, side_biased, gain_made = map(
                sem, ("side_loaded", "unit_added", "group_reduced", "side_biased", "gain_made"))
            side_stage, side_acc = sb("side_stage", [P, GROUP_COLS]), sb("side_acc", [P, 2, GROUP_COLS])
            side_ps = ctx.enter_context(nc.psum_tensor(f"side_ps_f{layer}", [P, 512], F32))
            own_groups = OWN_GROUPS if own else 0
            own_loaded = [sem(f"own_loaded{n}") for n in range(4)] if own else None
        if last_layer:
            final = NormSemaphores(sem, "final")
            final_scaled, final_stored = sem("final_scaled"), sem("final_stored")
            fb = NormBuffers(sq=hidden, acc=sb("final_acc", [P, SEQ]), rstd=sb("final_rstd", [P, SEQ]), tmp=None, ps=ps)
        up0, down0 = OUT_TILES, OUT_TILES + FF_CHUNK_TILES

        @block.sync
        def _(sp):
            for u in range(2):
                sp.dma_start(stage[:, u], e.w_dram[layer, OUT0 + u]).then_inc(slot_loaded[u], 16)
            def load(n, u, i):
                sp.wait_ge(w_lo_made, n + u - 1 + 2 * i)
                sp.dma_start(stage[:, u], e.w_dram[layer, bass.ds(OUT0 + n + u + 2 * i, 1)].rearrange(
                    "a p c -> p (a c)")).then_inc(slot_loaded[u], 16)

            def chunk_load(c, n):
                load(OUT_TILES + n - n % 2, n % 2, FF_SLOTS // 2 * c)

            def own_load(n, i):
                if i is not None:
                    sp.wait_ge(unit_added, 2 * (n - 4) + 2 + 2 * KT * i)
                    sp.dma_start(own_stage[:, n % 4], e.units_dram[bass.ds(n + KT * i, 1)].rearrange(
                        "a p c -> p (a c)")).then_inc(own_loaded[n % 4], 16)
                else:
                    sp.dma_start(own_stage[:, n % 4], e.units_dram[n]).then_inc(own_loaded[n % 4], 16)

            def side_load(c, n):
                if side:
                    if n > 0:
                        sp.wait_ge(unit_added, 2 * KT * own_groups + 2 * n + 2 * KT * c)
                    sp.dma_start(side_stage[:], e.units_dram[bass.ds(KT * OWN_GROUPS + n + KT * c, 1)].rearrange(
                        "a p c -> p (a c)")).then_inc(side_loaded, 16)

            x_from = (e.x_dram if layer == 0 else e.x_kept)[:, :, 0:width]
            for u in range(2):
                sp.dma_start(e.X[:, u, 0:width], x_from[u]).then_inc(x_loaded[u], 16)
            if own:
                for n in range(4):
                    own_load(n, None)
            with sp.Fori(0, OUT_TILES // 2 - 1) as i:
                for u in range(2):
                    load(2, u, i)
                    sp.wait_ge(x_loaded[u], 16 * i + 16)
                    sp.dma_start(e.X[:, bass.ds(2 + u + 2 * i, 1), 0:width].rearrange("p k t -> p (k t)"),
                                 x_from[bass.ds(2 + u + 2 * i, 1)].rearrange("k p t -> p (k t)")).then_inc(x_loaded[u], 16)
                    if own:
                        for r in range(4):
                            own_load(4 + 4 * u + r, i)
            for u in range(2):
                load(OUT_TILES, u, 0)
                if own and u == 0:
                    for r in range(4):
                        own_load(4 + r + KT * (OWN_GROUPS - 1), 0)
            for n in range(2, FF_SLOTS // 2):
                chunk_load(0, n)
            side_load(0, 0)

            def chunk(c, more):
                for j in range(FF_CHUNK_TILES):
                    chunk_load(c, FF_SLOTS // 2 + j)
                    side_load(c, 2 * j + 1)
                    if j < FF_CHUNK_TILES - 1:
                        side_load(c, 2 * j + 2)
                if more:
                    for n in range(FF_SLOTS // 2):
                        chunk_load(c + 1, n)
                    side_load_first(c + 1)

            def side_load_first(c):
                if side:
                    sp.wait_ge(unit_added, 2 * KT * own_groups + 2 * KT * c)
                    side_load(c, 0)

            with sp.Fori(0, FF_CHUNKS - 1) as c:
                chunk(c, True)
            chunk(FF_CHUNKS - 1, False)
            if last_layer:
                for k in range(KT):
                    sp.wait_ge(final_scaled, k + 1)
                    sp.dma_start(e.out_dram[k], e.X[:, k, 0:SEQ]).then_inc(final_stored, 16)
                sp.wait_ge(final_stored, 16 * KT)

        @block.scalar
        def _(act):
            def split(u, count):
                act.wait_ge(slot_loaded[u], count)
                nc.scalar.activation(w_hi[:, u], stage[:, u], ACT.Copy).then_inc(w_hi_made, 1)

            nc.scalar.activation(e.SCRAP[:, 0:1], e.UNIT[:, 0:1], ACT.Copy).then_inc(out_added, 2)
            split(0, 16)
            split(1, 16)
            with act.Fori(0, OUT_TILES // 2) as i:
                for u in range(2):
                    act.wait_ge(out_done, 2 * i + u + 1)
                    split(u, 16 * i + 32)
                    act.wait_ge(out_added, 2 * i + u + 3)
                    square_tile(nc, act, s, b, e.X[:, bass.ds(u + 2 * i, 1), 0:width].rearrange("p k t -> p (k t)"), u,
                                2 * i + u)
            inverse_rms(nc, act, e, s, b, width)
            norm_hi(nc, act, e, s, b, width)

            def split_after(n, c):
                split(n % 2, 16 * (n // 2 + 2) + 16 * (FF_SLOTS // 2) * c)

            def up(c, j):
                act.wait_ge(up_done, FF_CHUNK_TILES * c + j + 1)
                if j >= 2:
                    act.wait_ge(g_lo_made, FF_CHUNK_TILES * c + j - 1)
                nc.scalar.activation(hidden[:, j % 2, 0:width], ps[:, j % 2, 0:width], ACT.Relu).then_inc(up_relu, 1)
                act.wait_ge(up_relu, FF_CHUNK_TILES * c + j + 1)
                nc.scalar.activation(hidden[:, j % 2, 0:width], hidden[:, j % 2, 0:width], ACT.Square).then_inc(up_squared, 1)
                act.wait_ge(up_squared, FF_CHUNK_TILES * c + j + 1)
                nc.scalar.activation(g_hi[:, j, 0:width], hidden[:, j % 2, 0:width], ACT.Copy).then_inc(g_hi_made, 1)
                split_after(up0 + j, c)

            def down(c, j, more):
                act.wait_ge(down_done, KT * c + 2 * j + 2)
                if more:
                    split_after(down0 + j, c)

            with act.Fori(0, FF_CHUNKS - 1) as c:
                for j in range(FF_CHUNK_TILES):
                    up(c, j)
                for j in range(KT // 2):
                    down(c, j, True)
            for j in range(FF_CHUNK_TILES):
                up(FF_CHUNKS - 1, j)
            for j in range(KT // 2):
                down(FF_CHUNKS - 1, j, j < KT // 2 - 2)
                if last_layer:
                    if j == 0:
                        act.wait_ge(g_lo_made, FF_CHUNK_TILES * FF_CHUNKS)
                    for m in (2 * j, 2 * j + 1):
                        act.wait_ge(down_added, KT * (FF_CHUNKS - 1) + 2 + m + 1)
                        square_tile(nc, act, final, fb, e.X[:, m, 0:width], m % 2, m)
            if last_layer:
                inverse_rms(nc, act, e, final, fb, width)

        @block.tensor
        def _(pe):
            def product(u, j, x_hi, x_lo, first, n_k, ready, count):
                for k in range(n_k):
                    if ready is not None:
                        pe.wait_ge(ready, count + k + 1)
                    kk = slice((first + k) * P, (first + k + 1) * P)
                    for a, z in blocks(width):
                        last = mm3(nc, ps[:, u, a:z], w_hi[:, j, kk], w_lo[:, j, kk], x_hi[:, k, a:z],
                                   x_lo[:, k, a:z], k == 0, k == n_k - 1)
                return last

            def side_reduce(g):
                if side:
                    pe.wait_ge(side_biased, g + 1)
                    pe.wait_ge(unit_added, 2 * KT * g + 2 * KT)
                    for m in range(GROUP):
                        for v in range(2):
                            t = nc.tensor.matmul(side_ps[:, 2 * m + v:2 * m + v + 1], side_acc[:, v, m * P:(m + 1) * P],
                                                 e.ONES[:, 0:1], start=True, stop=True)
                    t.then_inc(group_reduced, 1)

            with pe.Fori(0, OUT_TILES // 2) as i:
                for u in range(2):
                    pe.wait_ge(w_lo_made, 2 * i + u + 1)
                    pe.wait_ge(out_added, 2 * i + u + 1)
                    product(u, u, e.H_HI, e.H_LO, 0, KT, None, 0).then_inc(out_done, 1)
                if own:
                    side_reduce(i)
            norm_pe(nc, pe, e, s, b, width)
            with pe.Fori(0, FF_CHUNKS) as c:
                for j in range(FF_CHUNK_TILES):
                    pe.wait_ge(w_lo_made, up0 + 1 + j + FF_SLOTS * c)
                    if j < 2:
                        pe.wait_ge(down_added, KT * c + 1 + j)
                    else:
                        pe.wait_ge(up_relu, FF_CHUNK_TILES * c + j - 1)
                    product(j % 2, j % 2, e.H_HI, e.H_LO, 0, KT, s.lo, 0).then_inc(up_done, 1)
                for m in range(KT):
                    j = m // 2
                    pe.wait_ge(w_lo_made, down0 + 1 + j + FF_SLOTS * c)
                    if m < 2:
                        pe.wait_ge(up_relu, FF_CHUNK_TILES * c + 3 + m)
                    else:
                        pe.wait_ge(down_added, KT * c + 1 + m)
                    product(m % 2, j % 2, g_hi, g_lo, FF_CHUNK_TILES * (m % 2), FF_CHUNK_TILES, g_lo_made,
                            FF_CHUNK_TILES * c).then_inc(down_done, 1)
                    if m == 3 and side:
                        side_reduce(own_groups + c)

            if last_layer:
                norm_pe(nc, pe, e, final, fb, width)

        @block.gpsimd
        def _(pool):
            norm_pool(nc, pool, e, s, b, width, layer, e.GAIN2, 3)

        @block.vector
        def _(dve):
            def split_rest(u, count):
                dve.wait_ge(w_hi_made, count)
                nc.vector.tensor_tensor(w_lo[:, u], stage[:, u], w_hi[:, u].bitcast(F32),
                                        ALU.subtract).then_inc(w_lo_made, 1)

            def add_gated(u, x_of, gate_of, added):
                for n, (side, a, z) in enumerate(sides):
                    op = nc.vector.scalar_tensor_tensor(x_of(a, z), ps[:, u, a:z], gate_of(side), x_of(a, z),
                                                        ALU.mult, ALU.add)
                op.then_inc(added, 1)

            def unit(n, g, place):
                for v in range(2):
                    c = e.COND[:, n, v:v + 1]
                    if n == 0:
                        if v == 0:
                            dve.wait_ge(group_reduced, g)
                        nc.vector.tensor_scalar(side_acc[:, v], place, c, None, ALU.mult).then_inc(unit_added, 1)
                    else:
                        dve.wait_ge(unit_added, 2 * KT * g + 2 * n + v - 1)
                        nc.vector.scalar_tensor_tensor(side_acc[:, v], place, c, side_acc[:, v], ALU.mult,
                                                       ALU.add).then_inc(unit_added, 1)

            def own_units(i, u):
                if own:
                    for n in range(4 * u, 4 * u + 4):
                        dve.wait_ge(own_loaded[n % 4], 16 * (n // 4 + 1) + 32 * i)
                        unit(n, i, own_stage[:, n % 4])

            def chunk_units(c, j):
                if side:
                    for n in (2 * j, 2 * j + 1):
                        dve.wait_ge(side_loaded, 16 * (n + 1) + 16 * KT * c)
                        unit(n, own_groups + c, side_stage[:])

            def group_bias(g, of_layer, first):
                dve.wait_ge(group_reduced, g + 1)
                add_bias(nc, e, of_layer, side_ps, first, GROUP).then_inc(side_biased, 1)

            nc.vector.tensor_copy(e.SCRAP[:, 1:2], e.UNIT[:, 0:1]).then_inc(down_added, 2)
            if side:
                nc.vector.tensor_copy(e.SCRAP[:, 2:3], e.UNIT[:, 0:1]).then_inc(side_biased, 1)
            split_rest(0, 1)
            split_rest(1, 2)
            clear_sum(nc, s, b)
            with dve.Fori(0, OUT_TILES // 2) as i:
                for u in range(2):
                    own_units(i, u)
                    dve.wait_ge(out_done, 2 * i + u + 1)
                    dve.wait_ge(x_loaded[u], 16 * i + 16)
                    add_gated(u, lambda a, z: e.X[:, bass.ds(u + 2 * i, 1), a:z].rearrange("p k t -> p (k t)"),
                              lambda side: e.MOD[:, bass.ds(2 * (ADA_TILES * layer + 2 * KT + u) + side + 4 * i, 1)], out_added)
                    split_rest(u, 2 * i + u + 3)
                    add_square(nc, dve, s, b, width, u, 2 * i + u)
                if own:
                    group_bias(i, layer, FIRST_TILES + GROUP * i)
            if own:
                dve.wait_ge(side_biased, OWN_GROUPS + 1)
                make_gain(nc, e, layer, e.GAIN2, N2W, 4).then_inc(gain_made, 1)
            dve.wait_ge(out_added, OUT_TILES + 2)
            dve.wait_ge(s.rstd, 1)
            norm_dve(nc, dve, e, s, b, width)

            def up(c, j):
                dve.wait_ge(g_hi_made, FF_CHUNK_TILES * c + j + 1)
                nc.vector.tensor_tensor(g_lo[:, j, 0:width], hidden[:, j % 2, 0:width],
                                        g_hi[:, j, 0:width].bitcast(F32), ALU.subtract).then_inc(g_lo_made, 1)
                split_rest(j % 2, up0 + j + 3 + FF_SLOTS * c)
                chunk_units(c, j)

            def down(c, j, more):
                for m in (2 * j, 2 * j + 1):
                    dve.wait_ge(down_done, KT * c + m + 1)
                    dve.wait_ge(down_added, KT * c + 2)
                    add_gated(m % 2, lambda a, z: e.X[:, m, a:z],
                              lambda side: e.MOD[:, bass.ds(2 * (ADA_TILES * layer + 5 * KT + m) + side, 1)], down_added)
                if more:
                    split_rest(j % 2, down0 + j + 3 + FF_SLOTS * c)
                if side and j == 2:
                    group_bias(own_groups + c, layer + 1, GROUP * c)

            with dve.Fori(0, FF_CHUNKS - 1) as c:
                for j in range(FF_CHUNK_TILES):
                    up(c, j)
                for j in range(KT // 2):
                    down(c, j, True)
            for j in range(FF_CHUNK_TILES):
                up(FF_CHUNKS - 1, j)
            if last_layer:
                clear_sum(nc, final, fb)
            for j in range(KT // 2):
                down(FF_CHUNKS - 1, j, j < KT // 2 - 2)
                if last_layer:
                    for m in (2 * j - 1, 2 * j) if j else (0,):
                        add_square(nc, dve, final, fb, width, m % 2, m)
            if last_layer:
                add_square(nc, dve, final, fb, width, (KT - 1) % 2, KT - 1)
                dve.wait_ge(final.rstd, 1)
                for k in range(KT):
                    nc.vector.scalar_tensor_tensor(e.X[:, k, 0:SEQ], e.X[:, k, 0:SEQ], sv(e, "final", k),
                                                   fb.rstd[:], ALU.mult, ALU.mult).then_inc(final_scaled, 1)
            if side:
                dve.wait_ge(side_biased, own_groups + FF_CHUNKS + 1)
                make_gain(nc, e, layer + 1, e.GAIN1, N1W, 1).then_inc(gain_made, 1)
                dve.wait_ge(s.shifted, 2 * KT)
                make_gain(nc, e, layer + 1, e.GAIN2, N2W, 4).then_inc(gain_made, 1)


def build_program(nc, x_dram, cond_dram, id1_dram, sv_dram, mv_dram, ada_dram, units_dram, w_dram, rope_dram, rt_dram, out_dram, layers=DEPTH):
    with ExitStack() as ctx:
        sb = lambda n, s, d=F32: ctx.enter_context(nc.sbuf_tensor(n, s, d))
        e = Shared()
        e.x_dram, e.cond_dram, e.id1_dram, e.sv_dram = x_dram, cond_dram, id1_dram, sv_dram
        e.mv_dram, e.ada_dram, e.units_dram, e.w_dram, e.rope_dram, e.rt_dram, e.out_dram = mv_dram, ada_dram, units_dram, w_dram, rope_dram, rt_dram, out_dram
        e.scratch = [nc.dram_tensor(f"projected{i}", (IN_TILES, P, T), F32).ap() for i in range(layers)]
        e.H_HI, e.H_LO = sb("h_hi", [P, KT, T], R32), sb("h_lo", [P, KT, T], R32)
        e.x_kept = nc.dram_tensor("x_kept", (KT, P, T), F32).ap()
        e.ID1, e.ONES, e.SV = sb("identity", [P, P]), sb("ones", [P, P]), sb("vectors", [P, SV_LEN])
        e.COND, e.MOD = sb("cond", [P, KT, 2]), sb("mod", [P, 2 * ADA_TILES * DEPTH])
        e.MV = sb("modulation_vectors", [P, MV_LEN * DEPTH])
        e.GAIN1, e.GAIN2 = sb("gain1", [P, KT, 2]), sb("gain2", [P, KT, 2])
        e.EPS, e.UNIT, e.SCRAP, e.POOL_SCRAP = sb("eps", [P, 1]), sb("unit", [P, 2]), sb("scrap", [P, 4]), sb("pool_scrap", [P, 2])
        e.LGA, e.LGP, e.CHUNK_DECAY = sb("lga", [P, 8]), sb("lgp", [P, 4]), sb("chunk_decay", [P, 4])
        e.K_DECAY, e.NEG_LAM, e.DGN = sb("k_decay", [P, 2, HEADS]), sb("neg_lam", [P, 1]), sb("dgn", [P, HEADS])
        e.IDENT = e.ID1[:]
        x_place = ExitStack()

        def place_x(n):
            e.X = x_place.enter_context(nc.sbuf_tensor(f"x{n}", [P, KT, T], F32))

        for layer in range(layers):
            last = layer == DEPTH - 1
            layer_semaphores = ExitStack()
            e.semaphore = lambda name: e.held.append(layer_semaphores.enter_context(nc.semaphore(name))) or e.held[-1]
            e.held = []
            if layer == 0:
                place_x(0)
                with nc.sbuf_tensor("first_rstd", [P, T], F32) as e.FIRST_RSTD:
                    with nc.sbuf_tensor("first_acc", [P, T], F32) as e.RSTD_ACC:
                        modulation_block(nc, e)
                    projection_block(nc, e, layer, last)
            else:
                projection_block(nc, e, layer, last)
            x_place.close()
            with (nc.sbuf_tensor(f"k_twice{layer}", [P, 2, T], F32) as e.K_TWICE,
                  nc.sbuf_tensor(f"q_twice{layer}", [P, T], F32) as e.Q_TWICE0,
                  nc.sbuf_tensor(f"v_head{layer}", [P, T], F32) as e.V_HEAD):
                with (nc.sbuf_tensor(f"rt{layer}", [P, RT_LEN], F32) as e.RT,
                      nc.sbuf_tensor(f"intra{layer}", [P, HEADS, P], F32) as e.INTRA,
                      nc.sbuf_tensor(f"q_decay{layer}", [P, 4, P], F32) as e.Q_DECAY):
                    retention_block(nc, e, layer)
                attention_block(nc, e, layer, last)
            place_x(layer + 1)
            mlp_block(nc, e, layer, last)
            if not last:
                with nc.Block() as block:
                    @block.sync
                    def _(sp):
                        for s in e.held:
                            sp.sem_clear(s)
            layer_semaphores.close()
        x_place.close()


def rope_tables():
    f = np.float32
    half = DK // 2
    inv = f(ROPE_BASE) ** (-np.arange(0, DK, 2, dtype=f) / f(DK))
    inv_ax = f(ROPE_BASE) ** (-np.arange(0, half, 2, dtype=f) / f(half))
    pos = np.arange(SEQ)
    ret, ax = pos[:, None].astype(f) * inv[None, :], None
    rows, cols = (pos // GRID_W)[:, None].astype(f) * inv_ax, (pos % GRID_W)[:, None].astype(f) * inv_ax
    p = np.arange(P) % DK
    sign = np.where(p % 32 < 16, -1.0, 1.0).astype(f)[:, None]
    plain = ret[:, 16 * (p // 32) + p % 16].T
    axial = np.where(p[:, None] < 32, rows[:, p % 16].T, cols[:, p % 16].T)
    out = np.zeros((2, P, 2, T), f)
    out[:, :, 0] = 1.0
    for i, ang in enumerate((plain, axial)):
        out[i, :, 0, :SEQ] = np.cos(ang.astype(f))
        out[i, :, 1, :SEQ] = np.sin(ang.astype(f)) * sign
    return out


def retention_tables():
    f = np.float32
    s, c = np.arange(P)[:, None], np.arange(P)[None, :]
    one = np.ones((P, P))
    head = (s // DK == c // DK)
    tables = [np.maximum(c - s, 0), c >= s, np.maximum(s - c, 0), s >= c, (c + 1) * one, (P - c) * one, head, head / DK,
              P - 1 - s, s]
    return np.concatenate([t.astype(f) for t in tables], axis=1)


def columns(v):
    return v.reshape(-1, P).T


def kernel(**inputs):
    import concourse.bacc as bacc
    from concourse.bass_utils import run_bass_kernel_spmd

    a = {k: np.ascontiguousarray(v) for k, v in inputs.items()}
    x_t = np.concatenate([a["x"][0].T, a["ctx"][0].T], axis=1).reshape(KT, P, T)
    cond = np.stack([a["c"][0].reshape(KT, P).T, a["c_ctx"].reshape(KT, P).T], axis=-1)

    pair = np.arange(DK).reshape(2, 2, 16).transpose(1, 0, 2).reshape(-1)
    heads = (np.arange(HEADS)[:, None] * DK + pair).reshape(-1)
    width = HEADS * DK
    start = dict(rq=0, rk=width, rv=2 * width, rg=3 * width, dq=4 * width, dk=6 * width, dv=8 * width,
                 cv=10 * width, cg=11 * width)
    plain = np.arange(width)
    wide = np.arange(2 * width)
    order = np.concatenate([start["cv"] + plain, start["cg"] + plain, start["rq"] + heads, start["rk"] + heads,
                            start["rv"] + plain, start["rg"] + plain, start["dq"] + wide, start["dk"] + wide,
                            start["dv"] + wide])

    def slots(w):
        k, m = w.shape
        return w.reshape(k // P, P, m // P, P).transpose(2, 1, 0, 3).reshape(m // P, P, k)

    def units(w):
        k, m = w.shape
        return w.reshape(KT, P, m // GROUP_COLS, GROUP_COLS).transpose(2, 0, 1, 3).reshape(-1, P, GROUP_COLS)

    weights, vectors, mod_vectors = [], [], []
    for i in range(DEPTH):
        parts = [slots(a["w_in"][i][:, order]), slots(a["w_out"][i])]
        up, rows = slots(a["mlp_w1"][i]), FF_CHUNK_TILES * P
        for c in range(FF_CHUNKS):
            parts.append(up[FF_CHUNK_TILES * c:FF_CHUNK_TILES * (c + 1)])
            down = slots(a["mlp_w2"][i][rows * c:rows * (c + 1)])
            parts.append(down.reshape(KT // 2, 2, P, rows).transpose(0, 2, 1, 3).reshape(KT // 2, P, SLOT))
        weights.append(np.concatenate(parts))
        decay = a["ret_log_decay"][i]
        mod_vectors.append(np.concatenate([columns(a["norm1_w"][i]), columns(a["norm2_w"][i]), columns(a["ada_b"][i])], axis=1))
        vectors.append(np.concatenate([
            columns(a["ret_gn_w"][i]),
            columns(a["diff_gn_w"][i]),
            a["conv_w"][i].reshape(TAPS, CONV_TILES, P).transpose(2, 1, 0).reshape(P, CONV_TILES * TAPS),
            columns(a["conv_b"][i]), columns(a["conv_ln_w"][i]), columns(a["conv_ln_b"][i]),
            np.tile(decay.reshape(1, -1), (P, 1)),
            np.repeat(decay.reshape(2, 2, 2), DK, axis=2).reshape(4, P).T,
            np.tile(a["diff_lam"][i].reshape(1, -1), (P, 1)),
            columns(a["final_norm_w"])], axis=1))

    arrays = {"x_t": x_t, "cond_in": cond, "identity_in": np.eye(P, dtype=np.float32), "vectors_in": np.stack(vectors),
              "mod_vectors_in": np.concatenate(mod_vectors, axis=1),
              "modulation_first": slots(a["ada_w"][0])[:FIRST_TILES],
              "modulation_units": np.concatenate([units(a["ada_w"][0][:, FIRST_TILES * P:])]
                                                 + [units(a["ada_w"][i]) for i in range(1, DEPTH)]),
              "weights": np.stack(weights), "rope": rope_tables(), "retention": retention_tables()}
    arrays = {k: np.ascontiguousarray(v) for k, v in arrays.items()}
    nc = bacc.Bacc("TRN2", target_bir_lowering=False, num_devices=1)
    args = [nc.dram_tensor(k, v.shape, F32, kind="ExternalInput").ap() for k, v in arrays.items()]
    out = nc.dram_tensor("out_t", (KT, P, SEQ), F32, kind="ExternalOutput").ap()
    build_program(nc, *args, out)
    got = run_bass_kernel_spmd(nc, [arrays], core_ids=[0]).results[0]["out_t"]
    return np.ascontiguousarray(got.reshape(D_MODEL, SEQ).T)[None]
```
